# Optimizing a Trainium2 kernel written in Bass

```python
import math
import jax
import jax.numpy as jnp
from jax import lax
import numpy as np

D_MODEL = 1024
BATCH = 1
SEQ = 256
DEPTH = 1
DEC_BATCH = 1
DEC_SEQ = 512
PAST_LEN = 128

HEAD_DIM = 64
N_ATTN_HEADS = 8
ATTN_WIDTH = N_ATTN_HEADS * HEAD_DIM
HYENA_WIDTH = D_MODEL - ATTN_WIDTH
HYENA_ORDER = 2
SHORT_CONV = 3
FILTER_EMB = 33
FILTER_BANDS = (FILTER_EMB - 1) // 2
FILTER_HIDDEN = 64
FAST_DECAY_PCT = 0.3
SLOW_DECAY_PCT = 1.5
DECAY_TARGET = 1e-2
DILATED_PATTERNS = ((128, 1), (512, 4), (2048, 16))
N_EXPERTS = 16
EC_CAPACITY = 2
D_EXPERT = 2816
NORM_EPS = 1e-6
MASK_VALUE = -1e30
IN_WIDTH = 3 * ATTN_WIDTH + 3 * HYENA_WIDTH

kernel_name = 'hymba_longnet_hyena_ec_encoder'

def rms_norm(x, g):
    xf = x.astype(jnp.float32)
    y = xf * lax.rsqrt(jnp.mean(xf * xf, axis=-1, keepdims=True) + NORM_EPS)
    return (y * g.astype(jnp.float32)).astype(x.dtype)

def alibi_slopes(n_heads):
    return np.array([2.0 ** (-8.0 * (h + 1) / n_heads) for h in range(n_heads)], dtype=np.float32)

def dilated_window_attention(q, k, v, window, dilation, slopes):
    B, S, H, Dh = q.shape
    radius = window // (2 * dilation)
    blk = radius
    n = S // dilation
    nb = -(-n // blk)
    n_pad = nb * blk

    def residue_split(a):
        return a.reshape(B, n, dilation, H, Dh).transpose(0, 2, 1, 3, 4)

    def key_windows(a):
        ap = jnp.pad(a, ((0, 0), (0, 0), (blk, n_pad - n + blk), (0, 0), (0, 0)))
        ap = ap.reshape(B, dilation, nb + 2, blk, H, Dh)
        return jnp.concatenate([ap[:, :, 0:nb], ap[:, :, 1:nb + 1], ap[:, :, 2:nb + 2]], axis=3)

    qr = residue_split(q)
    qb = jnp.pad(qr, ((0, 0), (0, 0), (0, n_pad - n), (0, 0), (0, 0))).reshape(B, dilation, nb, blk, H, Dh)
    kb = key_windows(residue_split(k))
    vb = key_windows(residue_split(v))

    s = jnp.einsum('brnqhc,brnkhc->brnhqk', qb, kb).astype(jnp.float32)
    qi = jnp.arange(blk)[:, None]
    kj = jnp.arange(3 * blk)[None, :]
    rel = kj - qi - blk
    j_abs = jnp.arange(nb)[:, None, None] * blk + kj[None] - blk
    valid = (jnp.abs(rel)[None] <= radius) & (j_abs >= 0) & (j_abs < n)
    bias = -jnp.asarray(slopes)[:, None, None] * (dilation * jnp.abs(rel)).astype(jnp.float32)[None]
    s = jnp.where(valid[None, None, :, None], s + bias[None, None, None], MASK_VALUE)
    m = jnp.max(s, axis=-1, keepdims=True)
    p = jnp.exp(s - m)
    l = jnp.sum(p, axis=-1, keepdims=True)
    o = jnp.einsum('brnhqk,brnkhc->brnqhc', p.astype(v.dtype), vb).astype(jnp.float32)
    denom = l[..., 0].transpose(0, 1, 2, 4, 3)
    lse = (m[..., 0] + jnp.log(l[..., 0])).transpose(0, 1, 2, 4, 3)
    o = o / denom[..., None]
    o = o.reshape(B, dilation, n_pad, H, Dh)[:, :, :n].transpose(0, 2, 1, 3, 4).reshape(B, S, H, Dh)
    lse = lse.reshape(B, dilation, n_pad, H)[:, :, :n].transpose(0, 2, 1, 3).reshape(B, S, H)
    return o, lse

def dilated_attention_mixture(q, k, v, slopes):
    outs, lses = [], []
    for window, dilation in DILATED_PATTERNS:
        o, lse = dilated_window_attention(q, k, v, window, dilation, slopes)
        outs.append(o)
        lses.append(lse)
    wts = jax.nn.softmax(jnp.stack(lses, axis=0), axis=0)
    return jnp.sum(wts[..., None] * jnp.stack(outs, axis=0), axis=0)

def short_conv(u, w, b):
    L = u.shape[1]
    half = SHORT_CONV // 2
    up = jnp.pad(u, ((0, 0), (half, half), (0, 0)))
    y = up[:, 0:L] * w[0]
    for i in range(1, SHORT_CONV):
        y = y + up[:, i:i + L] * w[i]
    return y + b

def hyena_filters(L, w1, b1, w2, b2, w3, b3, w4, freq):
    f32 = lambda a: a.astype(jnp.float32)
    t = jnp.linspace(0.0, 1.0, L, dtype=jnp.float32)[:, None]
    wpos = 2.0 * math.pi * jnp.arange(L, dtype=jnp.float32)[:, None] / L
    bands = jnp.linspace(1e-4, FILTER_BANDS - 1, FILTER_BANDS, dtype=jnp.float32)[None]
    feats = jnp.concatenate([t, jnp.cos(bands * wpos), -jnp.sin(bands * wpos)], axis=-1)
    fr = f32(freq)
    h = jnp.sin(fr * (feats @ f32(w1) + f32(b1)))
    h = jnp.sin(fr * (h @ f32(w2) + f32(b2)))
    h = jnp.sin(fr * (h @ f32(w3) + f32(b3)))
    h = (h @ f32(w4)).reshape(L, HYENA_ORDER, 2, HYENA_WIDTH)
    min_decay = math.log(DECAY_TARGET) / FAST_DECAY_PCT
    max_decay = math.log(DECAY_TARGET) / SLOW_DECAY_PCT
    deltas = jnp.linspace(min_decay, max_decay, HYENA_WIDTH, dtype=jnp.float32)
    decay = jnp.exp(-t * jnp.abs(deltas))
    return h * decay[:, None, None, :]

def bidirectional_long_conv(u, h_fwd, h_bwd, skip):
    L = u.shape[1]
    kern = jnp.concatenate([h_fwd, jnp.zeros_like(h_fwd[:1]), h_bwd[:0:-1]], axis=0)
    uf = u.astype(jnp.float32)
    U = jnp.fft.rfft(uf, n=2 * L, axis=1)
    K = jnp.fft.rfft(kern, n=2 * L, axis=0)
    y = jnp.fft.irfft(U * K[None], n=2 * L, axis=1)[:, :L]
    return y + uf * skip.astype(jnp.float32)

def hyena_operator(u, sw, sb, w1, b1, w2, b2, w3, b3, w4, freq, skip):
    L = u.shape[1]
    uc = short_conv(u, sw, sb)
    v, x1, x2 = jnp.split(uc, 3, axis=-1)
    filt = hyena_filters(L, w1, b1, w2, b2, w3, b3, w4, freq)
    z = x1.astype(jnp.float32) * bidirectional_long_conv(v, filt[:, 0, 0], filt[:, 0, 1], skip[0])
    return x2.astype(jnp.float32) * bidirectional_long_conv(z, filt[:, 1, 0], filt[:, 1, 1], skip[1])

def expert_choice_ffn(x, w_router, w_gate, w_up, w_down):
    B, S, D = x.shape
    N = B * S
    cap = EC_CAPACITY * N // N_EXPERTS
    xt = x.reshape(N, D)
    affinity = jax.nn.softmax((xt @ w_router).astype(jnp.float32), axis=-1)
    gates, idx = lax.top_k(affinity.T, cap)

    def one_expert(args):
        ids, g, wg, wu, wd = args
        xe = xt[ids]
        hdn = jax.nn.silu(xe @ wg) * (xe @ wu)
        return (hdn @ wd) * g[:, None].astype(x.dtype)

    ye = lax.map(one_expert, (idx, gates, w_gate, w_up, w_down))
    out = jnp.zeros_like(xt).at[idx.reshape(-1)].add(ye.reshape(-1, D))
    return out.reshape(B, S, D)

def encoder_trunk(x, norm_mix_g, w_in, short_w, short_b, filt_w1, filt_b1, filt_w2, filt_b2,
                  filt_w3, filt_b3, filt_w4, filt_freq, hyena_skip, attn_out_g, hyena_out_g,
                  w_out, norm_ffn_g, w_router, w_gate, w_up, w_down, final_g):
    B, S, _ = x.shape
    slopes = alibi_slopes(N_ATTN_HEADS)
    for l in range(DEPTH):
        h = rms_norm(x, norm_mix_g[l])
        proj = h @ w_in[l]
        q, k, v, u = jnp.split(proj, [ATTN_WIDTH, 2 * ATTN_WIDTH, 3 * ATTN_WIDTH], axis=-1)
        q = q.reshape(B, S, N_ATTN_HEADS, HEAD_DIM) * (HEAD_DIM ** -0.5)
        k = k.reshape(B, S, N_ATTN_HEADS, HEAD_DIM)
        v = v.reshape(B, S, N_ATTN_HEADS, HEAD_DIM)
        attn = dilated_attention_mixture(q, k, v, slopes).reshape(B, S, ATTN_WIDTH)
        hy = hyena_operator(u, short_w[l], short_b[l], filt_w1[l], filt_b1[l], filt_w2[l], filt_b2[l],
                            filt_w3[l], filt_b3[l], filt_w4[l], filt_freq[l], hyena_skip[l])
        mixed = jnp.concatenate([rms_norm(attn, attn_out_g[l]), rms_norm(hy, hyena_out_g[l])], axis=-1).astype(x.dtype)
        x = x + mixed @ w_out[l]
        x = x + expert_choice_ffn(rms_norm(x, norm_ffn_g[l]), w_router[l], w_gate[l], w_up[l], w_down[l])
    return rms_norm(x, final_g)

def setup_inputs(seed: int = 0) -> dict:
    key = jax.random.key(seed)
    ks = jax.random.split(key, 24)
    nrm = lambda k, shape, scale: jax.random.normal(k, shape, jnp.float32) * scale
    gain = lambda k, shape: 1.0 + 0.02 * jax.random.normal(k, shape, jnp.float32)
    return {
        'x_prompt': nrm(ks[0], (BATCH, SEQ, D_MODEL), 1.0),
        'x_sample': nrm(ks[1], (DEC_BATCH, DEC_SEQ, D_MODEL), 1.0),
        'norm_mix_g': gain(ks[2], (DEPTH, D_MODEL)),
        'w_in': nrm(ks[3], (DEPTH, D_MODEL, IN_WIDTH), D_MODEL ** -0.5),
        'short_w': nrm(ks[4], (DEPTH, SHORT_CONV, 3 * HYENA_WIDTH), SHORT_CONV ** -0.5),
        'short_b': nrm(ks[5], (DEPTH, 3 * HYENA_WIDTH), 0.02),
        'filt_w1': nrm(ks[6], (DEPTH, FILTER_EMB, FILTER_HIDDEN), FILTER_EMB ** -0.5),
        'filt_b1': nrm(ks[7], (DEPTH, FILTER_HIDDEN), 0.1),
        'filt_w2': nrm(ks[8], (DEPTH, FILTER_HIDDEN, FILTER_HIDDEN), FILTER_HIDDEN ** -0.5),
        'filt_b2': nrm(ks[9], (DEPTH, FILTER_HIDDEN), 0.1),
        'filt_w3': nrm(ks[10], (DEPTH, FILTER_HIDDEN, FILTER_HIDDEN), FILTER_HIDDEN ** -0.5),
        'filt_b3': nrm(ks[11], (DEPTH, FILTER_HIDDEN), 0.1),
        'filt_w4': nrm(ks[12], (DEPTH, FILTER_HIDDEN, HYENA_ORDER * 2 * HYENA_WIDTH), 0.1 * FILTER_HIDDEN ** -0.5),
        'filt_freq': gain(ks[13], (DEPTH, FILTER_HIDDEN)),
        'hyena_skip': nrm(ks[14], (DEPTH, HYENA_ORDER, HYENA_WIDTH), 1.0),
        'attn_out_g': gain(ks[15], (DEPTH, ATTN_WIDTH)),
        'hyena_out_g': gain(ks[16], (DEPTH, HYENA_WIDTH)),
        'w_out': nrm(ks[17], (DEPTH, D_MODEL, D_MODEL), D_MODEL ** -0.5),
        'norm_ffn_g': gain(ks[18], (DEPTH, D_MODEL)),
        'w_router': nrm(ks[19], (DEPTH, D_MODEL, N_EXPERTS), D_MODEL ** -0.5),
        'w_gate': nrm(ks[20], (DEPTH, N_EXPERTS, D_MODEL, D_EXPERT), D_MODEL ** -0.5),
        'w_up': nrm(ks[21], (DEPTH, N_EXPERTS, D_MODEL, D_EXPERT), D_MODEL ** -0.5),
        'w_down': nrm(ks[22], (DEPTH, N_EXPERTS, D_EXPERT, D_MODEL), D_EXPERT ** -0.5),
        'final_g': gain(ks[23], (D_MODEL,)),
    }

def reference(x_prompt, x_sample, norm_mix_g, w_in, short_w, short_b, filt_w1, filt_b1, filt_w2,
              filt_b2, filt_w3, filt_b3, filt_w4, filt_freq, hyena_skip, attn_out_g, hyena_out_g,
              w_out, norm_ffn_g, w_router, w_gate, w_up, w_down, final_g):
    params = (norm_mix_g, w_in, short_w, short_b, filt_w1, filt_b1, filt_w2, filt_b2, filt_w3,
              filt_b3, filt_w4, filt_freq, hyena_skip, attn_out_g, hyena_out_g, w_out, norm_ffn_g,
              w_router, w_gate, w_up, w_down, final_g)
    y_prompt = encoder_trunk(x_prompt, *params)
    y_sample = encoder_trunk(x_sample, *params)
    return (y_prompt, y_sample)


_drawn_inputs = setup_inputs


def setup_inputs(seed=0):
    import zlib

    import numpy as np

    out = dict(_drawn_inputs(seed))
    spreads = {}
    factors = {'filt_freq': 6.315,
     'attn_out_g': 4.315,
     'hyena_out_g': 4.484,
     'norm_ffn_g': 4.434,
     'final_g': 2.902}
    for name, (base, spread) in spreads.items():
        noise = np.random.default_rng([zlib.crc32(name.encode()), seed]).standard_normal(out[name].shape)
        drawn = base * np.exp(spread * noise) if base else spread * noise
        out[name] = jnp.asarray(drawn.astype(out[name].dtype))
    for name, factor in factors.items():
        out[name] = (out[name] * factor).astype(out[name].dtype)
    return out
```

```python
import math
from contextlib import ExitStack

import numpy as np

import concourse.bass as bass
from concourse import mybir

F32 = mybir.dt.float32
BF16 = mybir.dt.bfloat16
U32 = mybir.dt.uint32
ALU = mybir.AluOpType
ACT = mybir.ActivationFunctionType
AX = mybir.AxisListType

P = 128
D = 1024
KD = D // P
W = 512
HEADS, DH = 8, 64
L_PROMPT, L_SAMPLE = 256, 512
TOKENS = L_PROMPT + L_SAMPLE
TILES = TOKENS // P
FIRST_TILE = (0, L_PROMPT // P)
GROUP_LEN = (L_PROMPT, L_SAMPLE)
PATTERNS = ((128, 1), (512, 4), (2048, 16))
NEG = -1e30
EPS = 1e-6
FILTER_EMB, FILTER_HID, ORDER = 33, 64, 2
EXPERTS, FF = 16, 2816
CAP_SAMPLE, CAP_PROMPT = 2 * L_SAMPLE // EXPERTS, 2 * L_PROMPT // EXPERTS
SLOTS = CAP_SAMPLE + CAP_PROMPT
BIAS_OFF = L_SAMPLE - P
BIAS_W = L_SAMPLE + BIAS_OFF
FT = FF // P
CHUNK = 2
CHUNKS = FT // CHUNK
RING = 4
ROUND_MAGIC = 1.5 * 2.0 ** 23
TWO_PI_HI = 6.28125
TWO_PI_LO = 2.0 * math.pi - TWO_PI_HI
PI_IN = 3.1415925

KB = 256


def group_of(tile):
    return 0 if tile < FIRST_TILE[1] else 1


def encoder(nc, t, out_prompt, out_sample):
    xn_dram = nc.dram_tensor("xn_rows", [TOKENS, D], F32).ap()
    y_dram = nc.dram_tensor("y_rows", [TOKENS, D], F32).ap()

    with ExitStack() as ctx:
        def sb(name, shape, dt=F32):
            return ctx.enter_context(nc.sbuf_tensor(name, shape, dt))

        def sem(name):
            return ctx.enter_context(nc.semaphore(name))

        xreg = sb("xreg", [P, 24 * KB])
        hreg = sb("hreg", [P, 24 * KB])
        wreg = sb("wreg", [P, 32 * KB])
        areg = sb("areg", [P, 12 * KB])
        vreg = sb("vreg", [P, 12 * KB])
        breg = sb("breg", [P, 96 * KB])
        ident = sb("ident", [P, P])
        gbc = sb("gbc", [P, D])
        ssq = sb("ssq", [P, 30])
        msq = sb("msq", [P, 30])
        root = sb("root", [P, 30])
        rinv = sb("rinv", [P, 30])
        negmax = sb("negmax", [P, TILES * HEADS])
        den = sb("den", [P, TILES * HEADS])
        rden = sb("rden", [P, TILES * HEADS])
        wrt = sb("wrt", [P, KD, EXPERTS])
        convw = sb("convw", [P, 4, 12])

        def view(reg, kb, shape, parts=P, dt=None):
            n = int(np.prod(shape))
            start = int(kb * KB)
            v = reg[0:parts, start:start + n]
            names = "abcd"[:len(shape)]
            if len(shape) == 1:
                return v
            return v.rearrange("p (" + " ".join(names) + ") -> p " + " ".join(names),
                               **{c: s for c, s in zip(names[:-1], shape[:-1])})

        x = view(xreg, 0, (TILES, D))
        hT = view(hreg, 0, (KD, TOKENS))
        wbuf = [view(wreg, 16 * s, (KD, W)) for s in range(2)]
        attn = view(areg, 0, (TILES, W))
        hrow = [view(areg, 4 * s, (D,)) for s in range(2)]
        uv = view(vreg, 0, (TILES, W))
        qT = view(breg, 0, (4, TOKENS))
        kT = view(breg, 12, (4, TOKENS))
        vrow = view(breg, 24, (TILES, W))
        bias = view(breg, 36, (HEADS, BIAS_W))
        s_sb = [view(breg, 64 + 2 * s, (W,)) for s in range(2)]
        p_sb = [view(breg, 68 + 2 * s, (W,)) for s in range(2)]
        pT = [view(breg, 72 + 2 * s, (4, P)) for s in range(2)]
        feats = view(breg, 64, (TOKENS,), FILTER_EMB)
        mlp_y = view(breg, 67, (TOKENS,), FILTER_HID)
        mlp_k = view(breg, 70, (TOKENS,), FILTER_HID)
        mlp_w = view(breg, 73, (3, FILTER_HID), FILTER_HID)
        mlp_b = view(breg, 74, (4,), FILTER_HID)
        junk1 = view(breg, 76, (D,))
        hid = view(breg, 92, (TOKENS,), FILTER_HID)
        x12 = view(breg, 0, (2, TILES, W))
        dft = [view(breg, 24, (4, 2, L_PROMPT)), view(breg, 32, (4, 4, L_SAMPLE))]
        decay = view(breg, 64, (TILES, W))
        kf = view(breg, 76, (2, 4, W))
        uraw = [view(breg, 76 + 4 * s, (TOKENS + 4,)) for s in range(2)]
        uc = [view(breg, 84 + 4 * s, (TOKENS + 2,)) for s in range(2)]
        zsel = view(breg, 95, (2, P))
        ab = view(hreg, 0, (2, 4, W))
        prod = [view(hreg, 16 + 2 * s, (W,)) for s in range(2)]
        w4 = view(wreg, 0, (2, ORDER, W), FILTER_HID)
        w4b_skip = view(gbc, 0, (ORDER, W), FILTER_HID + 1)
        ring_g = [view(breg, 24 * s, (KD, CHUNK * P)) for s in range(RING)]
        ring_u = [view(breg, 24 * s + 8, (KD, CHUNK * P)) for s in range(RING)]
        ring_d = [view(breg, 24 * s + 16, (CHUNK, D)) for s in range(RING)]
        xg = view(xreg, 0, (D,), SLOTS)
        ysc = view(xreg, 4, (D,), SLOTS)
        xeT = view(xreg, 8, (KD, SLOTS))
        yT = view(xreg, 11, (KD, SLOTS))
        hbuf = [view(xreg, 14 + s * 0.5, (SLOTS,)) for s in range(2)]
        silu = [view(xreg, 15 + s * 0.5, (SLOTS,)) for s in range(2)]
        affT = view(xreg, 16, (TOKENS,), EXPERTS)
        lmax = view(xreg, 19, (TILES,))
        lsum = view(xreg, 19.125, (TILES,))
        aff = view(xreg, 19.5, (TILES, EXPERTS))
        vals = view(xreg, 20, (SLOTS,), EXPERTS)
        idxf = view(xreg, 20.5, (SLOTS,), EXPERTS)
        idxu = view(xreg, 21, (SLOTS,), EXPERTS).bitcast(U32)
        idxT = view(xreg, 21.5, (EXPERTS + 1,), SLOTS).bitcast(U32)
        gateT = view(xreg, 22, (EXPERTS,), SLOTS)
        idx_gather = view(xreg, 22.25, (1,), SLOTS).bitcast(U32)
        idx_scatter = view(xreg, 22.5, (1,), SLOTS).bitcast(U32)
        gate_now = view(xreg, 22.75, (1,), SLOTS)
        yfin = view(hreg, 0, (TILES, D))

        bank = [ctx.enter_context(nc.psum_tensor(f"bank{i}", [P, 512], F32)) for i in range(8)]

        def cols(b, n, w, parts=P):
            return bank[b][0:parts, 0:n * w].rearrange("p (n w) -> p n w", n=n)

        x_in = [sem(f"x_in{i}") for i in range(TILES)]
        consts_in, mlp_in, bias_in, gain_in = (sem(n) for n in ("consts_in", "mlp_in", "bias_in", "gain_in"))
        w_in_sem = [sem(f"wbuf_in{s}") for s in range(2)]
        hy_in, w4_in = sem("hyena_tables_in"), sem("w4_in")
        act_step, dve_step = sem("act_step"), sem("dve_step")
        ssq_done, msq_done, root_done = sem("ssq_done"), sem("msq_done"), sem("root_done")
        mlp_mm, mlp_pre, mlp_sin = sem("mlp_mm"), sem("mlp_pre"), sem("mlp_sin")
        h_row, h_turned, h_act, h_dve = (sem(n) for n in ("h_row", "h_turned", "h_evac_act", "h_evac_dve"))
        qk_mm, qk_act, qk_dve = sem("qk_mm"), sem("qk_evac_act"), sem("qk_evac_dve")
        v_mm, v_act, v_dve = sem("v_mm"), sem("v_evac_act"), sem("v_evac_dve")
        score_mm, biased, exp_done = sem("score_mm"), sem("biased"), sem("exp_done")
        pt_mm, pt_done, pv_mm, attn_row = sem("pt_mm"), sem("pt_done"), sem("pv_mm"), sem("attn_row")
        u_mm, u_act, u_dve, pads = sem("u_mm"), sem("u_raw_act"), sem("u_raw_dve"), sem("pads")
        conv_mid, conv_done, u_turned = sem("conv_mid"), sem("conv_done"), sem("u_turned")
        ut_act, ut_dve = sem("u_row_act"), sem("u_row_dve")
        w4_done = sem("w4_done")
        ab_mm, ab_done, kf_mm, kf_done = sem("ab_mm"), sem("ab_done"), sem("kf_mm"), sem("kf_done")
        uf_mm, y_done, inv_mm, z_done = sem("uf_mm"), sem("y_done"), sem("inv_mm"), sem("z_done")
        mix_row, mix_turned, mix_act, mix_dve = (sem(n) for n in ("mix_row", "mix_turned", "mix_evac_act", "mix_evac_dve"))
        out_mm, res_done, y_init = sem("out_mm"), sem("residual_done"), sem("y_init")
        xn_row, xn_turned, xn_act, xn_dve, xn_out = (sem(n) for n in ("xn_row", "xn_turned", "xn_evac_act", "xn_evac_dve", "xn_out"))
        logit_mm, logit_off, logit_exp, aff_done = (sem(n) for n in ("logit_mm", "logit_off", "logit_exp", "aff_done"))
        affT_mm, chosen, chosen_mm, chosen_done = (sem(n) for n in ("affT_mm", "chosen", "chosen_mm", "chosen_done"))
        gu_in = [sem(f"gate_up_in{s}") for s in range(RING)]
        dn_in = [sem(f"down_in{s}") for s in range(RING)]
        first_index = sem("first_index")
        pool_step, gathered, scattered, gate_set = (sem(n) for n in ("pool_step", "gathered", "scattered", "gate_set"))
        xe_mm, xe_done, gate_mm, up_mm = sem("xe_mm"), sem("xe_done"), sem("gate_mm"), sem("up_mm")
        silu_done, h_done, down_mm = sem("silu_done"), sem("h_done"), sem("down_mm")
        yT_done, yt_mm, ysc_done = sem("yT_done"), sem("yt_mm"), sem("ysc_done")
        yfin_in = [sem(f"yfin_in{i}") for i in range(TILES)]
        fin_row, out_done = sem("fin_row"), sem("out_done")

        N_X, N_MIX, N_FFN, N_FIN = 0, 6, 18, 24
        HY = [(0, 0), (1, 0), (0, 1), (1, 1)]
        HY_N = [GROUP_LEN[g] // P for g, _ in HY]
        HY_BASE = [sum(HY_N[:q]) for q in range(5)]
        UNITS = TILES * HEADS
        NU = 12

        def attn_cols(tile):
            g = group_of(tile)
            tok0 = FIRST_TILE[g] * P
            return tok0, GROUP_LEN[g], BIAS_OFF - (tile - FIRST_TILE[g]) * P

        def uc_col(tile):
            return tile * P if tile < FIRST_TILE[1] else 2 + tile * P

        block = ctx.enter_context(nc.Block())

        @block.sync
        def _(sp):
            sp.dma_start(x[:, 0, :], t["x_prompt"][0, 0:P, :]).then_inc(x_in[0], 16)
            sp.dma_start(ident[:, :], t["ident"]).then_inc(consts_in, 16)
            sp.dma_start(feats, t["features"]).then_inc(mlp_in, 16)
            sp.dma_start(mlp_w[0:FILTER_EMB, 0, :], t["filt_w1"][0]).then_inc(mlp_in, 16)
            sp.dma_start(mlp_w[:, 1, :], t["filt_w2"][0]).then_inc(mlp_in, 16)
            sp.dma_start(mlp_w[:, 2, :], t["filt_w3"][0]).then_inc(mlp_in, 16)
            for n, name in enumerate(("filt_b1", "filt_b2", "filt_b3", "filt_freq")):
                sp.dma_start(mlp_b[:, n:n + 1], t[name].rearrange("o h -> h o")).then_inc(mlp_in, 16)
            for i in range(1, TILES):
                g = group_of(i)
                src = (t["x_prompt"], t["x_sample"])[g][0, (i - FIRST_TILE[g]) * P:(i - FIRST_TILE[g] + 1) * P, :]
                sp.dma_start(x[:, i, :], src).then_inc(x_in[i], 16)
            sp.dma_start(gbc[:, :], t["norm_mix_g"][0].partition_broadcast(P)).then_inc(gain_in, 16)

            w_in = t["w_in"][0].rearrange("(k p) n -> p k n", p=P)
            def load_chunk(n):
                sp.dma_start(wbuf[n % 2], w_in[:, :, n * W:(n + 1) * W]).then_inc(w_in_sem[n % 2], 16)

            load_chunk(0)
            load_chunk(1)
            sp.dma_start(bias, t["attn_bias"].rearrange("p (h c) -> p h c", h=HEADS)).then_inc(bias_in, 16)
            for n in range(3):
                sp.dma_start(convw[:, n, :], t["short_w"][0, n].rearrange("(c p) -> p c", p=P),
                             allow_slow_non_contiguous=True).then_inc(consts_in, 16)
            sp.dma_start(convw[:, 3, :], t["short_b"][0].rearrange("(c p) -> p c", p=P),
                         allow_slow_non_contiguous=True).then_inc(consts_in, 16)
            sp.dma_start(wrt[:, :, :], t["w_router"][0].rearrange("(k p) e -> p k e", p=P)).then_inc(consts_in, 16)
            sp.wait_ge(qk_mm, 4)
            load_chunk(2)
            sp.wait_ge(qk_mm, 8)
            load_chunk(3)
            sp.wait_ge(v_mm, TILES)
            load_chunk(4)
            sp.wait_ge(attn_row, TILES)
            for g in range(2):
                tab = t[("dft_prompt", "dft_sample")[g]].rearrange("m (i p) f -> p m i f", p=P)
                for m in range(4):
                    sp.dma_start(dft[g][:, m], tab[:, m]).then_inc(hy_in, 16)
            sp.dma_start(decay, t["decay"].rearrange("(i p) c -> p i c", p=P)).then_inc(hy_in, 16)
            w4_src = t["filt_w4"][0].rearrange("h (o d c) -> h o d c", o=ORDER, d=2)
            sp.wait_ge(h_row, TILES)
            sp.dma_start(w4b_skip[0:FILTER_HID], w4_src[:, :, 1, :]).then_inc(w4_in, 16)
            sp.dma_start(w4b_skip[FILTER_HID:FILTER_HID + 1], t["hyena_skip"]).then_inc(w4_in, 16)
            sp.wait_ge(u_mm, 4)
            load_chunk(5)
            sp.wait_ge(u_mm, 8)
            sp.dma_start(w4[:, 0], w4_src[:, :, 0, :]).then_inc(w4_in, 16)
            w_out = t["w_out"][0].rearrange("(k p) n -> p k n", p=P)
            sp.wait_ge(u_mm, 12)
            sp.dma_start(wbuf[1], w_out[:, :, 0:W]).then_inc(w_in_sem[1], 16)
            sp.wait_ge(ab_mm, 2 * HY_BASE[4])
            sp.dma_start(wbuf[0], w_out[:, :, W:D]).then_inc(w_in_sem[0], 16)
            sp.dma_start(gbc[:, 0:W], t["attn_out_g"][0].partition_broadcast(P)).then_inc(gain_in, 16)
            sp.dma_start(gbc[:, W:D], t["hyena_out_g"][0].partition_broadcast(P)).then_inc(gain_in, 16)

            w_gate, w_up, w_down = (t[n][0] for n in ("w_gate", "w_up", "w_down"))

            def load_expert_chunk(e, c):
                s, f0 = c % RING, c * CHUNK * P
                for ring, w in ((ring_g, w_gate), (ring_u, w_up)):
                    src = w[bass.ds(e, 1), :, f0:f0 + CHUNK * P].rearrange("o (k p) f -> p (o k) f", p=P)
                    sp.dma_start(ring[s], src).then_inc(gu_in[s], 16)

            def load_expert_down(e, c):
                f0 = c * CHUNK * P
                src = w_down[bass.ds(e, 1), f0:f0 + CHUNK * P, :].rearrange("o (j p) d -> p (o j) d", p=P)
                sp.dma_start(ring_d[c % RING], src).then_inc(dn_in[c % RING], 16)

            sp.wait_ge(z_done, HY_BASE[4])
            for c in range(RING):
                load_expert_chunk(0, c)
                load_expert_down(0, c)
            sp.wait_ge(mix_row, 2 * TILES)
            sp.dma_start(gbc[:, :], t["norm_ffn_g"][0].partition_broadcast(P)).then_inc(gain_in, 16)
            for i in range(TILES):
                sp.wait_ge(res_done, 2 * (i + 1))
                sp.dma_start(y_dram[i * P:(i + 1) * P, :], x[:, i, :]).then_inc(y_init, 16)
                sp.wait_ge(xn_row, 2 * (i + 1))
                sp.dma_start(xn_dram[i * P:(i + 1) * P, 0:W], attn[:, i, :]).then_inc(xn_out, 16)
                sp.dma_start(xn_dram[i * P:(i + 1) * P, W:D], uv[:, i, :]).then_inc(xn_out, 16)
            sp.dma_start(gbc[:, :], t["final_g"].partition_broadcast(P)).then_inc(gain_in, 16)

            def refill(e, c, base, last_user):
                sp.wait_ge(up_mm, base + 2 * last_user + 2)
                load_expert_chunk(e, c)
                sp.wait_ge(down_mm, base + 2 * last_user + 4)
                load_expert_down(e, c)

            with sp.Fori(0, EXPERTS - 1) as e:
                for c in range(RING, CHUNKS):
                    refill(e, c, e * FT, c - RING)
                for c in range(RING):
                    refill(e + 1, c, e * FT, CHUNKS - 1 - (CHUNKS - 1 - c) % RING)
            for c in range(RING, CHUNKS):
                refill(EXPERTS - 1, c, (EXPERTS - 1) * FT, c - RING)

            sp.wait_ge(scattered, 16 * EXPERTS)
            for i in range(TILES):
                sp.dma_start(yfin[:, i, :], y_dram[i * P:(i + 1) * P, :]).then_inc(yfin_in[i], 16)
            for i in range(TILES):
                g = group_of(i)
                dst = (out_prompt, out_sample)[g][0, (i - FIRST_TILE[g]) * P:(i - FIRST_TILE[g] + 1) * P, :]
                sp.wait_ge(fin_row, i + 1)
                sp.dma_start(dst, yfin[:, i, :]).then_inc(out_done, 16)
            sp.wait_ge(out_done, 16 * TILES)
            sp.wait_ge(y_init, 16 * TILES)
            sp.wait_ge(xn_out, 32 * TILES)

        @block.tensor
        def _(pe):
            def filter_layer(n):
                if n == 0:
                    pe.wait_ge(mlp_in, 16 * 8)
                else:
                    pe.wait_ge(mlp_sin, n)
                for g in range(2):
                    lo, n_pos = FIRST_TILE[g] * P, GROUP_LEN[g]
                    lhsT = mlp_w[0:FILTER_EMB, 0, :] if n == 0 else mlp_w[:, n, :]
                    rhs = (feats if n == 0 else hid)[:, lo:lo + n_pos]
                    mm = pe.matmul(bank[6 + g][0:FILTER_HID, 0:n_pos], lhsT, rhs, start=True, stop=True)
                mm.then_inc(mlp_mm, 1)

            def turn(rows, b, turned):
                for half in range(2):
                    for k in range(4):
                        mm = pe.transpose(cols(b + half, 4, P)[:, k, :], rows[half][:, k * P:(k + 1) * P], ident[:, :])
                    mm.then_inc(turned, 1)

            filter_layer(0)
            pe.wait_ge(consts_in, 96)
            for i in range(TILES):
                pe.wait_ge(h_row, i + 1)
                if i >= 2:
                    pe.wait_ge(h_act, i - 1)
                    pe.wait_ge(h_dve, i - 1)
                turn([hrow[i % 2][:, 0:W], hrow[i % 2][:, W:D]], 2 * (i % 2), h_turned)
            filter_layer(1)

            def project(c, m, r, done, freed):
                for ready, count in freed:
                    pe.wait_ge(ready, count)
                b = 2 * (r % 2)
                for k in range(KD):
                    lhsT = wbuf[c % 2][:, k, m * P:(m + 1) * P]
                    pe.matmul(bank[b][:, 0:L_SAMPLE], lhsT, hT[:, k, L_PROMPT:TOKENS],
                              start=(k == 0), stop=(k == KD - 1))
                    mm = pe.matmul(bank[b + 1][:, 0:L_PROMPT], lhsT, hT[:, k, 0:L_PROMPT],
                                   start=(k == 0), stop=(k == KD - 1))
                mm.then_inc(done, 1)

            pe.wait_ge(h_act, TILES)
            pe.wait_ge(h_dve, TILES)
            for c in range(2):
                pe.wait_ge(w_in_sem[c], 16)
                for m in range(4):
                    r = 4 * c + m
                    project(c, m, r, qk_mm, [(qk_act, r - 1), (qk_dve, r - 1)] if r >= 2 else [])
                if c == 0:
                    filter_layer(2)
            pe.wait_ge(w_in_sem[0], 32)
            for i in range(TILES):
                if i >= 2:
                    pe.wait_ge(v_act if i % 2 == 0 else v_dve, i // 2)
                for k in range(KD):
                    mm = pe.matmul(bank[4 + i % 2][:, :], hT[:, k, i * P:(i + 1) * P], wbuf[0][:, k, :],
                                   start=(k == 0), stop=(k == KD - 1))
                mm.then_inc(v_mm, 1)

            def scores(u):
                tile, head = divmod(u, HEADS)
                tok0, n_keys, _ = attn_cols(tile)
                lo = DH * (head % 2)
                if u >= 2:
                    pe.wait_ge(biased, u - 1)
                pe.matmul(bank[u % 2][:, 0:n_keys], qT[lo:lo + DH, head // 2, tile * P:(tile + 1) * P],
                          kT[lo:lo + DH, head // 2, tok0:tok0 + n_keys], start=True, stop=True).then_inc(score_mm, 1)

            def turn_probs(u):
                _, n_keys, _ = attn_cols(u // HEADS)
                pe.wait_ge(exp_done, u + 1)
                if u >= 2:
                    pe.wait_ge(pt_done, u - 1)
                for j in range(n_keys // P):
                    mm = pe.transpose(cols(2 + u % 2, 4, P)[:, j, :], p_sb[u % 2][:, j * P:(j + 1) * P], ident[:, :])
                mm.then_inc(pt_mm, 1)

            def times_v(u):
                tile, head = divmod(u, HEADS)
                tok0, n_keys, _ = attn_cols(tile)
                pe.wait_ge(pt_done, u + 1)
                if head == 0 and tile >= 2:
                    pe.wait_ge(attn_row, tile - 1)
                for j in range(n_keys // P):
                    mm = pe.matmul(bank[4 + tile % 2][:, head * DH:(head + 1) * DH], pT[u % 2][:, j, :],
                                   vrow[:, tok0 // P + j, head * DH:(head + 1) * DH],
                                   start=(j == 0), stop=(j == n_keys // P - 1))
                mm.then_inc(pv_mm, 1)

            pe.wait_ge(qk_act, 8)
            pe.wait_ge(qk_dve, 8)
            pe.wait_ge(v_act, TILES // 2)
            pe.wait_ge(v_dve, TILES // 2)
            for s in range(UNITS + 3):
                if s < UNITS:
                    scores(s)
                if 2 <= s < UNITS + 2:
                    turn_probs(s - 2)
                if s >= 3:
                    times_v(s - 3)

            def turn_u(r):
                pe.wait_ge(conv_done, r + 1)
                if r >= 2:
                    pe.wait_ge(ut_act, r - 1)
                    pe.wait_ge(ut_dve, r - 1)
                for i in range(TILES):
                    mm = pe.transpose(cols(4 + 2 * (r % 2) + i // 3, 4, P)[:, i % 3, :],
                                      uc[r % 2][:, uc_col(i):uc_col(i) + P], ident[:, :])
                    if i % 3 == 2:
                        mm.then_inc(u_turned, 1)

            pe.wait_ge(biased, UNITS)
            pe.wait_ge(pt_done, UNITS)
            pe.wait_ge(attn_row, TILES)
            for r in range(NU):
                c = 3 + r // 4
                if r % 4 == 0:
                    pe.wait_ge(w_in_sem[c % 2], 16 * (c // 2 + 1))
                project(c, r % 4, r, u_mm, [(u_act, r - 1), (u_dve, r - 1)] if r >= 2 else [])
                if r >= 1:
                    turn_u(r - 1)
            turn_u(NU - 1)

            pe.wait_ge(hy_in, 16 * 9)
            pe.wait_ge(w4_in, 48)
            pe.wait_ge(w4_done, 1)
            pe.wait_ge(u_act, NU)
            pe.wait_ge(u_dve, NU)
            pe.wait_ge(ut_act, NU)
            pe.wait_ge(ut_dve, NU)
            for q, (g, o) in enumerate(HY):
                n, base = HY_N[q], HY_BASE[q]
                tile0 = FIRST_TILE[g]
                cos_half, sin_half, cos_lag, sin_lag = (dft[g][:, m] for m in range(4))
                for i in range(n):
                    if i >= 2:
                        pe.wait_ge(ab_done, 2 * (base + i - 1))
                    b = 2 * (i % 2)
                    h_cols = hid[:, (tile0 + i) * P:(tile0 + i + 1) * P]
                    mm = pe.matmul(bank[b][:, :], h_cols, w4[:, 0, o, :], start=True, stop=(i != 0))
                    if i == 0:
                        mm = pe.matmul(bank[b][:, :], zsel[0:FILTER_HID + 1, g, :], w4b_skip[:, o, :],
                                       start=False, stop=True)
                    mm.then_inc(ab_mm, 1)
                    pe.matmul(bank[b + 1][:, :], h_cols, w4[:, 1, o, :], start=True, stop=True).then_inc(ab_mm, 1)
                if q >= 1:
                    pe.wait_ge(z_done, base)
                for f in range(n):
                    if f >= 2:
                        pe.wait_ge(kf_done, 2 * (base + f - 1))
                    for part, table in enumerate((cos_lag, sin_lag)):
                        for i in range(n):
                            if f == 0:
                                pe.wait_ge(ab_done, 2 * (base + i + 1))
                            mm = pe.matmul(bank[4 + 2 * (f % 2) + part][:, :], table[:, i, f * P:(f + 1) * P],
                                           ab[:, part, i, :], start=(i == 0), stop=(i == n - 1))
                        mm.then_inc(kf_mm, 1)
                for f in range(n):
                    if f >= 2:
                        pe.wait_ge(y_done, base + f - 1)
                    for part, table in enumerate((cos_half, sin_half)):
                        for i in range(n):
                            mm = pe.matmul(bank[2 * (f % 2) + part][:, :], table[:, i, f * P:(f + 1) * P],
                                           uv[:, tile0 + i, :], start=(i == 0), stop=(i == n - 1))
                        mm.then_inc(uf_mm, 1)
                pe.wait_ge(kf_done, 2 * (base + n))
                for i in range(n):
                    for f in range(n):
                        if i == 0:
                            pe.wait_ge(y_done, base + f + 1)
                        pe.matmul(bank[4 + i][:, :], cos_half[:, f, i * P:(i + 1) * P], ab[:, 0, f, :],
                                  start=(f == 0), stop=False)
                        mm = pe.matmul(bank[4 + i][:, :], sin_half[:, f, i * P:(i + 1) * P], ab[:, 1, f, :],
                                       start=False, stop=(f == n - 1))
                    mm.then_inc(inv_mm, 1)

            def turn_mix(i):
                pe.wait_ge(mix_row, 2 * (i + 1))
                if i >= 1:
                    pe.wait_ge(mix_act, i)
                    pe.wait_ge(mix_dve, i)
                turn([attn[:, i, :], uv[:, i, :]], 0, mix_turned)

            def project_out(i):
                pe.wait_ge(mix_act, i + 1)
                pe.wait_ge(mix_dve, i + 1)
                for half in range(2):
                    if i >= 1:
                        pe.wait_ge(res_done, 2 * i - 1 + half)
                    for k in range(KD):
                        mm = pe.matmul(bank[4 + half][:, :], hT[:, k, i * P:(i + 1) * P], wbuf[1 - half][:, k, :],
                                       start=(k == 0), stop=(k == KD - 1))
                    mm.then_inc(out_mm, 1)

            def turn_xn(i):
                pe.wait_ge(xn_row, 2 * (i + 1))
                if i >= 1:
                    pe.wait_ge(xn_act, i)
                    pe.wait_ge(xn_dve, i)
                turn([attn[:, i, :], uv[:, i, :]], 2, xn_turned)

            def logits(i):
                pe.wait_ge(xn_act, i + 1)
                pe.wait_ge(xn_dve, i + 1)
                for k in range(KD):
                    mm = pe.matmul(bank[6][:, i * EXPERTS:(i + 1) * EXPERTS], hT[:, k, i * P:(i + 1) * P],
                                   wrt[:, k, :], start=(k == 0), stop=(k == KD - 1))
                mm.then_inc(logit_mm, 1)

            pe.wait_ge(z_done, HY_BASE[4])
            pe.wait_ge(w_in_sem[1], 64)
            pe.wait_ge(w_in_sem[0], 64)
            turn_mix(0)
            for i in range(TILES):
                if i + 1 < TILES:
                    turn_mix(i + 1)
                project_out(i)
                if i >= 1:
                    turn_xn(i - 1)
                if i >= 2:
                    logits(i - 2)
            logits(TILES - 2)
            turn_xn(TILES - 1)
            logits(TILES - 1)

            pe.wait_ge(aff_done, 1)
            for i in range(TILES):
                b, col = (1, i * P) if i < FIRST_TILE[1] else (0, (i - FIRST_TILE[1]) * P)
                mm = pe.matmul(bank[b][0:EXPERTS, col:col + P], aff[:, i, :], ident[:, :], start=True, stop=True)
            mm.then_inc(affT_mm, 1)
            pe.wait_ge(chosen, 1)
            pe.matmul(bank[2][0:SLOTS, 0:EXPERTS], idxf, ident[0:EXPERTS, 0:EXPERTS], start=True, stop=True)
            pe.matmul(bank[3][0:SLOTS, 0:EXPERTS], vals, ident[0:EXPERTS, 0:EXPERTS],
                      start=True, stop=True).then_inc(chosen_mm, 1)

            def turn_in():
                for half in range(2):
                    for k in range(4):
                        mm = pe.transpose(cols(6 + half, 4, SLOTS)[:, k, :],
                                          xg[:, (4 * half + k) * P:(4 * half + k + 1) * P], ident[0:SLOTS, 0:SLOTS])
                    mm.then_inc(xe_mm, 1)

            def gate_up(e, j):
                c, s = j // CHUNK, (j // CHUNK) % RING
                uses = len(range(s, CHUNKS, RING))
                if j % CHUNK == 0:
                    pe.wait_ge(gu_in[s], e * (32 * uses) + 32 * (c // RING + 1))
                pe.wait_ge(h_done, e * FT + (j + 1))
                f0 = (j % CHUNK) * P
                for b, w, done in ((0, ring_g, gate_mm), (2, ring_u, up_mm)):
                    for k in range(KD):
                        mm = pe.matmul(bank[b + j % 2][:, 0:SLOTS], w[s][:, k, f0:f0 + P], xeT[:, k, :],
                                       start=(k == 0), stop=(k == KD - 1))
                    mm.then_inc(done, 1)

            def down(e, j):
                c, s = j // CHUNK, (j // CHUNK) % RING
                uses = len(range(s, CHUNKS, RING))
                if j % CHUNK == 0:
                    pe.wait_ge(dn_in[s], e * (16 * uses) + 16 * (c // RING + 1))
                pe.wait_ge(h_done, e * FT + (j + 3))
                for d in range(KD):
                    mm = pe.matmul(cols(4 + d // 4, 4, SLOTS)[:, d % 4, :], ring_d[s][:, j % CHUNK, d * P:(d + 1) * P],
                                   hbuf[j % 2], start=(j == 0 and d % 4 == 0), stop=(j == FT - 1),
                                   skip_group_check=True)
                mm.then_inc(down_mm, 1)

            pe.sem_inc(down_mm, 2)
            pe.wait_ge(gathered, 16)
            turn_in()
            with pe.Fori(0, EXPERTS) as e:
                pe.wait_ge(xe_done, e * 2 + 2)
                for j in range(FT):
                    gate_up(e, j)
                    if j >= 1:
                        down(e, j - 1)
                pe.wait_ge(gathered, e * 16 + 32)
                pe.wait_ge(gate_set, e + 1)
                turn_in()
                down(e, FT - 1)
                pe.wait_ge(yT_done, e * 2 + 2)
                pe.wait_ge(xe_done, e * 2 + 4)
                for half in range(2):
                    for k in range(4):
                        mm = pe.transpose(cols(6 + half, 4, P, SLOTS)[:, k, :], yT[:, 4 * half + k, :], ident[:, :])
                    mm.then_inc(yt_mm, 1)

        @block.scalar
        def _(act):
            def square_sum(src, col, junk):
                if col >= 1:
                    act.wait_ge(ssq_done, col)
                act.activation(junk, src, ACT.Square, accum_out=ssq[:, col:col + 1]).then_inc(ssq_done, 1)

            def take_root(n, c0, count):
                act.wait_ge(msq_done, n)
                act.activation(root[:, c0:c0 + count], msq[:, c0:c0 + count], ACT.Sqrt).then_inc(root_done, 1)

            def filter_sine(n):
                act.wait_ge(mlp_pre, n + 1)
                act.activation(hid, mlp_y, ACT.Sin).then_inc(mlp_sin, 1)

            filter_sine(0)
            for i in range(TILES):
                act.wait_ge(x_in[i], 16)
                square_sum(x[:, i, :], N_X + i, junk1)
            take_root(1, N_X, TILES)
            for i in range(TILES):
                act.wait_ge(h_turned, 2 * i + 1)
                act.copy(hT[:, 0:4, i * P:(i + 1) * P], cols(2 * (i % 2), 4, P)).then_inc(h_act, 1)
            filter_sine(1)

            for r in range(8):
                if r == 4:
                    filter_sine(2)
                act.wait_ge(qk_mm, r + 1)
                dst = (qT, kT)[r // 4][:, r % 4, L_PROMPT:TOKENS]
                act.activation(dst, bank[2 * (r % 2)][:, 0:L_SAMPLE], ACT.Copy,
                               scale=(-(DH ** -0.5) if r < 4 else 1.0)).then_inc(qk_act, 1)
            for i in range(0, TILES, 2):
                act.wait_ge(v_mm, i + 1)
                act.copy(vrow[:, i, :], bank[4][:, :]).then_inc(v_act, 1)

            for u in range(UNITS):
                _, n_keys, _ = attn_cols(u // HEADS)
                act.wait_ge(biased, u + 1)
                if u >= 2:
                    act.wait_ge(pt_mm, u - 1)
                act.activation(p_sb[u % 2][:, 0:n_keys], s_sb[u % 2][:, 0:n_keys], ACT.Exp,
                               bias=negmax[:, u:u + 1], scale=-1.0,
                               accum_out=den[:, u:u + 1]).then_inc(exp_done, 1)

            def rows_of_u(r):
                act.wait_ge(u_turned, 2 * r + 1)
                part, m = divmod(r, 4)
                dst = uv if part == 0 else x12[:, part - 1]
                act.copy(dst[:, 0:3, m * P:(m + 1) * P], cols(4 + 2 * (r % 2), 4, P)[:, 0:3, :]).then_inc(ut_act, 1)

            act.wait_ge(pads, 1)
            act.wait_ge(consts_in, 96)
            for r in range(NU):
                act.wait_ge(u_mm, r + 1)
                if r >= 2:
                    act.wait_ge(conv_done, r - 1)
                act.copy(uraw[r % 2][:, L_PROMPT + 3:TOKENS + 3], bank[2 * (r % 2)][:, 0:L_SAMPLE]).then_inc(u_act, 1)
                if r >= 1:
                    rows_of_u(r - 1)
                act.wait_ge(u_act, r + 1)
                act.wait_ge(u_dve, r + 1)
                if r >= 2:
                    act.wait_ge(u_turned, 2 * (r - 1))
                act.activation(uc[r % 2], uraw[r % 2][:, 1:TOKENS + 3], ACT.Identity,
                               bias=convw[:, 3, r:r + 1], scale=convw[:, 1, r:r + 1]).then_inc(conv_mid, 1)
            rows_of_u(NU - 1)

            for q in range(len(HY)):
                n, base = HY_N[q], HY_BASE[q]
                act.wait_ge(conv_done, NU)
                act.wait_ge(u_turned, 2 * NU)
                if q >= 1:
                    act.wait_ge(y_done, base)
                for f in range(n):
                    for part in range(2):
                        act.wait_ge(kf_mm, 2 * (base + f) + part + 1)
                        act.copy(kf[:, part, f, :], bank[4 + 2 * (f % 2) + part][:, :]).then_inc(kf_done, 1)

            act.wait_ge(z_done, HY_BASE[4])
            act.wait_ge(attn_row, TILES)
            for i in range(TILES):
                square_sum(attn[:, i, :], N_MIX + 2 * i, bank[7][:, :])
                square_sum(uv[:, i, :], N_MIX + 2 * i + 1, bank[7][:, :])
            take_root(2, N_MIX, 2 * TILES)

            def mix_columns(i):
                act.wait_ge(mix_turned, 2 * i + 1)
                act.copy(hT[:, 0:4, i * P:(i + 1) * P], cols(0, 4, P)).then_inc(mix_act, 1)

            def xn_columns(i):
                act.wait_ge(xn_turned, 2 * i + 1)
                act.copy(hT[:, 0:4, i * P:(i + 1) * P], cols(2, 4, P)).then_inc(xn_act, 1)

            mix_columns(0)
            for i in range(TILES):
                if i + 1 < TILES:
                    mix_columns(i + 1)
                act.wait_ge(res_done, 2 * (i + 1))
                act.wait_ge(mix_turned, 2 * i + 2)
                square_sum(x[:, i, :], N_FFN + i, attn[:, i, :].bitcast(BF16))
                take_root(3 + i, N_FFN + i, 1)
                if i >= 1:
                    xn_columns(i - 1)
            xn_columns(TILES - 1)
            act.wait_ge(logit_off, 1)
            act.activation(aff, aff, ACT.Exp).then_inc(logit_exp, 1)

            def copy_xe(n):
                act.wait_ge(xe_mm, n)
                act.copy(xeT[:, 0:4, :], cols(6, 4, SLOTS)).then_inc(xe_done, 1)

            copy_xe(1)
            with act.Fori(0, EXPERTS) as e:
                for j in range(FT):
                    act.wait_ge(gate_mm, e * FT + (j + 1))
                    act.wait_ge(h_done, e * FT + (j + 1))
                    act.activation(silu[j % 2], bank[j % 2][:, 0:SLOTS], ACT.Silu).then_inc(silu_done, 1)
                copy_xe(e * 2 + 3)
                act.wait_ge(down_mm, e * FT + (FT + 2))
                act.wait_ge(gate_set, e + 1)
                act.copy(yT[:, 0:4, :], cols(4, 4, SLOTS)).then_inc(yT_done, 1)
                act.wait_ge(yt_mm, e * 2 + 1)
                act.activation(ysc[:, 0:W], bank[6][0:SLOTS, :], ACT.Copy,
                               scale=gate_now).then_inc(ysc_done, 1)

            act.wait_ge(xe_done, 2 * EXPERTS + 2)
            act.wait_ge(xn_out, 32 * TILES)
            for i in range(TILES):
                act.wait_ge(yfin_in[i], 16)
                square_sum(yfin[:, i, :], N_FIN + i, attn[:, i, :].bitcast(BF16))
                take_root(9 + i, N_FIN + i, 1)

        @block.vector
        def _(dve):
            steps = [0]

            def step(ins):
                steps[0] += 1
                ins.then_inc(dve_step, 1)
                dve.wait_ge(dve_step, steps[0])

            def filter_arguments(n):
                dve.wait_ge(mlp_mm, n + 1)
                if n == 0:
                    dve.wait_ge(mlp_in, 16 * 8)
                else:
                    dve.wait_ge(mlp_sin, n)
                for g in range(2):
                    lo, n_pos = FIRST_TILE[g] * P, GROUP_LEN[g]
                    ins = dve.tensor_scalar(mlp_y[:, lo:lo + n_pos], bank[6 + g][0:FILTER_HID, 0:n_pos],
                                            mlp_b[:, n:n + 1], mlp_b[:, 3:4], ALU.add, ALU.mult)
                step(ins)
                step(dve.tensor_scalar(mlp_k, mlp_y, 1.0 / (2.0 * math.pi), ROUND_MAGIC, ALU.mult, ALU.add))
                step(dve.tensor_scalar(mlp_k, mlp_k, ROUND_MAGIC, None, ALU.subtract))
                step(dve.scalar_tensor_tensor(mlp_y, mlp_k, -TWO_PI_HI, mlp_y, ALU.mult, ALU.add))
                step(dve.scalar_tensor_tensor(mlp_y, mlp_k, -TWO_PI_LO, mlp_y, ALU.mult, ALU.add))
                dve.tensor_scalar(mlp_y, mlp_y, PI_IN, -PI_IN, ALU.min, ALU.max).then_inc(mlp_pre, 1)

            def mean_square(c0, count, width, n_sums):
                dve.wait_ge(ssq_done, n_sums)
                dve.tensor_scalar(msq[:, c0:c0 + count], ssq[:, c0:c0 + count], 1.0 / width, EPS,
                                  ALU.mult, ALU.add).then_inc(msq_done, 1)

            def inverse_root(n, c0, count):
                dve.wait_ge(root_done, n)
                step(dve.reciprocal(rinv[:, c0:c0 + count], root[:, c0:c0 + count]))

            def normed(dst, src, col, gain, done):
                dve.scalar_tensor_tensor(dst, src, rinv[:, col:col + 1], gain, ALU.mult, ALU.mult).then_inc(done, 1)

            filter_arguments(0)
            mean_square(N_X, TILES, D, TILES)
            inverse_root(1, N_X, TILES)
            dve.wait_ge(gain_in, 16)

            def h_columns(i):
                dve.wait_ge(h_turned, 2 * i + 2)
                dve.tensor_copy(hT[:, 4:8, i * P:(i + 1) * P], cols(2 * (i % 2) + 1, 4, P)).then_inc(h_dve, 1)

            for i in range(TILES):
                if i >= 2:
                    h_columns(i - 2)
                normed(hrow[i % 2], x[:, i, :], N_X + i, gbc[:, :], h_row)
            h_columns(TILES - 2)
            h_columns(TILES - 1)
            filter_arguments(1)
            for r in range(8):
                if r == 4:
                    filter_arguments(2)
                dve.wait_ge(qk_mm, r + 1)
                dst = (qT, kT)[r // 4][:, r % 4, 0:L_PROMPT]
                dve.tensor_scalar(dst, bank[2 * (r % 2) + 1][:, 0:L_PROMPT],
                                  -(DH ** -0.5) if r < 4 else 1.0, None, ALU.mult).then_inc(qk_dve, 1)
            for i in range(1, TILES, 2):
                dve.wait_ge(v_mm, i + 1)
                dve.tensor_copy(vrow[:, i, :], bank[5][:, :]).then_inc(v_dve, 1)

            def bias_scores(u):
                tile, head = divmod(u, HEADS)
                _, n_keys, c0 = attn_cols(tile)
                dve.wait_ge(score_mm, u + 1)
                if u >= 2:
                    dve.wait_ge(exp_done, u - 1)
                dve.tensor_tensor_reduce(s_sb[u % 2][:, 0:n_keys], bank[u % 2][:, 0:n_keys],
                                         bias[:, head, c0:c0 + n_keys], 1.0, 3e38, ALU.add, ALU.min,
                                         negmax[:, u:u + 1]).then_inc(biased, 1)

            def copy_probs(u):
                _, n_keys, _ = attn_cols(u // HEADS)
                dve.wait_ge(pt_mm, u + 1)
                if u >= 2:
                    dve.wait_ge(pv_mm, u - 1)
                n = n_keys // P
                dve.tensor_copy(pT[u % 2][:, 0:n, :], cols(2 + u % 2, 4, P)[:, 0:n, :]).then_inc(pt_done, 1)

            def attention_row(tile):
                h0 = tile * HEADS
                dve.wait_ge(exp_done, h0 + HEADS)
                step(dve.reciprocal(rden[:, h0:h0 + HEADS], den[:, h0:h0 + HEADS]))
                dve.wait_ge(pv_mm, h0 + HEADS)
                dve.tensor_tensor(attn[:, tile, :].rearrange("p (h c) -> p h c", h=HEADS),
                                  cols(4 + tile % 2, HEADS, DH),
                                  rden[:, h0:h0 + HEADS].unsqueeze(2).to_broadcast([P, HEADS, DH]),
                                  ALU.mult).then_inc(attn_row, 1)

            dve.wait_ge(bias_in, 16)
            dve.wait_ge(mlp_sin, 3)
            for s in range(UNITS + 4):
                if s < UNITS:
                    bias_scores(s)
                if 2 <= s < UNITS + 2:
                    copy_probs(s - 2)
                if s >= 4 and (s - 4) % HEADS == HEADS - 1:
                    attention_row((s - 4) // HEADS)

            for s in range(2):
                ins = dve.memset(uraw[s], 0.0)
            ins.then_inc(pads, 1)
            dve.wait_ge(pads, 1)
            dve.memset(zsel, 0.0).then_inc(pads, 1)
            dve.wait_ge(pads, 2)
            for g in range(2):
                tok0 = FIRST_TILE[g] * P
                dve.tensor_scalar(zsel[0:FILTER_HID, g, 0:1], hid[:, tok0:tok0 + 1], -1.0, None, ALU.mult)
                dve.memset(zsel[FILTER_HID:FILTER_HID + 1, g, 0:1], 1.0)

            def rows_of_u(r):
                dve.wait_ge(u_turned, 2 * r + 2)
                part, m = divmod(r, 4)
                dst = uv if part == 0 else x12[:, part - 1]
                dve.tensor_copy(dst[:, 3:6, m * P:(m + 1) * P],
                                cols(5 + 2 * (r % 2), 4, P)[:, 0:3, :]).then_inc(ut_dve, 1)

            for r in range(NU):
                dve.wait_ge(u_mm, r + 1)
                dve.tensor_copy(uraw[r % 2][:, 1:L_PROMPT + 1],
                                bank[2 * (r % 2) + 1][:, 0:L_PROMPT]).then_inc(u_dve, 1)
                if r >= 1:
                    rows_of_u(r - 1)
                dve.wait_ge(conv_mid, r + 1)
                step(dve.scalar_tensor_tensor(uc[r % 2], uraw[r % 2][:, 0:TOKENS + 2], convw[:, 0, r:r + 1],
                                              uc[r % 2], ALU.mult, ALU.add))
                dve.scalar_tensor_tensor(uc[r % 2], uraw[r % 2][:, 2:TOKENS + 4], convw[:, 2, r:r + 1],
                                         uc[r % 2], ALU.mult, ALU.add).then_inc(conv_done, 1)
            dve.wait_ge(w4_in, 48)
            step(dve.tensor_tensor(w4[:, 1], w4[:, 0], w4b_skip[0:FILTER_HID], ALU.subtract))
            dve.tensor_tensor(w4[:, 0], w4[:, 0], w4b_skip[0:FILTER_HID], ALU.add).then_inc(w4_done, 1)
            rows_of_u(NU - 1)

            dve.wait_ge(hy_in, 16 * 9)
            for q, (g, o) in enumerate(HY):
                n, base = HY_N[q], HY_BASE[q]
                tile0 = FIRST_TILE[g]
                if q >= 1:
                    dve.wait_ge(inv_mm, base)
                for i in range(n):
                    for part in range(2):
                        dve.wait_ge(ab_mm, 2 * (base + i) + part + 1)
                        dve.tensor_tensor(ab[:, part, i, :], bank[2 * (i % 2) + part][:, :],
                                          decay[:, tile0 + i, :], ALU.mult).then_inc(ab_done, 1)
                dve.wait_ge(kf_done, 2 * (base + n))
                for f in range(n):
                    dve.wait_ge(uf_mm, 2 * (base + f + 1))
                    u_cos, u_sin = bank[2 * (f % 2)][:, :], bank[2 * (f % 2) + 1][:, :]
                    dve.tensor_tensor(ab[:, 0, f, :], u_cos, kf[:, 0, f, :], ALU.mult)
                    step(dve.tensor_tensor(prod[0], u_sin, kf[:, 1, f, :], ALU.mult))
                    dve.tensor_tensor(ab[:, 0, f, :], ab[:, 0, f, :], prod[0], ALU.subtract)
                    dve.tensor_tensor(ab[:, 1, f, :], u_cos, kf[:, 1, f, :], ALU.mult)
                    step(dve.tensor_tensor(prod[1], u_sin, kf[:, 0, f, :], ALU.mult))
                    dve.tensor_tensor(ab[:, 1, f, :], ab[:, 1, f, :], prod[1], ALU.add).then_inc(y_done, 1)
                for i in range(n):
                    dve.wait_ge(inv_mm, base + i + 1)
                    dve.tensor_tensor(uv[:, tile0 + i, :], bank[4 + i][:, :], x12[:, o, tile0 + i, :],
                                      ALU.mult).then_inc(z_done, 1)

            mean_square(N_MIX, 2 * TILES, W, N_FFN)
            inverse_root(2, N_MIX, 2 * TILES)
            dve.wait_ge(gain_in, 48)

            def mix_rows(i):
                normed(attn[:, i, :], attn[:, i, :], N_MIX + 2 * i, gbc[:, 0:W], mix_row)
                normed(uv[:, i, :], uv[:, i, :], N_MIX + 2 * i + 1, gbc[:, W:D], mix_row)

            def mix_columns(i):
                dve.wait_ge(mix_turned, 2 * i + 2)
                dve.tensor_copy(hT[:, 4:8, i * P:(i + 1) * P], cols(1, 4, P)).then_inc(mix_dve, 1)

            def xn_columns(i):
                dve.wait_ge(xn_turned, 2 * i + 2)
                dve.tensor_copy(hT[:, 4:8, i * P:(i + 1) * P], cols(3, 4, P)).then_inc(xn_dve, 1)

            for i in range(TILES):
                mix_rows(i)
            mix_columns(0)
            for i in range(TILES):
                if i + 1 < TILES:
                    mix_columns(i + 1)
                for half in range(2):
                    dve.wait_ge(out_mm, 2 * i + half + 1)
                    dve.tensor_tensor(x[:, i, half * W:(half + 1) * W], x[:, i, half * W:(half + 1) * W],
                                      bank[4 + half][:, :], ALU.add).then_inc(res_done, 1)
                if i >= 1:
                    xn_columns(i - 1)
                mean_square(N_FFN + i, 1, D, N_FFN + i + 1)
                inverse_root(3 + i, N_FFN + i, 1)
                if i == 0:
                    dve.wait_ge(gain_in, 64)
                dve.wait_ge(mix_turned, 2 * i + 2)
                normed(attn[:, i, :], x[:, i, 0:W], N_FFN + i, gbc[:, 0:W], xn_row)
                normed(uv[:, i, :], x[:, i, W:D], N_FFN + i, gbc[:, W:D], xn_row)
            xn_columns(TILES - 1)

            dve.wait_ge(logit_mm, TILES)
            dve.wait_ge(y_init, 16 * TILES)
            logit = cols(6, TILES, EXPERTS)
            step(dve.tensor_reduce(lmax, logit, AX.X, ALU.max))
            dve.tensor_tensor(aff, logit, lmax.unsqueeze(2).to_broadcast([P, TILES, EXPERTS]),
                              ALU.subtract).then_inc(logit_off, 1)
            dve.wait_ge(logit_exp, 1)
            step(dve.tensor_reduce(lsum, aff, AX.X, ALU.add))
            step(dve.reciprocal(lmax, lsum))
            dve.tensor_tensor(aff, aff, lmax.unsqueeze(2).to_broadcast([P, TILES, EXPERTS]),
                              ALU.mult).then_inc(aff_done, 1)
            dve.wait_ge(affT_mm, 1)
            dve.tensor_copy(affT[:, 0:L_SAMPLE], bank[0][0:EXPERTS, 0:L_SAMPLE])
            step(dve.tensor_copy(affT[:, L_SAMPLE:TOKENS], bank[1][0:EXPERTS, 0:L_PROMPT]))
            for lo, hi, slot0, cap in ((0, L_SAMPLE, 0, CAP_SAMPLE), (L_SAMPLE, TOKENS, CAP_SAMPLE, CAP_PROMPT)):
                for n in range(slot0, slot0 + cap, 8):
                    step(dve.max(vals[:, n:n + 8], affT[:, lo:hi]))
                    step(dve.max_index(idxu[:, n:n + 8], vals[:, n:n + 8], affT[:, lo:hi]))
                    if n + 8 < slot0 + cap:
                        step(dve.match_replace(affT[:, lo:hi], vals[:, n:n + 8], affT[:, lo:hi], -1.0))
            dve.tensor_copy(idxf[:, CAP_SAMPLE:SLOTS], idxu[:, CAP_SAMPLE:SLOTS])
            dve.tensor_scalar(idxf[:, 0:CAP_SAMPLE], idxu[:, 0:CAP_SAMPLE], float(L_PROMPT), None,
                              ALU.add).then_inc(chosen, 1)
            dve.wait_ge(chosen_mm, 1)
            dve.tensor_copy(idxT[:, 0:EXPERTS], bank[2][0:SLOTS, 0:EXPERTS])
            dve.tensor_copy(idxT[:, EXPERTS:EXPERTS + 1], bank[2][0:SLOTS, EXPERTS - 1:EXPERTS])
            dve.tensor_copy(gateT, bank[3][0:SLOTS, 0:EXPERTS]).then_inc(chosen_done, 1)

            def copy_xe(n):
                dve.wait_ge(xe_mm, n)
                dve.tensor_copy(xeT[:, 4:8, :], cols(7, 4, SLOTS)).then_inc(xe_done, 1)

            dve.sem_inc(h_done, 2)
            copy_xe(2)
            with dve.Fori(0, EXPERTS) as e:
                for j in range(FT):
                    dve.wait_ge(up_mm, e * FT + (j + 1))
                    dve.wait_ge(silu_done, e * FT + (j + 1))
                    dve.wait_ge(down_mm, e * FT + (j + 1))
                    dve.tensor_tensor(hbuf[j % 2], bank[2 + j % 2][:, 0:SLOTS], silu[j % 2],
                                      ALU.mult).then_inc(h_done, 1)
                copy_xe(e * 2 + 4)
                dve.wait_ge(down_mm, e * FT + (FT + 2))
                dve.wait_ge(gate_set, e + 1)
                dve.tensor_copy(yT[:, 4:8, :], cols(5, 4, SLOTS)).then_inc(yT_done, 1)
                dve.wait_ge(yt_mm, e * 2 + 2)
                dve.tensor_scalar(ysc[:, W:D], bank[7][0:SLOTS, :], gate_now, None, ALU.mult).then_inc(ysc_done, 1)

            dve.wait_ge(gain_in, 80)
            for i in range(TILES):
                mean_square(N_FIN + i, 1, D, N_FIN + i + 1)
                inverse_root(9 + i, N_FIN + i, 1)
                normed(yfin[:, i, :], yfin[:, i, :], N_FIN + i, gbc[:, :], fin_row)

        @block.gpsimd
        def _(pool):
            last_row = pool.to_reg(TOKENS - 1)

            def gather(index_set, count):
                pool.wait_ge(xn_out, 32 * TILES)
                pool.wait_ge(index_set, count)
                pool.indirect_dma_start(xg, None, xn_dram, bass.IndirectOffsetOnAxis(ap=idx_gather, axis=0),
                                        bounds_check=last_row).then_inc(gathered, 16)

            pool.wait_ge(chosen_done, 1)
            pool.tensor_copy(idx_gather, idxT[:, 0:1]).then_inc(first_index, 1)
            gather(first_index, 1)
            with pool.Fori(0, EXPERTS) as e:
                pool.tensor_copy(gate_now, gateT[:, bass.ds(e, 1)]).then_inc(gate_set, 1)
                pool.tensor_copy(idx_scatter, idxT[:, bass.ds(e, 1)]).then_inc(pool_step, 1)
                pool.wait_ge(gathered, e * 16 + 16)
                pool.wait_ge(xe_mm, e * 2 + 2)
                pool.tensor_copy(idx_gather, idxT[:, bass.ds(e + 1, 1)]).then_inc(pool_step, 1)
                gather(pool_step, e * 2 + 2)
                pool.wait_ge(y_init, 16 * TILES)
                pool.wait_ge(ysc_done, e * 2 + 2)
                pool.indirect_dma_start(y_dram, bass.IndirectOffsetOnAxis(ap=idx_scatter, axis=0), ysc, None,
                                        bounds_check=last_row, compute_op=ALU.add).then_inc(scattered, 16)
                pool.wait_ge(scattered, e * 16 + 16)
            pool.wait_ge(gathered, 16 * (EXPERTS + 1))


def shape_tables():
    f32 = np.float32
    tables = {"ident": np.eye(P, dtype=f32)}
    dist = np.abs(np.arange(P)[:, None] - (np.arange(BIAS_W)[None, :] - BIAS_OFF))
    count = np.zeros(dist.shape)
    for window, dil in PATTERNS:
        count += (dist % dil == 0) & (dist // dil <= window // (2 * dil))
    slopes = 2.0 ** (-8.0 * (np.arange(HEADS) + 1) / HEADS)
    ln = np.log(np.maximum(count, 1))
    table = np.where(count[:, None] > 0, slopes[None, :, None] * dist[:, None] - ln[:, None], -NEG)
    tables["attn_bias"] = table.reshape(P, HEADS * BIAS_W).astype(f32)
    feats, decays = [], []
    bands = np.linspace(1e-4, (FILTER_EMB - 1) // 2 - 1, (FILTER_EMB - 1) // 2, dtype=f32)[None]
    deltas = np.linspace(math.log(1e-2) / 0.3, math.log(1e-2) / 1.5, W, dtype=f32)
    for length in GROUP_LEN:
        pos = np.linspace(0.0, 1.0, length, dtype=f32)[:, None]
        wpos = f32(2.0 * math.pi) * np.arange(length, dtype=f32)[:, None] / f32(length)
        feats.append(np.concatenate([pos, np.cos(bands * wpos), -np.sin(bands * wpos)], axis=1))
        decays.append(np.exp(-pos * np.abs(deltas)))
    tables["features"] = np.ascontiguousarray(np.concatenate(feats).T.astype(f32))
    tables["decay"] = np.concatenate(decays).astype(f32)
    for name, length in zip(("dft_prompt", "dft_sample"), GROUP_LEN):
        f, n = np.arange(length) + 0.5, np.arange(length)
        half = np.pi * np.outer(n + 0.5, f) / length
        lag = np.pi * np.outer(n, f) / length
        tables[name] = np.stack([np.cos(half), np.sin(half), np.cos(lag) / length,
                                 np.sin(lag) / length]).astype(f32)
    return tables


_INS = ['x_prompt', 'x_sample', 'norm_mix_g', 'w_in', 'short_w', 'short_b', 'filt_w1', 'filt_b1', 'filt_w2',
        'filt_b2', 'filt_w3', 'filt_b3', 'filt_w4', 'filt_freq', 'hyena_skip', 'attn_out_g', 'hyena_out_g',
        'w_out', 'norm_ffn_g', 'w_router', 'w_gate', 'w_up', 'w_down', 'final_g']


def kernel(**inputs):
    import concourse.bacc as _bacc
    from concourse.bass_utils import run_bass_kernel_spmd as _run

    nc = _bacc.Bacc("TRN2", target_bir_lowering=False, num_devices=1)
    arrays, aps = {}, {}
    for name, a in [(n, np.ascontiguousarray(inputs[n])) for n in _INS] + list(shape_tables().items()):
        arrays[f"in_{name}"] = a
        aps[name] = nc.dram_tensor(f"in_{name}", a.shape, mybir.dt.from_np(a.dtype), kind="ExternalInput").ap()
    outs = [nc.dram_tensor(f"out_{n}", (1, length, D), F32, kind="ExternalOutput").ap()
            for n, length in zip(("prompt", "sample"), GROUP_LEN)]
    encoder(nc, aps, *outs)
    r = _run(nc, [arrays], core_ids=[0])
    return r.results[0]["out_prompt"], r.results[0]["out_sample"]
```

```python
import math
from contextlib import ExitStack

import numpy as np

import concourse.bass as bass
from concourse import mybir

F32 = mybir.dt.float32
F32R = mybir.dt.float32r
BF16 = mybir.dt.bfloat16
U32 = mybir.dt.uint32
ALU = mybir.AluOpType
ACT = mybir.ActivationFunctionType
AX = mybir.AxisListType

P = 128
D = 1024
KD = D // P
W = 512
HEADS, DH = 8, 64
L_PROMPT, L_SAMPLE = 256, 512
TOKENS = L_PROMPT + L_SAMPLE
TILES = TOKENS // P
FIRST_TILE = (0, L_PROMPT // P)
GROUP_LEN = (L_PROMPT, L_SAMPLE)
PATTERNS = ((128, 1), (512, 4), (2048, 16))
NEG = -1e30
EPS = 1e-6
FILTER_EMB, FILTER_HID, ORDER = 33, 64, 2
EXPERTS, FF = 16, 2816
CAP_SAMPLE, CAP_PROMPT = 2 * L_SAMPLE // EXPERTS, 2 * L_PROMPT // EXPERTS
SLOTS = CAP_SAMPLE + CAP_PROMPT
BIAS_OFF = L_SAMPLE - P
BIAS_W = L_SAMPLE + BIAS_OFF
CHUNK = 2
CW = CHUNK * P
CHUNKS = FF // CW
UNITS_PER_EXPERT = 3 * CHUNKS
UNIT_W = D * CW // P
RAW_RING, SPLIT_RING = 11, 3
ALL_UNITS = EXPERTS * UNITS_PER_EXPERT
SBUF_BASE = 16512
ROUND_MAGIC = 1.5 * 2.0 ** 23
TWO_PI_HI = 6.28125
TWO_PI_LO = 2.0 * math.pi - TWO_PI_HI
PI_IN = 3.1415925

KB = 256


def unit_at(n):
    if n < 2:
        return "gu"[n], 0, 0
    m, kind = divmod(n - 2, 3)
    if kind == 2 or n == ALL_UNITS - 1:
        return "d", m % CHUNKS, m // CHUNKS
    return "gu"[kind], (m + 1) % CHUNKS, (m + 1) // CHUNKS


def group_of(tile):
    return 0 if tile < FIRST_TILE[1] else 1


def encoder(nc, t, out_prompt, out_sample):
    xn_dram = nc.dram_tensor("xn_rows", [TOKENS, D], F32).ap()
    y_dram = nc.dram_tensor("y_rows", [TOKENS, D], F32).ap()

    with ExitStack() as ctx:
        def sem(name):
            return ctx.enter_context(nc.semaphore(name))

        def region(name, kb, size_kb, dt=F32):
            return nc.alloc_sbuf_tensor_at(name, [P, int(size_kb * KB)], dt, offset=SBUF_BASE + int(kb * 1024))

        xreg = region("xreg", 0, 24)
        hreg = region("hreg", 24, 24)
        areg = region("areg", 48, 12)
        vreg = region("vreg", 60, 12)
        wreg = region("wreg", 72, 32)
        breg = region("breg", 104, 96)
        split = region("split_ring", 48, 48, F32R)
        xe_split = region("xe_split", 8, 6, F32R)
        ht_split = region("ht_split", 14, 1.5, F32R)
        at = [200 * 1024]

        def sb(name, shape):
            size = 4 * int(np.prod(shape[1:]))
            tensor = nc.alloc_sbuf_tensor_at(name, shape, F32, offset=SBUF_BASE + at[0])
            at[0] += -(-size // 32) * 32
            return tensor

        ident = sb("ident", [P, P])
        gbc = sb("gbc", [P, D])
        ssq = sb("ssq", [P, 30])
        msq = sb("msq", [P, 30])
        root = sb("root", [P, 30])
        rinv = sb("rinv", [P, 30])
        negmax = sb("negmax", [P, TILES * HEADS])
        den = sb("den", [P, TILES * HEADS])
        rden = sb("rden", [P, TILES * HEADS])
        wrt = sb("wrt", [P, KD, EXPERTS])
        convw = sb("convw", [P, 4, 12])

        def view(reg, kb, shape, parts=P, dt=None):
            n = int(np.prod(shape))
            start = int(kb * KB)
            v = reg[0:parts, start:start + n]
            names = "abcd"[:len(shape)]
            if len(shape) == 1:
                return v
            return v.rearrange("p (" + " ".join(names) + ") -> p " + " ".join(names),
                               **{c: s for c, s in zip(names[:-1], shape[:-1])})

        x = view(xreg, 0, (TILES, D))
        hT = view(hreg, 0, (KD, TOKENS))
        wbuf = [view(wreg, 16 * s, (KD, W)) for s in range(2)]
        attn = view(areg, 0, (TILES, W))
        hrow = [view(areg, 4 * s, (D,)) for s in range(2)]
        uv = view(vreg, 0, (TILES, W))
        qT = view(breg, 0, (4, TOKENS))
        kT = view(breg, 12, (4, TOKENS))
        vrow = view(breg, 24, (TILES, W))
        bias = view(breg, 36, (HEADS, BIAS_W))
        s_sb = [view(breg, 64 + 2 * s, (W,)) for s in range(2)]
        p_sb = [view(breg, 68 + 2 * s, (W,)) for s in range(2)]
        pT = [view(breg, 72 + 2 * s, (4, P)) for s in range(2)]
        feats = view(breg, 64, (TOKENS,), FILTER_EMB)
        mlp_y = view(breg, 67, (TOKENS,), FILTER_HID)
        mlp_k = view(breg, 70, (TOKENS,), FILTER_HID)
        mlp_w = view(breg, 73, (3, FILTER_HID), FILTER_HID)
        mlp_b = view(breg, 74, (4,), FILTER_HID)
        junk1 = view(breg, 76, (D,))
        hid = view(breg, 92, (TOKENS,), FILTER_HID)
        x12 = view(breg, 0, (2, TILES, W))
        dft = [view(breg, 24, (4, 2, L_PROMPT)), view(breg, 32, (4, 4, L_SAMPLE))]
        decay = view(breg, 64, (TILES, W))
        kf = view(breg, 76, (2, 4, W))
        uraw = [view(breg, 76 + 4 * s, (TOKENS + 4,)) for s in range(2)]
        uc = [view(breg, 84 + 4 * s, (TOKENS + 2,)) for s in range(2)]
        zsel = view(breg, 95, (2, P))
        ab = view(hreg, 0, (2, 4, W))
        prod = [view(hreg, 16 + 2 * s, (W,)) for s in range(2)]
        w4 = view(wreg, 0, (2, ORDER, W), FILTER_HID)
        w4b_skip = view(gbc, 0, (ORDER, W), FILTER_HID + 1)
        raw = [breg[:, s * UNIT_W:(s + 1) * UNIT_W] for s in range(RAW_RING)]
        sp_unit = [[split[:, (2 * s + part) * UNIT_W:(2 * s + part + 1) * UNIT_W] for part in range(2)]
                   for s in range(SPLIT_RING)]

        def by_rows(unit, kind):
            return unit.rearrange("p (k c) -> p k c", c=(D if kind == "d" else CW))

        xg = view(xreg, 0, (D,), SLOTS)
        ysc = view(xreg, 4, (D,), SLOTS)
        xeT = [xe_split[:, part * KD * SLOTS:(part + 1) * KD * SLOTS].rearrange("p (k s) -> p k s", k=KD)
               for part in range(2)]
        hsT = [ht_split[:, part * CHUNK * SLOTS:(part + 1) * CHUNK * SLOTS].rearrange("p (j s) -> p j s", j=CHUNK)
               for part in range(2)]
        h_now = view(xreg, 16, (CW,), SLOTS)
        silu = view(xreg, 17, (CW,), SLOTS)
        affT = view(xreg, 16, (TOKENS,), EXPERTS)
        lmax = view(xreg, 19, (TILES,))
        lsum = view(xreg, 19.125, (TILES,))
        aff = view(xreg, 19.5, (TILES, EXPERTS))
        vals = view(xreg, 20, (SLOTS,), EXPERTS)
        idxf = view(xreg, 20.5, (SLOTS,), EXPERTS)
        idxu = view(xreg, 21, (SLOTS,), EXPERTS).bitcast(U32)
        idxT = view(xreg, 21.5, (EXPERTS + 1,), SLOTS).bitcast(U32)
        gateT = view(xreg, 22, (EXPERTS,), SLOTS)
        idx_gather = view(xreg, 22.25, (1,), SLOTS).bitcast(U32)
        idx_scatter = view(xreg, 22.5, (1,), SLOTS).bitcast(U32)
        gate_now = view(xreg, 22.75, (1,), SLOTS)
        yfin = view(hreg, 0, (TILES, D))

        bank = [ctx.enter_context(nc.psum_tensor(f"bank{i}", [P, 512], F32)) for i in range(8)]

        def cols(b, n, w, parts=P):
            return bank[b][0:parts, 0:n * w].rearrange("p (n w) -> p n w", n=n)

        x_in = [sem(f"x_in{i}") for i in range(TILES)]
        consts_in, mlp_in, bias_in, gain_in = (sem(n) for n in ("consts_in", "mlp_in", "bias_in", "gain_in"))
        w_in_sem = [sem(f"wbuf_in{s}") for s in range(2)]
        hy_in, w4_in = sem("hyena_tables_in"), sem("w4_in")
        act_step, dve_step = sem("act_step"), sem("dve_step")
        ssq_done, msq_done, root_done = sem("ssq_done"), sem("msq_done"), sem("root_done")
        mlp_mm, mlp_pre, mlp_sin = sem("mlp_mm"), sem("mlp_pre"), sem("mlp_sin")
        h_row, h_turned, h_act, h_dve = (sem(n) for n in ("h_row", "h_turned", "h_evac_act", "h_evac_dve"))
        qk_mm, qk_act, qk_dve = sem("qk_mm"), sem("qk_evac_act"), sem("qk_evac_dve")
        v_mm, v_act, v_dve = sem("v_mm"), sem("v_evac_act"), sem("v_evac_dve")
        score_mm, biased, exp_done = sem("score_mm"), sem("biased"), sem("exp_done")
        pt_mm, pt_done, pv_mm, attn_row = sem("pt_mm"), sem("pt_done"), sem("pv_mm"), sem("attn_row")
        u_mm, u_act, u_dve, pads = sem("u_mm"), sem("u_raw_act"), sem("u_raw_dve"), sem("pads")
        conv_mid, conv_done, u_turned = sem("conv_mid"), sem("conv_done"), sem("u_turned")
        ut_act, ut_dve = sem("u_row_act"), sem("u_row_dve")
        w4_done = sem("w4_done")
        ab_mm, ab_done, kf_mm, kf_done = sem("ab_mm"), sem("ab_done"), sem("kf_mm"), sem("kf_done")
        uf_mm, y_done, inv_mm, z_done = sem("uf_mm"), sem("y_done"), sem("inv_mm"), sem("z_done")
        mix_row, mix_turned, mix_act, mix_dve = (sem(n) for n in ("mix_row", "mix_turned", "mix_evac_act", "mix_evac_dve"))
        out_mm, res_done, y_init = sem("out_mm"), sem("residual_done"), sem("y_init")
        xn_row, xn_turned, xn_act, xn_dve, xn_out = (sem(n) for n in ("xn_row", "xn_turned", "xn_evac_act", "xn_evac_dve", "xn_out"))
        logit_mm, logit_off, logit_exp, aff_done = (sem(n) for n in ("logit_mm", "logit_off", "logit_exp", "aff_done"))
        affT_mm, chosen, chosen_mm, chosen_done = (sem(n) for n in ("affT_mm", "chosen", "chosen_mm", "chosen_done"))
        raw_in = [sem(f"raw_in{s}") for s in range(RAW_RING)]
        hi_done, lo_done, unit_mm = sem("hi_done"), sem("lo_done"), sem("unit_mm")
        first_index = sem("first_index")
        pool_step, gathered, scattered, gate_set = (sem(n) for n in ("pool_step", "gathered", "scattered", "gate_set"))
        xe_mm, xe_hi, xe_done = sem("xe_mm"), sem("xe_hi"), sem("xe_done")
        silu_done, h_done, h_turned2 = sem("silu_done"), sem("h_done"), sem("expert_h_turned")
        hs_hi, hs_done, ysc_done = sem("hs_hi"), sem("hs_done"), sem("ysc_done")
        yfin_in = [sem(f"yfin_in{i}") for i in range(TILES)]
        fin_row, out_done = sem("fin_row"), sem("out_done")

        N_X, N_MIX, N_FFN, N_FIN = 0, 6, 18, 24
        HY = [(0, 0), (1, 0), (0, 1), (1, 1)]
        HY_N = [GROUP_LEN[g] // P for g, _ in HY]
        HY_BASE = [sum(HY_N[:q]) for q in range(5)]
        UNITS = TILES * HEADS
        NU = 12

        def attn_cols(tile):
            g = group_of(tile)
            tok0 = FIRST_TILE[g] * P
            return tok0, GROUP_LEN[g], BIAS_OFF - (tile - FIRST_TILE[g]) * P

        def uc_col(tile):
            return tile * P if tile < FIRST_TILE[1] else 2 + tile * P

        block = ctx.enter_context(nc.Block())

        @block.sync
        def _(sp):
            sp.dma_start(x[:, 0, :], t["x_prompt"][0, 0:P, :]).then_inc(x_in[0], 16)
            sp.dma_start(ident[:, :], t["ident"]).then_inc(consts_in, 16)
            sp.dma_start(feats, t["features"]).then_inc(mlp_in, 16)
            sp.dma_start(mlp_w[0:FILTER_EMB, 0, :], t["filt_w1"][0]).then_inc(mlp_in, 16)
            sp.dma_start(mlp_w[:, 1, :], t["filt_w2"][0]).then_inc(mlp_in, 16)
            sp.dma_start(mlp_w[:, 2, :], t["filt_w3"][0]).then_inc(mlp_in, 16)
            for n, name in enumerate(("filt_b1", "filt_b2", "filt_b3", "filt_freq")):
                sp.dma_start(mlp_b[:, n:n + 1], t[name].rearrange("o h -> h o")).then_inc(mlp_in, 16)
            for i in range(1, TILES):
                g = group_of(i)
                src = (t["x_prompt"], t["x_sample"])[g][0, (i - FIRST_TILE[g]) * P:(i - FIRST_TILE[g] + 1) * P, :]
                sp.dma_start(x[:, i, :], src).then_inc(x_in[i], 16)
            sp.dma_start(gbc[:, :], t["norm_mix_g"][0].partition_broadcast(P)).then_inc(gain_in, 16)

            w_in = t["w_in"][0].rearrange("(k p) n -> p k n", p=P)
            def load_chunk(n):
                sp.dma_start(wbuf[n % 2], w_in[:, :, n * W:(n + 1) * W]).then_inc(w_in_sem[n % 2], 16)

            load_chunk(0)
            load_chunk(1)
            sp.dma_start(bias, t["attn_bias"].rearrange("p (h c) -> p h c", h=HEADS)).then_inc(bias_in, 16)
            for n in range(3):
                sp.dma_start(convw[:, n, :], t["short_w"][0, n].rearrange("(c p) -> p c", p=P),
                             allow_slow_non_contiguous=True).then_inc(consts_in, 16)
            sp.dma_start(convw[:, 3, :], t["short_b"][0].rearrange("(c p) -> p c", p=P),
                         allow_slow_non_contiguous=True).then_inc(consts_in, 16)
            sp.dma_start(wrt[:, :, :], t["w_router"][0].rearrange("(k p) e -> p k e", p=P)).then_inc(consts_in, 16)
            sp.wait_ge(qk_mm, 4)
            load_chunk(2)
            sp.wait_ge(qk_mm, 8)
            load_chunk(3)
            sp.wait_ge(v_mm, TILES)
            load_chunk(4)
            sp.wait_ge(attn_row, TILES)
            for g in range(2):
                tab = t[("dft_prompt", "dft_sample")[g]].rearrange("m (i p) f -> p m i f", p=P)
                for m in range(4):
                    sp.dma_start(dft[g][:, m], tab[:, m]).then_inc(hy_in, 16)
            sp.dma_start(decay, t["decay"].rearrange("(i p) c -> p i c", p=P)).then_inc(hy_in, 16)
            w4_src = t["filt_w4"][0].rearrange("h (o d c) -> h o d c", o=ORDER, d=2)
            sp.wait_ge(h_row, TILES)
            sp.dma_start(w4b_skip[0:FILTER_HID], w4_src[:, :, 1, :]).then_inc(w4_in, 16)
            sp.dma_start(w4b_skip[FILTER_HID:FILTER_HID + 1], t["hyena_skip"]).then_inc(w4_in, 16)
            sp.wait_ge(u_mm, 4)
            load_chunk(5)
            sp.wait_ge(u_mm, 8)
            sp.dma_start(w4[:, 0], w4_src[:, :, 0, :]).then_inc(w4_in, 16)
            w_out = t["w_out"][0].rearrange("(k p) n -> p k n", p=P)
            sp.wait_ge(u_mm, 12)
            sp.dma_start(wbuf[1], w_out[:, :, 0:W]).then_inc(w_in_sem[1], 16)
            sp.wait_ge(ab_mm, 2 * HY_BASE[4])
            sp.dma_start(wbuf[0], w_out[:, :, W:D]).then_inc(w_in_sem[0], 16)
            sp.dma_start(gbc[:, 0:W], t["attn_out_g"][0].partition_broadcast(P)).then_inc(gain_in, 16)
            sp.dma_start(gbc[:, W:D], t["hyena_out_g"][0].partition_broadcast(P)).then_inc(gain_in, 16)

            w_gate, w_up, w_down = (t[n][0] for n in ("w_gate", "w_up", "w_down"))

            def load_unit(n, kind, c, e):
                if kind == "d":
                    src = w_down[bass.ds(e, 1), c * CW:(c + 1) * CW, :].rearrange("o (j p) d -> p (o j) d", p=P)
                else:
                    w = w_gate if kind == "g" else w_up
                    src = w[bass.ds(e, 1), :, c * CW:(c + 1) * CW].rearrange("o (k p) f -> p (o k) f", p=P)
                slot = n % RAW_RING
                sp.dma_start(by_rows(raw[slot], kind), src).then_inc(raw_in[slot], 16)

            sp.wait_ge(z_done, HY_BASE[4])
            for n in range(RAW_RING):
                load_unit(n, *unit_at(n))
            sp.wait_ge(mix_row, 2 * TILES)
            sp.dma_start(gbc[:, :], t["norm_ffn_g"][0].partition_broadcast(P)).then_inc(gain_in, 16)
            for i in range(TILES):
                sp.wait_ge(res_done, 2 * (i + 1))
                sp.dma_start(y_dram[i * P:(i + 1) * P, :], x[:, i, :]).then_inc(y_init, 16)
                sp.wait_ge(xn_row, 2 * (i + 1))
                sp.dma_start(xn_dram[i * P:(i + 1) * P, 0:W], attn[:, i, :]).then_inc(xn_out, 16)
                sp.dma_start(xn_dram[i * P:(i + 1) * P, W:D], uv[:, i, :]).then_inc(xn_out, 16)
            sp.dma_start(gbc[:, :], t["final_g"].partition_broadcast(P)).then_inc(gain_in, 16)

            with sp.Fori(0, EXPERTS - 1) as e:
                for n in range(RAW_RING, RAW_RING + UNITS_PER_EXPERT):
                    kind, c, ahead = unit_at(n)
                    sp.wait_ge(lo_done, e * UNITS_PER_EXPERT + (n - RAW_RING + 1))
                    load_unit(n, kind, c, e + ahead)
            for n in range(RAW_RING + (EXPERTS - 1) * UNITS_PER_EXPERT, ALL_UNITS):
                sp.wait_ge(lo_done, n - RAW_RING + 1)
                load_unit(n, *unit_at(n))

            sp.wait_ge(scattered, 16 * EXPERTS)
            for i in range(TILES):
                sp.dma_start(yfin[:, i, :], y_dram[i * P:(i + 1) * P, :]).then_inc(yfin_in[i], 16)
            for i in range(TILES):
                g = group_of(i)
                dst = (out_prompt, out_sample)[g][0, (i - FIRST_TILE[g]) * P:(i - FIRST_TILE[g] + 1) * P, :]
                sp.wait_ge(fin_row, i + 1)
                sp.dma_start(dst, yfin[:, i, :]).then_inc(out_done, 16)
            sp.wait_ge(out_done, 16 * TILES)
            sp.wait_ge(y_init, 16 * TILES)
            sp.wait_ge(xn_out, 32 * TILES)

        @block.tensor
        def _(pe):
            def filter_layer(n):
                if n == 0:
                    pe.wait_ge(mlp_in, 16 * 8)
                else:
                    pe.wait_ge(mlp_sin, n)
                for g in range(2):
                    lo, n_pos = FIRST_TILE[g] * P, GROUP_LEN[g]
                    lhsT = mlp_w[0:FILTER_EMB, 0, :] if n == 0 else mlp_w[:, n, :]
                    rhs = (feats if n == 0 else hid)[:, lo:lo + n_pos]
                    mm = pe.matmul(bank[6 + g][0:FILTER_HID, 0:n_pos], lhsT, rhs, start=True, stop=True)
                mm.then_inc(mlp_mm, 1)

            def turn(rows, b, turned):
                for half in range(2):
                    for k in range(4):
                        mm = pe.transpose(cols(b + half, 4, P)[:, k, :], rows[half][:, k * P:(k + 1) * P], ident[:, :])
                    mm.then_inc(turned, 1)

            filter_layer(0)
            pe.wait_ge(consts_in, 96)
            for i in range(TILES):
                pe.wait_ge(h_row, i + 1)
                if i >= 2:
                    pe.wait_ge(h_act, i - 1)
                    pe.wait_ge(h_dve, i - 1)
                turn([hrow[i % 2][:, 0:W], hrow[i % 2][:, W:D]], 2 * (i % 2), h_turned)
            filter_layer(1)

            def project(c, m, r, done, freed):
                for ready, count in freed:
                    pe.wait_ge(ready, count)
                b = 2 * (r % 2)
                for k in range(KD):
                    lhsT = wbuf[c % 2][:, k, m * P:(m + 1) * P]
                    pe.matmul(bank[b][:, 0:L_SAMPLE], lhsT, hT[:, k, L_PROMPT:TOKENS],
                              start=(k == 0), stop=(k == KD - 1))
                    mm = pe.matmul(bank[b + 1][:, 0:L_PROMPT], lhsT, hT[:, k, 0:L_PROMPT],
                                   start=(k == 0), stop=(k == KD - 1))
                mm.then_inc(done, 1)

            pe.wait_ge(h_act, TILES)
            pe.wait_ge(h_dve, TILES)
            for c in range(2):
                pe.wait_ge(w_in_sem[c], 16)
                for m in range(4):
                    r = 4 * c + m
                    project(c, m, r, qk_mm, [(qk_act, r - 1), (qk_dve, r - 1)] if r >= 2 else [])
                if c == 0:
                    filter_layer(2)
            pe.wait_ge(w_in_sem[0], 32)
            for i in range(TILES):
                if i >= 2:
                    pe.wait_ge(v_act if i % 2 == 0 else v_dve, i // 2)
                for k in range(KD):
                    mm = pe.matmul(bank[4 + i % 2][:, :], hT[:, k, i * P:(i + 1) * P], wbuf[0][:, k, :],
                                   start=(k == 0), stop=(k == KD - 1))
                mm.then_inc(v_mm, 1)

            def scores(u):
                tile, head = divmod(u, HEADS)
                tok0, n_keys, _ = attn_cols(tile)
                lo = DH * (head % 2)
                if u >= 2:
                    pe.wait_ge(biased, u - 1)
                pe.matmul(bank[u % 2][:, 0:n_keys], qT[lo:lo + DH, head // 2, tile * P:(tile + 1) * P],
                          kT[lo:lo + DH, head // 2, tok0:tok0 + n_keys], start=True, stop=True).then_inc(score_mm, 1)

            def turn_probs(u):
                _, n_keys, _ = attn_cols(u // HEADS)
                pe.wait_ge(exp_done, u + 1)
                if u >= 2:
                    pe.wait_ge(pt_done, u - 1)
                for j in range(n_keys // P):
                    mm = pe.transpose(cols(2 + u % 2, 4, P)[:, j, :], p_sb[u % 2][:, j * P:(j + 1) * P], ident[:, :])
                mm.then_inc(pt_mm, 1)

            def times_v(u):
                tile, head = divmod(u, HEADS)
                tok0, n_keys, _ = attn_cols(tile)
                pe.wait_ge(pt_done, u + 1)
                if head == 0 and tile >= 2:
                    pe.wait_ge(attn_row, tile - 1)
                for j in range(n_keys // P):
                    mm = pe.matmul(bank[4 + tile % 2][:, head * DH:(head + 1) * DH], pT[u % 2][:, j, :],
                                   vrow[:, tok0 // P + j, head * DH:(head + 1) * DH],
                                   start=(j == 0), stop=(j == n_keys // P - 1))
                mm.then_inc(pv_mm, 1)

            pe.wait_ge(qk_act, 8)
            pe.wait_ge(qk_dve, 8)
            pe.wait_ge(v_act, TILES // 2)
            pe.wait_ge(v_dve, TILES // 2)
            for s in range(UNITS + 3):
                if s < UNITS:
                    scores(s)
                if 2 <= s < UNITS + 2:
                    turn_probs(s - 2)
                if s >= 3:
                    times_v(s - 3)

            def turn_u(r):
                pe.wait_ge(conv_done, r + 1)
                if r >= 2:
                    pe.wait_ge(ut_act, r - 1)
                    pe.wait_ge(ut_dve, r - 1)
                for i in range(TILES):
                    mm = pe.transpose(cols(4 + 2 * (r % 2) + i // 3, 4, P)[:, i % 3, :],
                                      uc[r % 2][:, uc_col(i):uc_col(i) + P], ident[:, :])
                    if i % 3 == 2:
                        mm.then_inc(u_turned, 1)

            pe.wait_ge(biased, UNITS)
            pe.wait_ge(pt_done, UNITS)
            pe.wait_ge(attn_row, TILES)
            for r in range(NU):
                c = 3 + r // 4
                if r % 4 == 0:
                    pe.wait_ge(w_in_sem[c % 2], 16 * (c // 2 + 1))
                project(c, r % 4, r, u_mm, [(u_act, r - 1), (u_dve, r - 1)] if r >= 2 else [])
                if r >= 1:
                    turn_u(r - 1)
            turn_u(NU - 1)

            pe.wait_ge(hy_in, 16 * 9)
            pe.wait_ge(w4_in, 48)
            pe.wait_ge(w4_done, 1)
            pe.wait_ge(u_act, NU)
            pe.wait_ge(u_dve, NU)
            pe.wait_ge(ut_act, NU)
            pe.wait_ge(ut_dve, NU)
            for q, (g, o) in enumerate(HY):
                n, base = HY_N[q], HY_BASE[q]
                tile0 = FIRST_TILE[g]
                cos_half, sin_half, cos_lag, sin_lag = (dft[g][:, m] for m in range(4))
                for i in range(n):
                    if i >= 2:
                        pe.wait_ge(ab_done, 2 * (base + i - 1))
                    b = 2 * (i % 2)
                    h_cols = hid[:, (tile0 + i) * P:(tile0 + i + 1) * P]
                    mm = pe.matmul(bank[b][:, :], h_cols, w4[:, 0, o, :], start=True, stop=(i != 0))
                    if i == 0:
                        mm = pe.matmul(bank[b][:, :], zsel[0:FILTER_HID + 1, g, :], w4b_skip[:, o, :],
                                       start=False, stop=True)
                    mm.then_inc(ab_mm, 1)
                    pe.matmul(bank[b + 1][:, :], h_cols, w4[:, 1, o, :], start=True, stop=True).then_inc(ab_mm, 1)
                if q >= 1:
                    pe.wait_ge(z_done, base)
                for f in range(n):
                    if f >= 2:
                        pe.wait_ge(kf_done, 2 * (base + f - 1))
                    for part, table in enumerate((cos_lag, sin_lag)):
                        for i in range(n):
                            if f == 0:
                                pe.wait_ge(ab_done, 2 * (base + i + 1))
                            mm = pe.matmul(bank[4 + 2 * (f % 2) + part][:, :], table[:, i, f * P:(f + 1) * P],
                                           ab[:, part, i, :], start=(i == 0), stop=(i == n - 1))
                        mm.then_inc(kf_mm, 1)
                for f in range(n):
                    if f >= 2:
                        pe.wait_ge(y_done, base + f - 1)
                    for part, table in enumerate((cos_half, sin_half)):
                        for i in range(n):
                            mm = pe.matmul(bank[2 * (f % 2) + part][:, :], table[:, i, f * P:(f + 1) * P],
                                           uv[:, tile0 + i, :], start=(i == 0), stop=(i == n - 1))
                        mm.then_inc(uf_mm, 1)
                pe.wait_ge(kf_done, 2 * (base + n))
                for i in range(n):
                    for f in range(n):
                        if i == 0:
                            pe.wait_ge(y_done, base + f + 1)
                        pe.matmul(bank[4 + i][:, :], cos_half[:, f, i * P:(i + 1) * P], ab[:, 0, f, :],
                                  start=(f == 0), stop=False)
                        mm = pe.matmul(bank[4 + i][:, :], sin_half[:, f, i * P:(i + 1) * P], ab[:, 1, f, :],
                                       start=False, stop=(f == n - 1))
                    mm.then_inc(inv_mm, 1)

            def turn_mix(i):
                pe.wait_ge(mix_row, 2 * (i + 1))
                if i >= 1:
                    pe.wait_ge(mix_act, i)
                    pe.wait_ge(mix_dve, i)
                turn([attn[:, i, :], uv[:, i, :]], 0, mix_turned)

            def project_out(i):
                pe.wait_ge(mix_act, i + 1)
                pe.wait_ge(mix_dve, i + 1)
                for half in range(2):
                    if i >= 1:
                        pe.wait_ge(res_done, 2 * i - 1 + half)
                    for k in range(KD):
                        mm = pe.matmul(bank[4 + half][:, :], hT[:, k, i * P:(i + 1) * P], wbuf[1 - half][:, k, :],
                                       start=(k == 0), stop=(k == KD - 1))
                    mm.then_inc(out_mm, 1)

            def turn_xn(i):
                pe.wait_ge(xn_row, 2 * (i + 1))
                if i >= 1:
                    pe.wait_ge(xn_act, i)
                    pe.wait_ge(xn_dve, i)
                turn([attn[:, i, :], uv[:, i, :]], 2, xn_turned)

            def logits(i):
                pe.wait_ge(xn_act, i + 1)
                pe.wait_ge(xn_dve, i + 1)
                for k in range(KD):
                    mm = pe.matmul(bank[6][:, i * EXPERTS:(i + 1) * EXPERTS], hT[:, k, i * P:(i + 1) * P],
                                   wrt[:, k, :], start=(k == 0), stop=(k == KD - 1))
                mm.then_inc(logit_mm, 1)

            pe.wait_ge(z_done, HY_BASE[4])
            pe.wait_ge(w_in_sem[1], 64)
            pe.wait_ge(w_in_sem[0], 64)
            turn_mix(0)
            for i in range(TILES):
                if i + 1 < TILES:
                    turn_mix(i + 1)
                project_out(i)
                if i >= 1:
                    turn_xn(i - 1)
                if i >= 2:
                    logits(i - 2)
            logits(TILES - 2)
            turn_xn(TILES - 1)
            logits(TILES - 1)

            pe.wait_ge(aff_done, 1)
            for i in range(TILES):
                b, col = (1, i * P) if i < FIRST_TILE[1] else (0, (i - FIRST_TILE[1]) * P)
                mm = pe.matmul(bank[b][0:EXPERTS, col:col + P], aff[:, i, :], ident[:, :], start=True, stop=True)
            mm.then_inc(affT_mm, 1)
            pe.wait_ge(chosen, 1)
            pe.matmul(bank[2][0:SLOTS, 0:EXPERTS], idxf, ident[0:EXPERTS, 0:EXPERTS], start=True, stop=True)
            pe.matmul(bank[3][0:SLOTS, 0:EXPERTS], vals, ident[0:EXPERTS, 0:EXPERTS],
                      start=True, stop=True).then_inc(chosen_mm, 1)

            def turn_in():
                for half in range(2):
                    for k in range(4):
                        mm = pe.transpose(cols(6 + half, 4, SLOTS)[:, k, :],
                                          xg[:, (4 * half + k) * P:(4 * half + k + 1) * P], ident[0:SLOTS, 0:SLOTS])
                    mm.then_inc(xe_mm, 1)

            def three_passes(out, x_hi, x_lo, w_hi, w_lo, start, stop):
                pe.matmul(out, x_hi, w_hi, start=start, stop=False)
                pe.matmul(out, x_hi, w_lo, start=False, stop=False)
                return pe.matmul(out, x_lo, w_hi, start=False, stop=stop)

            def multiply(n, kind, c, count):
                w_hi, w_lo = (by_rows(sp_unit[n % SPLIT_RING][part], kind) for part in range(2))
                pe.wait_ge(lo_done, count + 1)
                if kind == "d":
                    for j in range(CHUNK):
                        for half in range(2):
                            mm = three_passes(bank[4 + half][0:SLOTS, :], hsT[0][:, j, :], hsT[1][:, j, :],
                                              w_hi[:, j, half * W:(half + 1) * W], w_lo[:, j, half * W:(half + 1) * W],
                                              c == 0 and j == 0, c == CHUNKS - 1 and j == CHUNK - 1)
                else:
                    out = bank["gu".index(kind)][0:SLOTS, 0:CW]
                    for k in range(KD):
                        mm = three_passes(out, xeT[0][:, k, :], xeT[1][:, k, :], w_hi[:, k, :], w_lo[:, k, :],
                                          k == 0, k == KD - 1)
                mm.then_inc(unit_mm, 1)

            def turn_hidden(done):
                pe.wait_ge(h_done, done + 1)
                for j in range(CHUNK):
                    mm = pe.transpose(cols(2, CHUNK, SLOTS)[:, j, :], h_now[:, j * P:(j + 1) * P],
                                      ident[0:SLOTS, 0:SLOTS])
                mm.then_inc(h_turned2, 1)

            def expert(e, last=False):
                for c in range(CHUNKS):
                    m, n = e * CHUNKS + (c + 1), 2 + 3 * c
                    count = e * UNITS_PER_EXPERT
                    more = not (last and c == CHUNKS - 1)
                    if more:
                        if c == CHUNKS - 1:
                            pe.wait_ge(xe_done, e + 2)
                        pe.wait_ge(silu_done, m)
                        multiply(n, "g", (c + 1) % CHUNKS, count + n)
                        pe.wait_ge(h_done, m)
                        multiply(n + 1, "u", (c + 1) % CHUNKS, count + (n + 1))
                    if c == CHUNKS - 2 and not last:
                        pe.wait_ge(gathered, e * 16 + 32)
                        pe.wait_ge(xe_done, e + 1)
                        turn_in()
                    if c == 0:
                        pe.wait_ge(gate_set, e + 1)
                    pe.wait_ge(hs_done, m)
                    d = n + 2 if more else n
                    multiply(d, "d", c, count + d)
                    if more:
                        turn_hidden(m)

            pe.wait_ge(gathered, 16)
            turn_in()
            pe.wait_ge(xe_done, 1)
            multiply(0, "g", 0, 0)
            multiply(1, "u", 0, 1)
            turn_hidden(0)
            with pe.Fori(0, EXPERTS - 1) as e:
                expert(e)
            expert(EXPERTS - 1, last=True)

        @block.scalar
        def _(act):
            def square_sum(src, col, junk):
                if col >= 1:
                    act.wait_ge(ssq_done, col)
                act.activation(junk, src, ACT.Square, accum_out=ssq[:, col:col + 1]).then_inc(ssq_done, 1)

            def take_root(n, c0, count):
                act.wait_ge(msq_done, n)
                act.activation(root[:, c0:c0 + count], msq[:, c0:c0 + count], ACT.Sqrt).then_inc(root_done, 1)

            def filter_sine(n):
                act.wait_ge(mlp_pre, n + 1)
                act.activation(hid, mlp_y, ACT.Sin).then_inc(mlp_sin, 1)

            filter_sine(0)
            for i in range(TILES):
                act.wait_ge(x_in[i], 16)
                square_sum(x[:, i, :], N_X + i, junk1)
            take_root(1, N_X, TILES)
            for i in range(TILES):
                act.wait_ge(h_turned, 2 * i + 1)
                act.copy(hT[:, 0:4, i * P:(i + 1) * P], cols(2 * (i % 2), 4, P)).then_inc(h_act, 1)
            filter_sine(1)

            for r in range(8):
                if r == 4:
                    filter_sine(2)
                act.wait_ge(qk_mm, r + 1)
                dst = (qT, kT)[r // 4][:, r % 4, L_PROMPT:TOKENS]
                act.activation(dst, bank[2 * (r % 2)][:, 0:L_SAMPLE], ACT.Copy,
                               scale=(-(DH ** -0.5) if r < 4 else 1.0)).then_inc(qk_act, 1)
            for i in range(0, TILES, 2):
                act.wait_ge(v_mm, i + 1)
                act.copy(vrow[:, i, :], bank[4][:, :]).then_inc(v_act, 1)

            for u in range(UNITS):
                _, n_keys, _ = attn_cols(u // HEADS)
                act.wait_ge(biased, u + 1)
                if u >= 2:
                    act.wait_ge(pt_mm, u - 1)
                act.activation(p_sb[u % 2][:, 0:n_keys], s_sb[u % 2][:, 0:n_keys], ACT.Exp,
                               bias=negmax[:, u:u + 1], scale=-1.0,
                               accum_out=den[:, u:u + 1]).then_inc(exp_done, 1)

            def rows_of_u(r):
                act.wait_ge(u_turned, 2 * r + 1)
                part, m = divmod(r, 4)
                dst = uv if part == 0 else x12[:, part - 1]
                act.copy(dst[:, 0:3, m * P:(m + 1) * P], cols(4 + 2 * (r % 2), 4, P)[:, 0:3, :]).then_inc(ut_act, 1)

            act.wait_ge(pads, 1)
            act.wait_ge(consts_in, 96)
            for r in range(NU):
                act.wait_ge(u_mm, r + 1)
                if r >= 2:
                    act.wait_ge(conv_done, r - 1)
                act.copy(uraw[r % 2][:, L_PROMPT + 3:TOKENS + 3], bank[2 * (r % 2)][:, 0:L_SAMPLE]).then_inc(u_act, 1)
                if r >= 1:
                    rows_of_u(r - 1)
                act.wait_ge(u_act, r + 1)
                act.wait_ge(u_dve, r + 1)
                if r >= 2:
                    act.wait_ge(u_turned, 2 * (r - 1))
                act.activation(uc[r % 2], uraw[r % 2][:, 1:TOKENS + 3], ACT.Identity,
                               bias=convw[:, 3, r:r + 1], scale=convw[:, 1, r:r + 1]).then_inc(conv_mid, 1)
            rows_of_u(NU - 1)

            for q in range(len(HY)):
                n, base = HY_N[q], HY_BASE[q]
                act.wait_ge(conv_done, NU)
                act.wait_ge(u_turned, 2 * NU)
                if q >= 1:
                    act.wait_ge(y_done, base)
                for f in range(n):
                    for part in range(2):
                        act.wait_ge(kf_mm, 2 * (base + f) + part + 1)
                        act.copy(kf[:, part, f, :], bank[4 + 2 * (f % 2) + part][:, :]).then_inc(kf_done, 1)

            act.wait_ge(z_done, HY_BASE[4])
            act.wait_ge(attn_row, TILES)
            for i in range(TILES):
                square_sum(attn[:, i, :], N_MIX + 2 * i, bank[7][:, :])
                square_sum(uv[:, i, :], N_MIX + 2 * i + 1, bank[7][:, :])
            take_root(2, N_MIX, 2 * TILES)

            def mix_columns(i):
                act.wait_ge(mix_turned, 2 * i + 1)
                act.copy(hT[:, 0:4, i * P:(i + 1) * P], cols(0, 4, P)).then_inc(mix_act, 1)

            def xn_columns(i):
                act.wait_ge(xn_turned, 2 * i + 1)
                act.copy(hT[:, 0:4, i * P:(i + 1) * P], cols(2, 4, P)).then_inc(xn_act, 1)

            mix_columns(0)
            for i in range(TILES):
                if i + 1 < TILES:
                    mix_columns(i + 1)
                act.wait_ge(res_done, 2 * (i + 1))
                act.wait_ge(mix_turned, 2 * i + 2)
                square_sum(x[:, i, :], N_FFN + i, attn[:, i, :].bitcast(BF16))
                take_root(3 + i, N_FFN + i, 1)
                if i >= 1:
                    xn_columns(i - 1)
            xn_columns(TILES - 1)
            act.wait_ge(logit_off, 1)
            act.activation(aff, aff, ACT.Exp).then_inc(logit_exp, 1)

            def hi_part(n, e):
                slot, turns = n % RAW_RING, n // RAW_RING
                laps = UNITS_PER_EXPERT // RAW_RING
                act.wait_ge(raw_in[slot], e * (16 * laps) + 16 * (turns + 1))
                if n >= SPLIT_RING:
                    done = e * UNITS_PER_EXPERT + (n - SPLIT_RING + 1)
                    act.wait_ge(unit_mm, done)
                act.copy(sp_unit[n % SPLIT_RING][0], raw[slot]).then_inc(hi_done, 1)

            def tokens_hi(count):
                for half in range(2):
                    act.wait_ge(xe_mm, count * 2 - 1 + half)
                    act.copy(xeT[0][:, 4 * half:4 * half + 4, :], cols(6 + half, 4, SLOTS)).then_inc(xe_hi, 1)

            def hidden_hi(count):
                act.wait_ge(h_turned2, count)
                act.copy(hsT[0], cols(2, CHUNK, SLOTS)).then_inc(hs_hi, 1)

            def expert(e, last=False):
                for c in range(CHUNKS):
                    m, n = e * CHUNKS + (c + 1), 2 + 3 * c
                    left = ALL_UNITS - (EXPERTS - 1) * UNITS_PER_EXPERT if last else 1 << 30
                    more = not (last and c == CHUNKS - 1)
                    for ahead in range(3):
                        if n + 3 + ahead < left:
                            hi_part(n + 3 + ahead, e)
                        if ahead == 0 and more:
                            act.wait_ge(unit_mm, e * UNITS_PER_EXPERT + (n + 1))
                            act.wait_ge(h_done, m)
                            act.activation(silu, bank[0][0:SLOTS, 0:CW], ACT.Silu).then_inc(silu_done, 1)
                        if ahead == 1 and c == CHUNKS - 2 and not last:
                            tokens_hi(e + 2)
                    if c == CHUNKS - 1:
                        act.wait_ge(unit_mm, e * UNITS_PER_EXPERT + (n + 3 if more else n + 1))
                        act.wait_ge(gate_set, e + 1)
                        act.activation(ysc[:, 0:W], bank[4][0:SLOTS, :], ACT.Copy,
                                       scale=gate_now).then_inc(ysc_done, 1)
                    if more:
                        hidden_hi(m + 1)

            act.wait_ge(chosen_done, 1)
            act.wait_ge(xn_out, 32 * TILES)
            act.wait_ge(out_mm, 2 * TILES)
            tokens_hi(1)
            for n in range(3):
                hi_part(n, 0)
            act.wait_ge(unit_mm, 1)
            act.activation(silu, bank[0][0:SLOTS, 0:CW], ACT.Silu).then_inc(silu_done, 1)
            for n in (3, 4):
                hi_part(n, 0)
            hidden_hi(1)
            with act.Fori(0, EXPERTS - 1) as e:
                expert(e)
            expert(EXPERTS - 1, last=True)

            act.wait_ge(scattered, 16 * EXPERTS)
            act.wait_ge(gathered, 16 * (EXPERTS + 1))
            sink = view(xreg, 0, (W,)).bitcast(BF16)
            for i in range(TILES):
                act.wait_ge(yfin_in[i], 16)
                square_sum(yfin[:, i, :], N_FIN + i, sink)
                take_root(9 + i, N_FIN + i, 1)

        @block.vector
        def _(dve):
            steps = [0]

            def step(ins):
                steps[0] += 1
                ins.then_inc(dve_step, 1)
                dve.wait_ge(dve_step, steps[0])

            def filter_arguments(n):
                dve.wait_ge(mlp_mm, n + 1)
                if n == 0:
                    dve.wait_ge(mlp_in, 16 * 8)
                else:
                    dve.wait_ge(mlp_sin, n)
                for g in range(2):
                    lo, n_pos = FIRST_TILE[g] * P, GROUP_LEN[g]
                    ins = dve.tensor_scalar(mlp_y[:, lo:lo + n_pos], bank[6 + g][0:FILTER_HID, 0:n_pos],
                                            mlp_b[:, n:n + 1], mlp_b[:, 3:4], ALU.add, ALU.mult)
                step(ins)
                step(dve.tensor_scalar(mlp_k, mlp_y, 1.0 / (2.0 * math.pi), ROUND_MAGIC, ALU.mult, ALU.add))
                step(dve.tensor_scalar(mlp_k, mlp_k, ROUND_MAGIC, None, ALU.subtract))
                step(dve.scalar_tensor_tensor(mlp_y, mlp_k, -TWO_PI_HI, mlp_y, ALU.mult, ALU.add))
                step(dve.scalar_tensor_tensor(mlp_y, mlp_k, -TWO_PI_LO, mlp_y, ALU.mult, ALU.add))
                dve.tensor_scalar(mlp_y, mlp_y, PI_IN, -PI_IN, ALU.min, ALU.max).then_inc(mlp_pre, 1)

            def mean_square(c0, count, width, n_sums):
                dve.wait_ge(ssq_done, n_sums)
                dve.tensor_scalar(msq[:, c0:c0 + count], ssq[:, c0:c0 + count], 1.0 / width, EPS,
                                  ALU.mult, ALU.add).then_inc(msq_done, 1)

            def inverse_root(n, c0, count):
                dve.wait_ge(root_done, n)
                step(dve.reciprocal(rinv[:, c0:c0 + count], root[:, c0:c0 + count]))

            def normed(dst, src, col, gain, done):
                dve.scalar_tensor_tensor(dst, src, rinv[:, col:col + 1], gain, ALU.mult, ALU.mult).then_inc(done, 1)

            filter_arguments(0)
            mean_square(N_X, TILES, D, TILES)
            inverse_root(1, N_X, TILES)
            dve.wait_ge(gain_in, 16)

            def h_columns(i):
                dve.wait_ge(h_turned, 2 * i + 2)
                dve.tensor_copy(hT[:, 4:8, i * P:(i + 1) * P], cols(2 * (i % 2) + 1, 4, P)).then_inc(h_dve, 1)

            for i in range(TILES):
                if i >= 2:
                    h_columns(i - 2)
                normed(hrow[i % 2], x[:, i, :], N_X + i, gbc[:, :], h_row)
            h_columns(TILES - 2)
            h_columns(TILES - 1)
            filter_arguments(1)
            for r in range(8):
                if r == 4:
                    filter_arguments(2)
                dve.wait_ge(qk_mm, r + 1)
                dst = (qT, kT)[r // 4][:, r % 4, 0:L_PROMPT]
                dve.tensor_scalar(dst, bank[2 * (r % 2) + 1][:, 0:L_PROMPT],
                                  -(DH ** -0.5) if r < 4 else 1.0, None, ALU.mult).then_inc(qk_dve, 1)
            for i in range(1, TILES, 2):
                dve.wait_ge(v_mm, i + 1)
                dve.tensor_copy(vrow[:, i, :], bank[5][:, :]).then_inc(v_dve, 1)

            def bias_scores(u):
                tile, head = divmod(u, HEADS)
                _, n_keys, c0 = attn_cols(tile)
                dve.wait_ge(score_mm, u + 1)
                if u >= 2:
                    dve.wait_ge(exp_done, u - 1)
                dve.tensor_tensor_reduce(s_sb[u % 2][:, 0:n_keys], bank[u % 2][:, 0:n_keys],
                                         bias[:, head, c0:c0 + n_keys], 1.0, 3e38, ALU.add, ALU.min,
                                         negmax[:, u:u + 1]).then_inc(biased, 1)

            def copy_probs(u):
                _, n_keys, _ = attn_cols(u // HEADS)
                dve.wait_ge(pt_mm, u + 1)
                if u >= 2:
                    dve.wait_ge(pv_mm, u - 1)
                n = n_keys // P
                dve.tensor_copy(pT[u % 2][:, 0:n, :], cols(2 + u % 2, 4, P)[:, 0:n, :]).then_inc(pt_done, 1)

            def attention_row(tile):
                h0 = tile * HEADS
                dve.wait_ge(exp_done, h0 + HEADS)
                step(dve.reciprocal(rden[:, h0:h0 + HEADS], den[:, h0:h0 + HEADS]))
                dve.wait_ge(pv_mm, h0 + HEADS)
                dve.tensor_tensor(attn[:, tile, :].rearrange("p (h c) -> p h c", h=HEADS),
                                  cols(4 + tile % 2, HEADS, DH),
                                  rden[:, h0:h0 + HEADS].unsqueeze(2).to_broadcast([P, HEADS, DH]),
                                  ALU.mult).then_inc(attn_row, 1)

            dve.wait_ge(bias_in, 16)
            dve.wait_ge(mlp_sin, 3)
            for s in range(UNITS + 4):
                if s < UNITS:
                    bias_scores(s)
                if 2 <= s < UNITS + 2:
                    copy_probs(s - 2)
                if s >= 4 and (s - 4) % HEADS == HEADS - 1:
                    attention_row((s - 4) // HEADS)

            for s in range(2):
                ins = dve.memset(uraw[s], 0.0)
            ins.then_inc(pads, 1)
            dve.wait_ge(pads, 1)
            dve.memset(zsel, 0.0).then_inc(pads, 1)
            dve.wait_ge(pads, 2)
            for g in range(2):
                tok0 = FIRST_TILE[g] * P
                dve.tensor_scalar(zsel[0:FILTER_HID, g, 0:1], hid[:, tok0:tok0 + 1], -1.0, None, ALU.mult)
                dve.memset(zsel[FILTER_HID:FILTER_HID + 1, g, 0:1], 1.0)

            def rows_of_u(r):
                dve.wait_ge(u_turned, 2 * r + 2)
                part, m = divmod(r, 4)
                dst = uv if part == 0 else x12[:, part - 1]
                dve.tensor_copy(dst[:, 3:6, m * P:(m + 1) * P],
                                cols(5 + 2 * (r % 2), 4, P)[:, 0:3, :]).then_inc(ut_dve, 1)

            for r in range(NU):
                dve.wait_ge(u_mm, r + 1)
                dve.tensor_copy(uraw[r % 2][:, 1:L_PROMPT + 1],
                                bank[2 * (r % 2) + 1][:, 0:L_PROMPT]).then_inc(u_dve, 1)
                if r >= 1:
                    rows_of_u(r - 1)
                dve.wait_ge(conv_mid, r + 1)
                step(dve.scalar_tensor_tensor(uc[r % 2], uraw[r % 2][:, 0:TOKENS + 2], convw[:, 0, r:r + 1],
                                              uc[r % 2], ALU.mult, ALU.add))
                dve.scalar_tensor_tensor(uc[r % 2], uraw[r % 2][:, 2:TOKENS + 4], convw[:, 2, r:r + 1],
                                         uc[r % 2], ALU.mult, ALU.add).then_inc(conv_done, 1)
            dve.wait_ge(w4_in, 48)
            step(dve.tensor_tensor(w4[:, 1], w4[:, 0], w4b_skip[0:FILTER_HID], ALU.subtract))
            dve.tensor_tensor(w4[:, 0], w4[:, 0], w4b_skip[0:FILTER_HID], ALU.add).then_inc(w4_done, 1)
            rows_of_u(NU - 1)

            dve.wait_ge(hy_in, 16 * 9)
            for q, (g, o) in enumerate(HY):
                n, base = HY_N[q], HY_BASE[q]
                tile0 = FIRST_TILE[g]
                if q >= 1:
                    dve.wait_ge(inv_mm, base)
                for i in range(n):
                    for part in range(2):
                        dve.wait_ge(ab_mm, 2 * (base + i) + part + 1)
                        dve.tensor_tensor(ab[:, part, i, :], bank[2 * (i % 2) + part][:, :],
                                          decay[:, tile0 + i, :], ALU.mult).then_inc(ab_done, 1)
                dve.wait_ge(kf_done, 2 * (base + n))
                for f in range(n):
                    dve.wait_ge(uf_mm, 2 * (base + f + 1))
                    u_cos, u_sin = bank[2 * (f % 2)][:, :], bank[2 * (f % 2) + 1][:, :]
                    dve.tensor_tensor(ab[:, 0, f, :], u_cos, kf[:, 0, f, :], ALU.mult)
                    step(dve.tensor_tensor(prod[0], u_sin, kf[:, 1, f, :], ALU.mult))
                    dve.tensor_tensor(ab[:, 0, f, :], ab[:, 0, f, :], prod[0], ALU.subtract)
                    dve.tensor_tensor(ab[:, 1, f, :], u_cos, kf[:, 1, f, :], ALU.mult)
                    step(dve.tensor_tensor(prod[1], u_sin, kf[:, 0, f, :], ALU.mult))
                    dve.tensor_tensor(ab[:, 1, f, :], ab[:, 1, f, :], prod[1], ALU.add).then_inc(y_done, 1)
                for i in range(n):
                    dve.wait_ge(inv_mm, base + i + 1)
                    dve.tensor_tensor(uv[:, tile0 + i, :], bank[4 + i][:, :], x12[:, o, tile0 + i, :],
                                      ALU.mult).then_inc(z_done, 1)

            mean_square(N_MIX, 2 * TILES, W, N_FFN)
            inverse_root(2, N_MIX, 2 * TILES)
            dve.wait_ge(gain_in, 48)

            def mix_rows(i):
                normed(attn[:, i, :], attn[:, i, :], N_MIX + 2 * i, gbc[:, 0:W], mix_row)
                normed(uv[:, i, :], uv[:, i, :], N_MIX + 2 * i + 1, gbc[:, W:D], mix_row)

            def mix_columns(i):
                dve.wait_ge(mix_turned, 2 * i + 2)
                dve.tensor_copy(hT[:, 4:8, i * P:(i + 1) * P], cols(1, 4, P)).then_inc(mix_dve, 1)

            def xn_columns(i):
                dve.wait_ge(xn_turned, 2 * i + 2)
                dve.tensor_copy(hT[:, 4:8, i * P:(i + 1) * P], cols(3, 4, P)).then_inc(xn_dve, 1)

            for i in range(TILES):
                mix_rows(i)
            mix_columns(0)
            for i in range(TILES):
                if i + 1 < TILES:
                    mix_columns(i + 1)
                for half in range(2):
                    dve.wait_ge(out_mm, 2 * i + half + 1)
                    dve.tensor_tensor(x[:, i, half * W:(half + 1) * W], x[:, i, half * W:(half + 1) * W],
                                      bank[4 + half][:, :], ALU.add).then_inc(res_done, 1)
                if i >= 1:
                    xn_columns(i - 1)
                mean_square(N_FFN + i, 1, D, N_FFN + i + 1)
                inverse_root(3 + i, N_FFN + i, 1)
                if i == 0:
                    dve.wait_ge(gain_in, 64)
                dve.wait_ge(mix_turned, 2 * i + 2)
                normed(attn[:, i, :], x[:, i, 0:W], N_FFN + i, gbc[:, 0:W], xn_row)
                normed(uv[:, i, :], x[:, i, W:D], N_FFN + i, gbc[:, W:D], xn_row)
            xn_columns(TILES - 1)

            dve.wait_ge(logit_mm, TILES)
            dve.wait_ge(y_init, 16 * TILES)
            logit = cols(6, TILES, EXPERTS)
            step(dve.tensor_reduce(lmax, logit, AX.X, ALU.max))
            dve.tensor_tensor(aff, logit, lmax.unsqueeze(2).to_broadcast([P, TILES, EXPERTS]),
                              ALU.subtract).then_inc(logit_off, 1)
            dve.wait_ge(logit_exp, 1)
            step(dve.tensor_reduce(lsum, aff, AX.X, ALU.add))
            step(dve.reciprocal(lmax, lsum))
            dve.tensor_tensor(aff, aff, lmax.unsqueeze(2).to_broadcast([P, TILES, EXPERTS]),
                              ALU.mult).then_inc(aff_done, 1)
            dve.wait_ge(affT_mm, 1)
            dve.tensor_copy(affT[:, 0:L_SAMPLE], bank[0][0:EXPERTS, 0:L_SAMPLE])
            step(dve.tensor_copy(affT[:, L_SAMPLE:TOKENS], bank[1][0:EXPERTS, 0:L_PROMPT]))
            for lo, hi, slot0, cap in ((0, L_SAMPLE, 0, CAP_SAMPLE), (L_SAMPLE, TOKENS, CAP_SAMPLE, CAP_PROMPT)):
                for n in range(slot0, slot0 + cap, 8):
                    step(dve.max(vals[:, n:n + 8], affT[:, lo:hi]))
                    step(dve.max_index(idxu[:, n:n + 8], vals[:, n:n + 8], affT[:, lo:hi]))
                    if n + 8 < slot0 + cap:
                        step(dve.match_replace(affT[:, lo:hi], vals[:, n:n + 8], affT[:, lo:hi], -1.0))
            dve.tensor_copy(idxf[:, CAP_SAMPLE:SLOTS], idxu[:, CAP_SAMPLE:SLOTS])
            dve.tensor_scalar(idxf[:, 0:CAP_SAMPLE], idxu[:, 0:CAP_SAMPLE], float(L_PROMPT), None,
                              ALU.add).then_inc(chosen, 1)
            dve.wait_ge(chosen_mm, 1)
            dve.tensor_copy(idxT[:, 0:EXPERTS], bank[2][0:SLOTS, 0:EXPERTS])
            dve.tensor_copy(idxT[:, EXPERTS:EXPERTS + 1], bank[2][0:SLOTS, EXPERTS - 1:EXPERTS])
            dve.tensor_copy(gateT, bank[3][0:SLOTS, 0:EXPERTS]).then_inc(chosen_done, 1)

            def lo_part(n, e):
                dve.wait_ge(hi_done, e * UNITS_PER_EXPERT + (n + 1))
                s = n % SPLIT_RING
                dve.tensor_tensor(sp_unit[s][1], raw[n % RAW_RING], sp_unit[s][0].bitcast(F32),
                                  ALU.subtract).then_inc(lo_done, 1)

            def hidden():
                dve.tensor_tensor(h_now, bank[1][0:SLOTS, 0:CW], silu, ALU.mult).then_inc(h_done, 1)

            def tokens_lo(count):
                dve.wait_ge(xe_hi, count * 2)
                for half in range(2):
                    ks = slice(4 * half, 4 * half + 4)
                    ins = dve.tensor_tensor(xeT[1][:, ks, :], cols(6 + half, 4, SLOTS), xeT[0][:, ks, :].bitcast(F32),
                                            ALU.subtract)
                ins.then_inc(xe_done, 1)

            def hidden_lo(count):
                dve.wait_ge(hs_hi, count)
                dve.tensor_tensor(hsT[1], cols(2, CHUNK, SLOTS), hsT[0].bitcast(F32),
                                  ALU.subtract).then_inc(hs_done, 1)

            def expert(e, last=False):
                for c in range(CHUNKS):
                    m, n = e * CHUNKS + (c + 1), 2 + 3 * c
                    left = ALL_UNITS - (EXPERTS - 1) * UNITS_PER_EXPERT if last else 1 << 30
                    more = not (last and c == CHUNKS - 1)
                    for ahead in range(3):
                        if n + 3 + ahead < left:
                            lo_part(n + 3 + ahead, e)
                        if ahead == 0 and more:
                            dve.wait_ge(unit_mm, e * UNITS_PER_EXPERT + (n + 2))
                            dve.wait_ge(silu_done, m + 1)
                            dve.wait_ge(h_turned2, m)
                            hidden()
                        if ahead == 1 and c == CHUNKS - 2 and not last:
                            tokens_lo(e + 2)
                    if c == CHUNKS - 1:
                        dve.wait_ge(unit_mm, e * UNITS_PER_EXPERT + (n + 3 if more else n + 1))
                        dve.wait_ge(gate_set, e + 1)
                        dve.tensor_scalar(ysc[:, W:D], bank[5][0:SLOTS, :], gate_now, None,
                                          ALU.mult).then_inc(ysc_done, 1)
                    if more:
                        hidden_lo(m + 1)

            tokens_lo(1)
            for n in range(3):
                lo_part(n, 0)
            dve.wait_ge(unit_mm, 2)
            dve.wait_ge(silu_done, 1)
            hidden()
            for n in (3, 4):
                lo_part(n, 0)
            hidden_lo(1)
            with dve.Fori(0, EXPERTS - 1) as e:
                expert(e)
            expert(EXPERTS - 1, last=True)

            dve.wait_ge(gain_in, 80)
            for i in range(TILES):
                mean_square(N_FIN + i, 1, D, N_FIN + i + 1)
                inverse_root(9 + i, N_FIN + i, 1)
                normed(yfin[:, i, :], yfin[:, i, :], N_FIN + i, gbc[:, :], fin_row)

        @block.gpsimd
        def _(pool):
            last_row = pool.to_reg(TOKENS - 1)

            def gather(index_set, count):
                pool.wait_ge(xn_out, 32 * TILES)
                pool.wait_ge(index_set, count)
                pool.indirect_dma_start(xg, None, xn_dram, bass.IndirectOffsetOnAxis(ap=idx_gather, axis=0),
                                        bounds_check=last_row).then_inc(gathered, 16)

            pool.wait_ge(chosen_done, 1)
            pool.tensor_copy(idx_gather, idxT[:, 0:1]).then_inc(first_index, 1)
            gather(first_index, 1)
            with pool.Fori(0, EXPERTS) as e:
                pool.tensor_copy(gate_now, gateT[:, bass.ds(e, 1)]).then_inc(gate_set, 1)
                pool.tensor_copy(idx_scatter, idxT[:, bass.ds(e, 1)]).then_inc(pool_step, 1)
                pool.wait_ge(gathered, e * 16 + 16)
                pool.wait_ge(xe_mm, e * 2 + 2)
                pool.tensor_copy(idx_gather, idxT[:, bass.ds(e + 1, 1)]).then_inc(pool_step, 1)
                gather(pool_step, e * 2 + 2)
                pool.wait_ge(y_init, 16 * TILES)
                pool.wait_ge(ysc_done, e * 2 + 2)
                pool.indirect_dma_start(y_dram, bass.IndirectOffsetOnAxis(ap=idx_scatter, axis=0), ysc, None,
                                        bounds_check=last_row, compute_op=ALU.add).then_inc(scattered, 16)
                pool.wait_ge(scattered, e * 16 + 16)
            pool.wait_ge(gathered, 16 * (EXPERTS + 1))


def shape_tables():
    f32 = np.float32
    tables = {"ident": np.eye(P, dtype=f32)}
    dist = np.abs(np.arange(P)[:, None] - (np.arange(BIAS_W)[None, :] - BIAS_OFF))
    count = np.zeros(dist.shape)
    for window, dil in PATTERNS:
        count += (dist % dil == 0) & (dist // dil <= window // (2 * dil))
    slopes = 2.0 ** (-8.0 * (np.arange(HEADS) + 1) / HEADS)
    ln = np.log(np.maximum(count, 1))
    table = np.where(count[:, None] > 0, slopes[None, :, None] * dist[:, None] - ln[:, None], -NEG)
    tables["attn_bias"] = table.reshape(P, HEADS * BIAS_W).astype(f32)
    feats, decays = [], []
    bands = np.linspace(1e-4, (FILTER_EMB - 1) // 2 - 1, (FILTER_EMB - 1) // 2, dtype=f32)[None]
    deltas = np.linspace(math.log(1e-2) / 0.3, math.log(1e-2) / 1.5, W, dtype=f32)
    for length in GROUP_LEN:
        pos = np.linspace(0.0, 1.0, length, dtype=f32)[:, None]
        wpos = f32(2.0 * math.pi) * np.arange(length, dtype=f32)[:, None] / f32(length)
        feats.append(np.concatenate([pos, np.cos(bands * wpos), -np.sin(bands * wpos)], axis=1))
        decays.append(np.exp(-pos * np.abs(deltas)))
    tables["features"] = np.ascontiguousarray(np.concatenate(feats).T.astype(f32))
    tables["decay"] = np.concatenate(decays).astype(f32)
    for name, length in zip(("dft_prompt", "dft_sample"), GROUP_LEN):
        f, n = np.arange(length) + 0.5, np.arange(length)
        half = np.pi * np.outer(n + 0.5, f) / length
        lag = np.pi * np.outer(n, f) / length
        tables[name] = np.stack([np.cos(half), np.sin(half), np.cos(lag) / length,
                                 np.sin(lag) / length]).astype(f32)
    return tables


_INS = ['x_prompt', 'x_sample', 'norm_mix_g', 'w_in', 'short_w', 'short_b', 'filt_w1', 'filt_b1', 'filt_w2',
        'filt_b2', 'filt_w3', 'filt_b3', 'filt_w4', 'filt_freq', 'hyena_skip', 'attn_out_g', 'hyena_out_g',
        'w_out', 'norm_ffn_g', 'w_router', 'w_gate', 'w_up', 'w_down', 'final_g']


def kernel(**inputs):
    import concourse.bacc as _bacc
    from concourse.bass_utils import run_bass_kernel_spmd as _run

    nc = _bacc.Bacc("TRN2", target_bir_lowering=False, num_devices=1)
    arrays, aps = {}, {}
    for name, a in [(n, np.ascontiguousarray(inputs[n])) for n in _INS] + list(shape_tables().items()):
        arrays[f"in_{name}"] = a
        aps[name] = nc.dram_tensor(f"in_{name}", a.shape, mybir.dt.from_np(a.dtype), kind="ExternalInput").ap()
    outs = [nc.dram_tensor(f"out_{n}", (1, length, D), F32, kind="ExternalOutput").ap()
            for n, length in zip(("prompt", "sample"), GROUP_LEN)]
    encoder(nc, aps, *outs)
    r = _run(nc, [arrays], core_ids=[0])
    return r.results[0]["out_prompt"], r.results[0]["out_sample"]
```

```python
import math
from contextlib import ExitStack

import numpy as np

import concourse.bass as bass
from concourse import mybir

F32 = mybir.dt.float32
F32R = mybir.dt.float32r
BF16 = mybir.dt.bfloat16
U32 = mybir.dt.uint32
ALU = mybir.AluOpType
ACT = mybir.ActivationFunctionType
AX = mybir.AxisListType

P = 128
D = 1024
KD = D // P
W = 512
HEADS, DH = 8, 64
L_PROMPT, L_SAMPLE = 256, 512
TOKENS = L_PROMPT + L_SAMPLE
TILES = TOKENS // P
FIRST_TILE = (0, L_PROMPT // P)
GROUP_LEN = (L_PROMPT, L_SAMPLE)
PATTERNS = ((128, 1), (512, 4), (2048, 16))
NEG = -1e30
EPS = 1e-6
FILTER_EMB, FILTER_HID, ORDER = 33, 64, 2
EXPERTS, FF = 16, 2816
CAP_SAMPLE, CAP_PROMPT = 2 * L_SAMPLE // EXPERTS, 2 * L_PROMPT // EXPERTS
SLOTS = CAP_SAMPLE + CAP_PROMPT
BIAS_OFF = L_SAMPLE - P
BIAS_W = L_SAMPLE + BIAS_OFF
CHUNK = 2
CW = CHUNK * P
CHUNKS = FF // CW
UNITS_PER_EXPERT = 3 * CHUNKS
UNIT_W = D * CW // P
W_RAW = 4
EXTRA = 3
RAW_RING, SPLIT_RING = 11, 3
FIRST_EXTRA = RAW_RING + SPLIT_RING
ALL_UNITS = EXPERTS * UNITS_PER_EXPERT
SBUF_BASE = 16512
ROUND_MAGIC = 1.5 * 2.0 ** 23
TWO_PI_HI = 6.28125
TWO_PI_LO = 2.0 * math.pi - TWO_PI_HI
PI_IN = 3.1415925

KB = 256


def unit_at(n):
    if n < 2:
        return "gu"[n], 0, 0
    m, kind = divmod(n - 2, 3)
    if kind == 2 or n == ALL_UNITS - 1:
        return "d", m % CHUNKS, m // CHUNKS
    return "gu"[kind], (m + 1) % CHUNKS, (m + 1) // CHUNKS


def raw_place(n):
    if FIRST_EXTRA <= n < FIRST_EXTRA + EXTRA:
        return RAW_RING + n - FIRST_EXTRA, 1
    turn = n if n < FIRST_EXTRA else n - EXTRA
    return turn % RAW_RING, turn // RAW_RING + 1


def raw_before(n):
    return n - RAW_RING if n < FIRST_EXTRA or n >= FIRST_EXTRA + EXTRA + RAW_RING else n - RAW_RING - EXTRA


def group_of(tile):
    return 0 if tile < FIRST_TILE[1] else 1


def encoder(nc, t, out_prompt, out_sample):
    xn_dram = nc.dram_tensor("xn_rows", [TOKENS, D], F32).ap()
    y_dram = nc.dram_tensor("y_rows", [TOKENS, D], F32).ap()

    with ExitStack() as ctx:
        def sem(name):
            return ctx.enter_context(nc.semaphore(name))

        def region(name, kb, size_kb, dt=F32):
            return nc.alloc_sbuf_tensor_at(name, [P, int(size_kb * KB)], dt, offset=SBUF_BASE + int(kb * 1024))

        xreg = region("xreg", 0, 24)
        hreg = region("hreg", 24, 24)
        areg = region("areg", 48, 12)
        vreg = region("vreg", 60, 12)
        wreg = region("wreg", 72, 32)
        breg = region("breg", 104, 96)
        split = region("split_ring", 48, 48, F32R)
        h_split = [region("h_high", 24, 16, F32R), region("h_low", 0, 16, F32R)]
        w_in_split = region("w_in_split", 88, 16, F32R)
        xe_split = region("xe_split", 8, 6, F32R)
        ht_split = region("ht_split", 14, 1.5, F32R)
        at = [200 * 1024]

        def sb(name, shape):
            size = 4 * int(np.prod(shape[1:]))
            tensor = nc.alloc_sbuf_tensor_at(name, shape, F32, offset=SBUF_BASE + at[0])
            at[0] += -(-size // 32) * 32
            return tensor

        ident = sb("ident", [P, P])
        gbc = sb("gbc", [P, D])
        ssq = sb("ssq", [P, 30])
        msq = sb("msq", [P, 30])
        root = sb("root", [P, 30])
        rinv = sb("rinv", [P, 30])
        negmax = sb("negmax", [P, TILES * HEADS])
        den = sb("den", [P, TILES * HEADS])
        rden = sb("rden", [P, TILES * HEADS])
        wrt = sb("wrt", [P, KD, EXPERTS])
        convw = sb("convw", [P, 4, 12])

        def view(reg, kb, shape, parts=P):
            n = int(np.prod(shape))
            start = int(kb * KB)
            v = reg[0:parts, start:start + n]
            names = "abcd"[:len(shape)]
            if len(shape) == 1:
                return v
            return v.rearrange("p (" + " ".join(names) + ") -> p " + " ".join(names),
                               **{c: s for c, s in zip(names[:-1], shape[:-1])})

        x = view(xreg, 0, (TILES, D))
        x_early = view(breg, 36, (TILES, D))
        hT_prompt = view(hreg, 16, (KD, L_PROMPT))
        hT_sample = [reg[:, :].rearrange("p (k t) -> p k t", k=KD) for reg in h_split]
        w_raw = [view(wreg, 4 * s, (KD, P)) for s in range(W_RAW)]
        w_parts = [[w_in_split[:, (2 * s + part) * D:(2 * s + part + 1) * D].rearrange("p (k c) -> p k c", k=KD)
                    for part in range(2)] for s in range(2)]
        w_out_raw = [[view(wreg, 16, (4, W)), view(wreg, 24, (4, W))], [view(wreg, 0, (4, W)), view(hreg, 16, (4, W))]]
        w_out_parts = [[[region(f"w_out_split{half}{part}{kh}", 104 + kb, 8, F32R)[:, :].rearrange("p (k c) -> p k c", k=4)
                         for kh, kb in enumerate(places)] for part, places in enumerate(by_part)]
                       for half, by_part in enumerate((((0, 8), (56, 64)), ((24, 32), (72, -24))))]
        mixT = [[reg[:, part * 2 * D:(part + 1) * 2 * D].rearrange("p (k t) -> p k t", k=KD) for part in range(2)]
                for reg in (region("mix_even", 24, 16, F32R), region("mix_odd", 88, 16, F32R))]
        xnT = [view(hreg, 16 + 4 * s, (KD, P)) for s in range(2)]
        attn = view(areg, 0, (TILES, W))
        hrow = [view(areg, 4 * s, (D,)) for s in range(2)]
        uv = view(vreg, 0, (TILES, W))
        qT = view(breg, 0, (4, TOKENS))
        kT = view(breg, 12, (4, TOKENS))
        vrow = view(breg, 24, (TILES, W))
        bias = view(breg, 36, (HEADS, BIAS_W))
        s_sb = [view(breg, 64 + 2 * s, (W,)) for s in range(2)]
        p_sb = [view(breg, 68 + 2 * s, (W,)) for s in range(2)]
        pT = [view(breg, 72 + 2 * s, (4, P)) for s in range(2)]
        vT = [view(breg, 80 + 3 * s, (TOKENS,)) for s in range(2)]
        feats = view(breg, 64, (TOKENS,), FILTER_EMB)
        mlp_y = view(breg, 67, (TOKENS,), FILTER_HID)
        mlp_k = view(breg, 70, (TOKENS,), FILTER_HID)
        mlp_w = view(breg, 73, (3, FILTER_HID), FILTER_HID)
        mlp_b = view(breg, 74, (4,), FILTER_HID)
        junk1 = view(breg, 76, (D,))
        hid = view(breg, 92, (TOKENS,), FILTER_HID)
        x12 = view(breg, 0, (2, TILES, W))
        fwd = [view(breg, 24, (4, 2, L_PROMPT // 2)), view(breg, 28, (4, 4, L_SAMPLE // 2))]
        inv = [view(breg, 44, (2, 1, L_PROMPT)), view(breg, 46, (2, 2, L_SAMPLE))]
        sink = view(breg, 54, (W,))
        decay = view(breg, 64, (TILES, W))
        kf = [view(breg, 56, (4, 1, W)), view(breg, 76, (4, 2, W))]
        uraw = [view(breg, 76 + 4 * s, (TOKENS + 4,)) for s in range(2)]
        uc = [view(breg, 84 + 4 * s, (TOKENS + 2,)) for s in range(2)]
        zsel = view(breg, 95, (2, P))
        ab = [view(hreg, 16, (2, 2, W)), view(hreg, 0, (2, 4, W))]
        ysum = [view(hreg, 16, (4, 1, W)), view(hreg, 0, (4, 2, W))]
        odd_sums = view(xreg, 16, (2, 2, W))
        uspec = view(wreg, 8, (4, W))
        w4 = view(wreg, 0, (2, ORDER, W), FILTER_HID)
        w4b_skip = view(gbc, 0, (ORDER, W), FILTER_HID + 1)
        raw = ([breg[:, s * UNIT_W:(s + 1) * UNIT_W] for s in range(RAW_RING)] +
               [hreg[:, s * UNIT_W:(s + 1) * UNIT_W] for s in range(EXTRA)])
        sp_unit = [[split[:, (2 * s + part) * UNIT_W:(2 * s + part + 1) * UNIT_W] for part in range(2)]
                   for s in range(SPLIT_RING)]

        def by_rows(unit, kind):
            return unit.rearrange("p (k c) -> p k c", c=(D if kind == "d" else CW))

        xg = view(xreg, 0, (D,), SLOTS)
        ysc = view(xreg, 4, (D,), SLOTS)
        xeT = [xe_split[:, part * KD * SLOTS:(part + 1) * KD * SLOTS].rearrange("p (k s) -> p k s", k=KD)
               for part in range(2)]
        hsT = [ht_split[:, part * CHUNK * SLOTS:(part + 1) * CHUNK * SLOTS].rearrange("p (j s) -> p j s", j=CHUNK)
               for part in range(2)]
        h_now = view(xreg, 16, (CW,), SLOTS)
        silu = view(xreg, 17, (CW,), SLOTS)
        S_TILES = TILES - FIRST_TILE[1]
        affT = [view(breg, 92, (L_PROMPT,), EXPERTS), view(xreg, 16, (L_SAMPLE,), EXPERTS)]
        lmax = [view(breg, 95.25, (2,)), view(xreg, 19, (S_TILES,))]
        lsum = [view(breg, 95.375, (2,)), view(xreg, 19.125, (S_TILES,))]
        aff = [view(breg, 95.5, (2, EXPERTS)), view(xreg, 19.5, (S_TILES, EXPERTS))]
        vals = view(breg, 93, (SLOTS,), EXPERTS)
        idxu = view(breg, 93.5, (SLOTS,), EXPERTS).bitcast(U32)
        idxf = view(breg, 94, (SLOTS,), EXPERTS)
        idxT = view(xreg, 21.5, (EXPERTS + 1,), SLOTS).bitcast(U32)
        gateT = view(xreg, 22, (EXPERTS,), SLOTS)
        idx_gather = view(xreg, 22.25, (1,), SLOTS).bitcast(U32)
        idx_scatter = view(xreg, 22.5, (1,), SLOTS).bitcast(U32)
        gate_now = view(xreg, 22.75, (1,), SLOTS)
        yfin = view(hreg, 0, (TILES, D))

        bank = [ctx.enter_context(nc.psum_tensor(f"bank{i}", [P, 512], F32)) for i in range(8)]

        def cols(b, n, w, parts=P):
            return bank[b][0:parts, 0:n * w].rearrange("p (n w) -> p n w", n=n)

        x_in = [sem(f"x_in{i}") for i in range(TILES)]
        ident_in, consts_in, mlp_in, bias_in, gain_in = (
            sem(n) for n in ("ident_in", "consts_in", "mlp_in", "bias_in", "gain_in"))
        w_raw_in = [sem(f"w_raw_in{s}") for s in range(W_RAW)]
        w_hi, w_lo, w_out_hi, w_out_lo = sem("w_hi"), sem("w_lo"), sem("w_out_hi"), sem("w_out_lo")
        w_out_in = [[sem(f"w_out_in{half}{kh}") for kh in range(2)] for half in range(2)]
        hy_in, w4_in = sem("hyena_tables_in"), sem("w4_in")
        dve_step = sem("dve_step")
        ssq_done, msq_done, root_done = sem("ssq_done"), sem("msq_done"), sem("root_done")
        mlp_mm, mlp_pre, mlp_sin = sem("mlp_mm"), sem("mlp_pre"), sem("mlp_sin")
        h_row, h_turned, h_hi, h_lo = (sem(n) for n in ("h_row", "h_turned", "h_hi", "h_lo"))
        proj_mm, proj_act, proj_dve = sem("proj_mm"), sem("proj_evac_act"), sem("proj_evac_dve")
        v_turned, vt_act, vt_dve = sem("v_turned"), sem("v_row_act"), sem("v_row_dve")
        score_mm, biased, exp_done = sem("score_mm"), sem("biased"), sem("exp_done")
        pt_mm, pt_done, pv_mm, attn_row = sem("pt_mm"), sem("pt_done"), sem("pv_mm"), sem("attn_row")
        pads = sem("pads")
        conv_mid, conv_done, u_turned = sem("conv_mid"), sem("conv_done"), sem("u_turned")
        ut_act, ut_dve = sem("u_row_act"), sem("u_row_dve")
        w4_done = sem("w4_done")
        job_mm, job_odd, job_read, y_done = sem("job_mm"), sem("job_odd_sums"), sem("job_read"), sem("y_done")
        mirror_read, mirror_step = sem("mirror_read"), sem("mirror_step")
        attn_normed, attn_turned, mix_hi = sem("attn_normed"), sem("attn_turned"), sem("mix_hi")
        hy_normed, hy_turned, mix_lo = sem("hy_normed"), sem("hy_turned"), sem("mix_lo")
        out_mm, res_done, y_init = sem("out_mm"), sem("residual_done"), sem("y_init")
        xn_row, xn_turned, xn_act, xn_dve, xn_out = (sem(n) for n in ("xn_row", "xn_turned", "xn_evac_act", "xn_evac_dve", "xn_out"))
        logit_mm, logit_off, logit_exp, aff_done = (sem(n) for n in ("logit_mm", "logit_off", "logit_exp", "aff_done"))
        affT_mm, chosen, chosen_mm, chosen_done = (sem(n) for n in ("affT_mm", "chosen", "chosen_mm", "chosen_done"))
        raw_in = [sem(f"raw_in{s}") for s in range(RAW_RING + EXTRA)]
        hi_done, lo_done, unit_mm = sem("hi_done"), sem("lo_done"), sem("unit_mm")
        pool_step, gathered, scattered, gate_set = (sem(n) for n in ("pool_step", "gathered", "scattered", "gate_set"))
        xe_mm, xe_hi, xe_done = sem("xe_mm"), sem("xe_hi"), sem("xe_done")
        silu_done, h_done, h_turned2 = sem("silu_done"), sem("h_done"), sem("expert_h_turned")
        hs_hi, hs_done, ysc_done = sem("hs_hi"), sem("hs_done"), sem("ysc_done")
        yfin_in = [sem(f"yfin_in{i}") for i in range(TILES)]
        fin_row, out_done = sem("fin_row"), sem("out_done")

        N_X, N_MIX, N_HY, N_FFN, N_FIN = 0, 6, 12, 18, 24
        HY = [(0, 0), (1, 0), (0, 1), (1, 1)]
        JOBS = [("A", 0, 0), ("A", 1, 0), ("A", 1, 1), ("K", 0, 0), ("U", 0, 0), ("K", 1, 0), ("K", 1, 1),
                ("U", 1, 0), ("I", 0, 0), ("U", 1, 1), ("A", 2, 0), ("I", 1, 0),
                ("K", 2, 0), ("A", 3, 0), ("A", 3, 1), ("U", 2, 0), ("K", 3, 0), ("K", 3, 1),
                ("U", 3, 0), ("I", 2, 0), ("U", 3, 1), ("I", 3, 0)]
        LAST_A = JOBS.index(("A", 3, 1)) + 1

        def through(kind, q):
            return max(n + 1 for n, job in enumerate(JOBS) if job[:2] == (kind, q))

        def half_tiles(q):
            return GROUP_LEN[HY[q][0]] // P // 2

        def ys_before(q):
            return sum(half_tiles(p) for p in range(q))

        UNITS = TILES * HEADS
        R_K, R_Q, R_U, NU, R_END = 4, 8, 12, 12, 24
        FILTER_AFTER = (5, 7, 9)

        def w_in_tile(r):
            return (8, 4, 0)[r // 4] + r % 4 if r < R_U else r

        def attn_cols(tile):
            g = group_of(tile)
            tok0 = FIRST_TILE[g] * P
            return tok0, GROUP_LEN[g], BIAS_OFF - (tile - FIRST_TILE[g]) * P

        def every_second(buf, col0, tile):
            start = col0 + (tile - tile % 2) * P + tile % 2
            return buf[:, start:start + 2 * P - 1:2]

        def mix_bank(i):
            return 2 if i == 1 else 0

        def mix_place(i, hyena, part):
            dst = mixT[i // 2 % 2][part]
            if not hyena:
                return dst[:, 0:4, (i % 2) * P:(i % 2 + 1) * P]
            return dst[:, 4:8, :].rearrange("p k (c o) -> p k c o", o=2)[:, :, :, i % 2]

        def later_place(n, e):
            if isinstance(e, int) and e == 0:
                return raw_place(n)
            slot, uses = raw_place(n + UNITS_PER_EXPERT)
            return slot, uses - UNITS_PER_EXPERT // RAW_RING

        block = ctx.enter_context(nc.Block())

        @block.sync
        def _(sp):
            def load_x(i, dst):
                g = group_of(i)
                src = (t["x_prompt"], t["x_sample"])[g][0, (i - FIRST_TILE[g]) * P:(i - FIRST_TILE[g] + 1) * P, :]
                sp.dma_start(dst[:, i, :], src).then_inc(x_in[i], 16)

            w_in = t["w_in"][0].rearrange("(k p) n -> p k n", p=P)

            def load_w(n):
                if n >= W_RAW:
                    sp.wait_ge(proj_mm, n - W_RAW + 1)
                sp.dma_start(w_raw[n % W_RAW], w_in[:, :, w_in_tile(n) * P:(w_in_tile(n) + 1) * P]).then_inc(w_raw_in[n % W_RAW], 16)

            load_x(0, x_early)
            sp.dma_start(ident[:, :], t["ident"]).then_inc(ident_in, 16)
            load_x(1, x_early)
            sp.dma_start(gbc[:, :], t["norm_mix_g"][0].partition_broadcast(P)).then_inc(gain_in, 16)
            load_x(2, x_early)
            load_w(0)
            load_x(3, x_early)
            load_w(1)
            load_x(4, x_early)
            load_x(5, x_early)
            sp.dma_start(feats, t["features"]).then_inc(mlp_in, 16)
            sp.dma_start(mlp_w[0:FILTER_EMB, 0, :], t["filt_w1"][0]).then_inc(mlp_in, 16)
            sp.dma_start(mlp_w[:, 1, :], t["filt_w2"][0]).then_inc(mlp_in, 16)
            sp.dma_start(mlp_w[:, 2, :], t["filt_w3"][0]).then_inc(mlp_in, 16)
            for n, name in enumerate(("filt_b1", "filt_b2", "filt_b3", "filt_freq")):
                sp.dma_start(mlp_b[:, n:n + 1], t[name].rearrange("o h -> h o")).then_inc(mlp_in, 16)
            load_w(2)
            load_w(3)
            for n in range(3):
                sp.dma_start(convw[:, n, :], t["short_w"][0, n].rearrange("(c p) -> p c", p=P),
                             allow_slow_non_contiguous=True).then_inc(consts_in, 16)
            sp.dma_start(convw[:, 3, :], t["short_b"][0].rearrange("(c p) -> p c", p=P),
                         allow_slow_non_contiguous=True).then_inc(consts_in, 16)
            sp.dma_start(wrt[:, :, :], t["w_router"][0].rearrange("(k p) e -> p k e", p=P)).then_inc(consts_in, 16)
            sp.wait_ge(h_row, TILES)
            sp.dma_start(bias, t["attn_bias"].rearrange("p (h c) -> p h c", h=HEADS)).then_inc(bias_in, 16)
            for n in range(W_RAW, R_U + W_RAW):
                load_w(n)
            sp.wait_ge(attn_row, TILES)
            for g in range(2):
                table = t[("fwd_prompt", "fwd_sample")[g]].rearrange("m (i p) f -> p m i f", p=P)
                for m in range(4):
                    sp.dma_start(fwd[g][:, m], table[:, m]).then_inc(hy_in, 16)
                table = t[("inv_prompt", "inv_sample")[g]].rearrange("m (i p) f -> p m i f", p=P)
                for m in range(2):
                    sp.dma_start(inv[g][:, m], table[:, m]).then_inc(hy_in, 16)
            sp.dma_start(decay, t["decay"].rearrange("(i p) c -> p i c", p=P)).then_inc(hy_in, 16)
            w4_src = t["filt_w4"][0].rearrange("h (o d c) -> h o d c", o=ORDER, d=2)
            sp.dma_start(w4b_skip[0:FILTER_HID], w4_src[:, :, 1, :]).then_inc(w4_in, 16)
            sp.dma_start(w4b_skip[FILTER_HID:FILTER_HID + 1], t["hyena_skip"]).then_inc(w4_in, 16)
            for n in range(R_U + W_RAW, R_END):
                load_w(n)
            sp.wait_ge(proj_mm, R_END - 3)
            sp.dma_start(w4[:, 0], w4_src[:, :, 0, :]).then_inc(w4_in, 16)
            w_out = t["w_out"][0].rearrange("(k p) n -> p k n", p=P)
            sp.wait_ge(proj_mm, R_END)

            def load_w_out(half, kh):
                sp.dma_start(w_out_raw[half][kh], w_out[:, 4 * kh:4 * kh + 4, half * W:(half + 1) * W]
                             ).then_inc(w_out_in[half][kh], 16)

            load_w_out(0, 0)
            load_w_out(0, 1)
            for i in range(TILES - 2):
                load_x(i, x)
            sp.wait_ge(job_mm, LAST_A)
            sp.dma_start(gbc[:, 0:W], t["attn_out_g"][0].partition_broadcast(P)).then_inc(gain_in, 16)
            sp.dma_start(gbc[:, W:D], t["hyena_out_g"][0].partition_broadcast(P)).then_inc(gain_in, 16)
            load_w_out(1, 0)
            sp.wait_ge(job_mm, through("I", 2))
            load_w_out(1, 1)
            sp.wait_ge(job_read, through("U", 3))
            for i in range(TILES - 2, TILES):
                load_x(i, x)

            w_gate, w_up, w_down = (t[n][0] for n in ("w_gate", "w_up", "w_down"))

            def load_unit(n, kind, c, e):
                if kind == "d":
                    src = w_down[bass.ds(e, 1), c * CW:(c + 1) * CW, :].rearrange("o (j p) d -> p (o j) d", p=P)
                else:
                    w = w_gate if kind == "g" else w_up
                    src = w[bass.ds(e, 1), :, c * CW:(c + 1) * CW].rearrange("o (k p) f -> p (o k) f", p=P)
                slot = raw_place(n)[0]
                sp.dma_start(by_rows(raw[slot], kind), src).then_inc(raw_in[slot], 16)

            sp.wait_ge(job_read, len(JOBS))
            no_w_out, after_first_half, after_second_half = (2, 5, 10, 6), (0, 1, 7, 8), (3, 4, 9)
            for n in no_w_out:
                if n == 6:
                    sp.wait_ge(ssq_done, N_FFN)
                load_unit(n, *unit_at(n))
            sp.wait_ge(attn_normed, TILES)
            sp.wait_ge(hy_normed, TILES)
            sp.dma_start(gbc[:, :], t["norm_ffn_g"][0].partition_broadcast(P)).then_inc(gain_in, 16)
            for i in range(TILES):
                if i == TILES - 1:
                    sp.wait_ge(out_mm, 2 * TILES - 1)
                    for n in after_first_half:
                        load_unit(n, *unit_at(n))
                sp.wait_ge(res_done, 2 * (i + 1))
                sp.dma_start(y_dram[i * P:(i + 1) * P, :], x[:, i, :]).then_inc(y_init, 16)
                if i == TILES - 1:
                    sp.wait_ge(out_mm, 2 * TILES)
                    load_unit(after_second_half[0], *unit_at(after_second_half[0]))
                sp.wait_ge(xn_row, 2 * (i + 1))
                sp.dma_start(xn_dram[i * P:(i + 1) * P, 0:W], attn[:, i, :]).then_inc(xn_out, 16)
                sp.dma_start(xn_dram[i * P:(i + 1) * P, W:D], uv[:, i, :]).then_inc(xn_out, 16)
            for n in after_second_half[1:]:
                load_unit(n, *unit_at(n))
            sp.dma_start(gbc[:, :], t["final_g"].partition_broadcast(P)).then_inc(gain_in, 16)

            start = FIRST_EXTRA + EXTRA + RAW_RING
            for n in range(RAW_RING, start):
                if FIRST_EXTRA <= n < FIRST_EXTRA + EXTRA:
                    sp.wait_ge(gathered, 16)
                else:
                    sp.wait_ge(lo_done, raw_before(n) + 1)
                load_unit(n, *unit_at(n))
            with sp.Fori(0, EXPERTS - 2) as e:
                for n in range(start, start + UNITS_PER_EXPERT):
                    kind, c, ahead = unit_at(n)
                    sp.wait_ge(lo_done, e * UNITS_PER_EXPERT + (raw_before(n) + 1))
                    load_unit(n, kind, c, e + ahead)
            for n in range(start + (EXPERTS - 2) * UNITS_PER_EXPERT, ALL_UNITS):
                sp.wait_ge(lo_done, raw_before(n) + 1)
                load_unit(n, *unit_at(n))

            sp.wait_ge(scattered, 16 * EXPERTS)
            for i in range(TILES):
                sp.dma_start(yfin[:, i, :], y_dram[i * P:(i + 1) * P, :]).then_inc(yfin_in[i], 16)
            for i in range(TILES):
                g = group_of(i)
                dst = (out_prompt, out_sample)[g][0, (i - FIRST_TILE[g]) * P:(i - FIRST_TILE[g] + 1) * P, :]
                sp.wait_ge(fin_row, i + 1)
                sp.dma_start(dst, yfin[:, i, :]).then_inc(out_done, 16)
            sp.wait_ge(out_done, 16 * TILES)
            sp.wait_ge(y_init, 16 * TILES)
            sp.wait_ge(xn_out, 32 * TILES)

        @block.tensor
        def _(pe):
            def filter_layer(n):
                if n == 0:
                    pe.wait_ge(mlp_in, 16 * 8)
                    pe.wait_ge(vt_act, 4)
                    pe.wait_ge(vt_dve, 4)
                else:
                    pe.wait_ge(mlp_sin, n)
                for g in range(2):
                    lo, n_pos = FIRST_TILE[g] * P, GROUP_LEN[g]
                    lhsT = mlp_w[0:FILTER_EMB, 0, :] if n == 0 else mlp_w[:, n, :]
                    rhs = (feats if n == 0 else hid)[:, lo:lo + n_pos]
                    mm = pe.matmul(bank[6 + g][0:FILTER_HID, 0:n_pos], lhsT, rhs, start=True, stop=True)
                mm.then_inc(mlp_mm, 1)

            def turn(rows, b, turned):
                for half in range(2):
                    for k in range(4):
                        mm = pe.transpose(cols(b + half, 4, P)[:, k, :], rows[half][:, k * P:(k + 1) * P], ident[:, :])
                    mm.then_inc(turned, 1)

            pe.wait_ge(ident_in, 16)

            def project_sample(r):
                pe.wait_ge(w_lo, r + 1)
                if r >= 2:
                    pe.wait_ge(proj_act, r - 1)
                    pe.wait_ge(proj_dve, r - 1)
                for k in range(KD):
                    for n, (w_part, h_part) in enumerate(((0, 0), (0, 1), (1, 0))):
                        mm = pe.matmul(bank[2 * (r % 2)][:, 0:L_SAMPLE], w_parts[r % 2][w_part][:, k, :],
                                       hT_sample[h_part][:, k, :],
                                       start=(k == 0 and n == 0), stop=(k == KD - 1 and n == 2))
                return mm

            def project_prompt(r):
                pe.wait_ge(w_raw_in[r % W_RAW], 16 * (r // W_RAW + 1))
                for k in range(KD):
                    mm = pe.matmul(bank[2 * (r % 2) + 1][:, 0:L_PROMPT], w_raw[r % W_RAW][:, k, :], hT_prompt[:, k, :],
                                   start=(k == 0), stop=(k == KD - 1))
                return mm

            def turn_v(m):
                pe.wait_ge(proj_act, m + 1)
                pe.wait_ge(proj_dve, m + 1)
                if m >= 2:
                    pe.wait_ge(vt_act, m - 1)
                    pe.wait_ge(vt_dve, m - 1)
                for i in range(TILES):
                    mm = pe.transpose(cols(4 + 2 * (m % 2) + i // 3, 4, P)[:, i % 3, :],
                                      vT[m % 2][:, i * P:(i + 1) * P], ident[:, :])
                mm.then_inc(v_turned, 1)

            def scores(u):
                tile, head = divmod(u, HEADS)
                tok0, n_keys, _ = attn_cols(tile)
                lo = DH * (head % 2)
                if u >= 2:
                    pe.wait_ge(biased, u - 1)
                if u == 2:
                    pe.wait_ge(proj_act, R_U)
                    pe.wait_ge(proj_dve, R_U)
                pe.matmul(bank[u % 2][:, 0:n_keys], qT[lo:lo + DH, head // 2, tile * P:(tile + 1) * P],
                          kT[lo:lo + DH, head // 2, tok0:tok0 + n_keys], start=True, stop=True).then_inc(score_mm, 1)

            def turn_probs(u):
                _, n_keys, _ = attn_cols(u // HEADS)
                pe.wait_ge(exp_done, u + 1)
                if u >= 2:
                    pe.wait_ge(pt_done, u - 1)
                for j in range(n_keys // P):
                    mm = pe.transpose(cols(2 + u % 2, 4, P)[:, j, :], p_sb[u % 2][:, j * P:(j + 1) * P], ident[:, :])
                mm.then_inc(pt_mm, 1)

            def times_v(u):
                tile, head = divmod(u, HEADS)
                tok0, n_keys, _ = attn_cols(tile)
                pe.wait_ge(pt_done, u + 1)
                if head == 0 and tile >= 2:
                    pe.wait_ge(attn_row, tile - 1)
                for j in range(n_keys // P):
                    mm = pe.matmul(bank[4 + tile % 2][:, head * DH:(head + 1) * DH], pT[u % 2][:, j, :],
                                   vrow[:, tok0 // P + j, head * DH:(head + 1) * DH],
                                   start=(j == 0), stop=(j == n_keys // P - 1))
                mm.then_inc(pv_mm, 1)

            for i in range(TILES):
                pe.wait_ge(h_row, i + 1)
                if i >= 2:
                    pe.wait_ge(h_lo, i - 1)
                    if i - 2 < FIRST_TILE[1]:
                        pe.wait_ge(h_hi, i - 1)
                turn([hrow[i % 2][:, 0:W], hrow[i % 2][:, W:D]], 4 + 2 * (i % 2), h_turned)
                if i in (3, 4):
                    project_prompt(i - 3)
            pe.wait_ge(h_lo, TILES)
            for r in range(R_U):
                mm = project_sample(r)
                if r == R_U - 1:
                    pe.wait_ge(proj_act, R_U - 1)
                    pe.wait_ge(proj_dve, R_U - 1)
                    scores(0)
                    scores(1)
                if r >= 2:
                    mm = project_prompt(r)
                mm.then_inc(proj_mm, 1)
                if 1 <= r <= 4:
                    turn_v(r - 1)
                if r in FILTER_AFTER:
                    filter_layer(FILTER_AFTER.index(r))

            for s in range(2, UNITS + 3):
                if s < UNITS:
                    scores(s)
                if 2 <= s < UNITS + 2:
                    turn_probs(s - 2)
                if s >= 3:
                    times_v(s - 3)

            def turn_u(r):
                pe.wait_ge(conv_done, r + 1)
                if r >= 2:
                    pe.wait_ge(ut_act, r - 1)
                    pe.wait_ge(ut_dve, r - 1)
                for i in range(TILES):
                    mm = pe.transpose(cols(4 + 2 * (r % 2) + i // 3, 4, P)[:, i % 3, :],
                                      every_second(uc[r % 2], 2 * group_of(i), i), ident[:, :])
                    if i % 3 == 2:
                        mm.then_inc(u_turned, 1)

            pe.wait_ge(biased, UNITS)
            pe.wait_ge(pt_done, UNITS)
            pe.wait_ge(attn_row, TILES)
            for r in range(NU):
                project_sample(R_U + r)
                project_prompt(R_U + r).then_inc(proj_mm, 1)
                if r >= 1:
                    turn_u(r - 1)

            pe.wait_ge(hy_in, 16 * 13)
            pe.wait_ge(w4_in, 48)
            pe.wait_ge(w4_done, 1)
            pe.wait_ge(proj_act, R_END)
            pe.wait_ge(proj_dve, R_END)
            for n, (kind, q, at_tile) in enumerate(JOBS):
                g, o = HY[q]
                halves, tile0, b = half_tiles(q), FIRST_TILE[g], 4 * (n % 2)
                if n == 1:
                    turn_u(NU - 1)
                    pe.wait_ge(ut_act, NU)
                    pe.wait_ge(ut_dve, NU)
                if n >= 2:
                    pe.wait_ge(job_read, n - 1)
                if kind == "A":
                    for odd in range(2):
                        h_cols = every_second(hid, 0, tile0 + 2 * at_tile + odd)
                        zero_lag = at_tile == 0 and odd == 0
                        pe.matmul(bank[b + 2 * odd][:, :], h_cols, w4[:, 0, o, :], start=True, stop=not zero_lag)
                        if zero_lag:
                            pe.matmul(bank[b][:, :], zsel[0:FILTER_HID + 1, g, :], w4b_skip[:, o, :],
                                      start=False, stop=True)
                        mm = pe.matmul(bank[b + 2 * odd + 1][:, :], h_cols, w4[:, 1, o, :], start=True, stop=True)
                if kind in "KU":
                    if kind == "K":
                        pe.wait_ge(job_read, through("A", q))
                    elif o > 0:
                        pe.wait_ge(job_read, through("I", q - 2))
                    for part in range(2):
                        table = fwd[g][:, part + (2 if kind == "K" else 0)]
                        for odd in range(2):
                            for pair in range(halves):
                                i = 2 * pair + odd
                                rhs = ab[g][:, part, i, :] if kind == "K" else uv[:, tile0 + i, :]
                                mm = pe.matmul(bank[b + 2 * part + odd][:, :],
                                               table[:, i, at_tile * P:(at_tile + 1) * P], rhs,
                                               start=(pair == 0), stop=(pair == halves - 1))
                if kind == "I":
                    for f in range(halves):
                        pe.wait_ge(y_done, ys_before(q) + f + 1)
                        for i in range(2 * halves):
                            for part in range(2):
                                mm = pe.matmul(bank[b + i][:, :], inv[g][:, part, f, i * P:(i + 1) * P],
                                               ysum[g][:, 2 * part + i % 2, f, :],
                                               start=(f == 0 and part == 0), stop=(f == halves - 1 and part == 1))
                mm.then_inc(job_mm, 1)

            def turn_four(src, b):
                for k in range(4):
                    mm = pe.transpose(cols(b, 4, P)[:, k, :], src[:, k * P:(k + 1) * P], ident[:, :])
                return mm

            def turn_attn(i):
                pe.wait_ge(attn_normed, i + 1)
                if i >= 2:
                    pe.wait_ge(mix_lo, 2 * i - 1)
                turn_four(attn[:, i, :], mix_bank(i)).then_inc(attn_turned, 1)

            def turn_hy(i):
                pe.wait_ge(hy_normed, i + 1)
                if i >= 2:
                    pe.wait_ge(mix_lo, 2 * i)
                turn_four(uv[:, i, :], mix_bank(i) + 1).then_inc(hy_turned, 1)

            def project_out(i, half):
                if half == 0:
                    pe.wait_ge(mix_lo, 2 * ((i | 1) + 1))
                if i == 0:
                    pe.wait_ge(w_out_lo, 2 * half + 2)
                if i >= 1:
                    pe.wait_ge(res_done, 2 * i - 1 + half)
                for k in range(KD):
                    for n, (m_part, w_part) in enumerate(((0, 0), (0, 1), (1, 0))):
                        mm = pe.matmul(bank[4 + half][:, :], mixT[i // 2 % 2][m_part][:, k, (i % 2) * P:(i % 2 + 1) * P],
                                       w_out_parts[half][w_part][k // 4][:, k % 4, :],
                                       start=(k == 0 and n == 0), stop=(k == KD - 1 and n == 2))
                mm.then_inc(out_mm, 1)

            def turn_xn(i):
                pe.wait_ge(xn_row, 2 * (i + 1))
                if i >= 1:
                    pe.wait_ge(xn_act, i)
                    pe.wait_ge(xn_dve, i)
                turn([attn[:, i, :], uv[:, i, :]], 2, xn_turned)

            def logits(i):
                pe.wait_ge(consts_in, 80)
                pe.wait_ge(xn_act, i + 1)
                pe.wait_ge(xn_dve, i + 1)
                for k in range(KD):
                    mm = pe.matmul(bank[7 - group_of(i)][:, i * EXPERTS:(i + 1) * EXPERTS], xnT[i % 2][:, k, :],
                                   wrt[:, k, :], start=(k == 0), stop=(k == KD - 1))
                mm.then_inc(logit_mm, 1)

            for i in range(2):
                turn_attn(i)
                turn_hy(i)
            def turn_affinities(g):
                pe.wait_ge(aff_done, g + 1)
                for i in range(GROUP_LEN[g] // P):
                    mm = pe.matmul(bank[(7, 0)[g]][0:EXPERTS, i * P:(i + 1) * P], aff[g][:, i, :], ident[:, :],
                                   start=True, stop=True)
                mm.then_inc(affT_mm, 1)

            pe.wait_ge(job_read, len(JOBS))
            for i in range(TILES):
                if 1 <= i < TILES - 2:
                    turn_attn(i + 2)
                    turn_hy(i + 2)
                project_out(i, 0)
                if i == 0:
                    turn_attn(2)
                    turn_hy(2)
                project_out(i, 1)
                if i >= 1:
                    turn_xn(i - 1)
                if i >= 2:
                    logits(i - 2)
                if i == TILES - 2:
                    turn_affinities(0)
            logits(TILES - 2)
            turn_xn(TILES - 1)
            logits(TILES - 1)

            turn_affinities(1)
            pe.wait_ge(chosen, 1)
            pe.matmul(bank[2][0:SLOTS, 0:EXPERTS], idxf, ident[0:EXPERTS, 0:EXPERTS], start=True, stop=True)
            pe.matmul(bank[3][0:SLOTS, 0:EXPERTS], vals, ident[0:EXPERTS, 0:EXPERTS],
                      start=True, stop=True).then_inc(chosen_mm, 1)

            def turn_in():
                for half in range(2):
                    for k in range(4):
                        mm = pe.transpose(cols(6 + half, 4, SLOTS)[:, k, :],
                                          xg[:, (4 * half + k) * P:(4 * half + k + 1) * P], ident[0:SLOTS, 0:SLOTS])
                    mm.then_inc(xe_mm, 1)

            def three_passes(out, x_hi, x_lo, w_hi, w_lo, start, stop):
                pe.matmul(out, x_hi, w_hi, start=start, stop=False)
                pe.matmul(out, x_hi, w_lo, start=False, stop=False)
                return pe.matmul(out, x_lo, w_hi, start=False, stop=stop)

            def multiply(n, kind, c, count):
                w_hi, w_lo = (by_rows(sp_unit[n % SPLIT_RING][part], kind) for part in range(2))
                pe.wait_ge(lo_done, count + 1)
                if kind == "d":
                    for j in range(CHUNK):
                        for half in range(2):
                            mm = three_passes(bank[4 + half][0:SLOTS, :], hsT[0][:, j, :], hsT[1][:, j, :],
                                              w_hi[:, j, half * W:(half + 1) * W], w_lo[:, j, half * W:(half + 1) * W],
                                              c == 0 and j == 0, c == CHUNKS - 1 and j == CHUNK - 1)
                else:
                    out = bank["gu".index(kind)][0:SLOTS, 0:CW]
                    for k in range(KD):
                        mm = three_passes(out, xeT[0][:, k, :], xeT[1][:, k, :], w_hi[:, k, :], w_lo[:, k, :],
                                          k == 0, k == KD - 1)
                mm.then_inc(unit_mm, 1)

            def turn_hidden(done):
                pe.wait_ge(h_done, done + 1)
                for j in range(CHUNK):
                    mm = pe.transpose(cols(2, CHUNK, SLOTS)[:, j, :], h_now[:, j * P:(j + 1) * P],
                                      ident[0:SLOTS, 0:SLOTS])
                mm.then_inc(h_turned2, 1)

            def expert(e, last=False):
                for c in range(CHUNKS):
                    m, n = e * CHUNKS + (c + 1), 2 + 3 * c
                    count = e * UNITS_PER_EXPERT
                    more = not (last and c == CHUNKS - 1)
                    if more:
                        if c == CHUNKS - 1:
                            pe.wait_ge(xe_done, e + 2)
                        pe.wait_ge(silu_done, m)
                        multiply(n, "g", (c + 1) % CHUNKS, count + n)
                        pe.wait_ge(h_done, m)
                        multiply(n + 1, "u", (c + 1) % CHUNKS, count + (n + 1))
                    if c == CHUNKS - 2 and not last:
                        pe.wait_ge(gathered, e * 16 + 32)
                        pe.wait_ge(xe_done, e + 1)
                        turn_in()
                    if c == 0:
                        pe.wait_ge(ysc_done, e * 2 + 2)
                    pe.wait_ge(hs_done, m)
                    d = n + 2 if more else n
                    multiply(d, "d", c, count + d)
                    if more:
                        turn_hidden(m)

            pe.sem_inc(xe_mm, 2)
            pe.wait_ge(gathered, 16)
            turn_in()
            pe.wait_ge(xe_done, 1)
            pe.wait_ge(lo_done, SPLIT_RING)
            multiply(0, "g", 0, 0)
            multiply(1, "u", 0, 1)
            turn_hidden(0)
            with pe.Fori(0, EXPERTS - 1) as e:
                expert(e)
            expert(EXPERTS - 1, last=True)

        @block.scalar
        def _(act):
            def square_sum(src, col, junk):
                if col >= 1:
                    act.wait_ge(ssq_done, col)
                act.activation(junk, src, ACT.Square, accum_out=ssq[:, col:col + 1]).then_inc(ssq_done, 1)

            def take_root(n, c0, count):
                act.wait_ge(msq_done, n)
                act.activation(root[:, c0:c0 + count], msq[:, c0:c0 + count], ACT.Sqrt).then_inc(root_done, 1)

            def filter_sine(n):
                act.wait_ge(mlp_pre, n + 1)
                act.activation(hid, mlp_y, ACT.Sin).then_inc(mlp_sin, 1)

            def h_high(i):
                i0 = i - FIRST_TILE[1]
                if i0 < 0:
                    act.wait_ge(h_turned, 2 * i + 1)
                    act.copy(hT_prompt[:, 0:4, i * P:(i + 1) * P], cols(4 + 2 * (i % 2), 4, P)).then_inc(h_hi, 1)
                    return
                for half in range(2):
                    act.wait_ge(h_turned, 2 * i + half + 1)
                    act.copy(hT_sample[0][:, 4 * half:4 * half + 4, i0 * P:(i0 + 1) * P],
                             cols(4 + 2 * (i % 2) + half, 4, P)).then_inc(h_hi, 1)

            def w_high(n):
                if n >= 2:
                    act.wait_ge(proj_mm, n - 1)
                act.wait_ge(w_raw_in[n % W_RAW], 16 * (n // W_RAW + 1))
                act.copy(w_parts[n % 2][0], w_raw[n % W_RAW]).then_inc(w_hi, 1)

            for i in range(TILES + 3):
                if i < TILES:
                    act.wait_ge(x_in[i], 16)
                    square_sum(x_early[:, i, :], N_X + i, junk1)
                if 1 <= i <= TILES:
                    take_root(i, N_X + i - 1, 1)
                if i >= 3:
                    h_high(i - 3)
                if i in (TILES, TILES + 1):
                    w_high(i - TILES)

            def rows_of_v(m):
                act.wait_ge(v_turned, m + 1)
                act.copy(vrow[:, 0:3, m * P:(m + 1) * P], cols(4 + 2 * (m % 2), 4, P)[:, 0:3, :]).then_inc(vt_act, 1)

            def probabilities(u):
                _, n_keys, _ = attn_cols(u // HEADS)
                act.wait_ge(biased, u + 1)
                if u >= 2:
                    act.wait_ge(pt_mm, u - 1)
                act.activation(p_sb[u % 2][:, 0:n_keys], s_sb[u % 2][:, 0:n_keys], ACT.Exp,
                               bias=negmax[:, u:u + 1], scale=-1.0,
                               accum_out=den[:, u:u + 1]).then_inc(exp_done, 1)

            for r in range(R_U):
                if r == R_U - 1:
                    probabilities(0)
                    probabilities(1)
                if r - 1 in FILTER_AFTER:
                    filter_sine(FILTER_AFTER.index(r - 1))
                act.wait_ge(proj_mm, r + 1)
                if r in (2, 3):
                    act.wait_ge(v_turned, r - 1)
                dst = (vT[r % 2] if r < R_K else (kT if r < R_Q else qT)[:, r % 4, :])[:, L_PROMPT:TOKENS]
                act.activation(dst, bank[2 * (r % 2)][:, 0:L_SAMPLE], ACT.Copy,
                               scale=(-(DH ** -0.5) if r >= R_Q else 1.0)).then_inc(proj_act, 1)
                if r < R_U - 1:
                    w_high(r + 2)
                if 1 <= r <= 4:
                    rows_of_v(r - 1)

            for u in range(2, UNITS):
                probabilities(u)
            w_high(R_U + 1)

            def rows_of_u(r):
                act.wait_ge(u_turned, 2 * r + 1)
                part, m = divmod(r, 4)
                dst = uv if part == 0 else x12[:, part - 1]
                act.copy(dst[:, 0:3, m * P:(m + 1) * P], cols(4 + 2 * (r % 2), 4, P)[:, 0:3, :]).then_inc(ut_act, 1)

            act.wait_ge(pads, 1)
            act.wait_ge(consts_in, 80)
            for r in range(NU):
                act.wait_ge(proj_mm, R_U + r + 1)
                if r >= 2:
                    act.wait_ge(conv_done, r - 1)
                act.copy(uraw[r % 2][:, L_PROMPT + 3:TOKENS + 3], bank[2 * (r % 2)][:, 0:L_SAMPLE]).then_inc(proj_act, 1)
                if r + 2 < NU:
                    w_high(R_U + r + 2)
                if r >= 1:
                    rows_of_u(r - 1)
                act.wait_ge(proj_act, R_U + r + 1)
                act.wait_ge(proj_dve, R_U + r + 1)
                if r >= 2:
                    act.wait_ge(u_turned, 2 * (r - 1))
                act.activation(uc[r % 2], uraw[r % 2][:, 1:TOKENS + 3], ACT.Identity,
                               bias=convw[:, 3, r:r + 1], scale=convw[:, 1, r:r + 1]).then_inc(conv_mid, 1)
            rows_of_u(NU - 1)

            def mix_high(i):
                for hyena, turned in enumerate((attn_turned, hy_turned)):
                    act.wait_ge(turned, i + 1)
                    if i == 2 and not hyena:
                        act.wait_ge(w_out_lo, 2)
                    if i >= 4 and not hyena:
                        act.wait_ge(out_mm, 2 * (i - i % 2 - 2))
                    act.copy(mix_place(i, hyena, 0), cols(mix_bank(i) + hyena, 4, P)).then_inc(mix_hi, 1)

            def w_out_high(half, kh):
                act.wait_ge(w_out_in[half][kh], 16)
                act.copy(w_out_parts[half][0][kh], w_out_raw[half][kh]).then_inc(w_out_hi, 1)

            act.wait_ge(conv_done, NU)
            for n, (kind, q, _) in enumerate(JOBS):
                if kind in "KU":
                    act.wait_ge(job_mm, n + 1)
                    for part in range(2):
                        ins = act.copy(odd_sums[:, n % 2, part, :], bank[4 * (n % 2) + 2 * part + 1][:, :])
                    ins.then_inc(job_odd, 1)
                if n == JOBS.index(("U", 0, 0)):
                    for i in range(TILES):
                        square_sum(attn[:, i, :], N_MIX + i, sink)
                if n == JOBS.index(("K", 3, 0)):
                    act.wait_ge(job_read, through("I", 1))
                    w_out_high(0, 0)
                if n == JOBS.index(("U", 3, 1)):
                    act.wait_ge(job_read, through("I", 2))
                    for i in range(FIRST_TILE[1]):
                        square_sum(uv[:, i, :], N_HY + i, sink)
                    w_out_high(0, 1)
            w_out_high(1, 0)
            w_out_high(1, 1)
            take_root(7, N_MIX, TILES)
            take_root(8, N_HY, FIRST_TILE[1])
            mix_high(0)
            mix_high(1)
            act.wait_ge(job_read, len(JOBS))
            for i in range(FIRST_TILE[1], TILES):
                square_sum(uv[:, i, :], N_HY + i, sink)
            take_root(9, N_HY + FIRST_TILE[1], TILES - FIRST_TILE[1])

            def xn_columns(i):
                act.wait_ge(xn_turned, 2 * i + 1)
                if i >= 2:
                    act.wait_ge(logit_mm, i - 1)
                act.copy(xnT[i % 2][:, 0:4, :], cols(2, 4, P)).then_inc(xn_act, 1)

            def router_exp(g):
                act.wait_ge(logit_off, g + 1)
                act.activation(aff[g], aff[g], ACT.Exp).then_inc(logit_exp, 1)

            for i in range(TILES):
                if i + 2 < TILES:
                    mix_high(i + 2)
                if i == TILES - 2:
                    router_exp(0)
                act.wait_ge(res_done, 2 * (i + 1))
                square_sum(x[:, i, :], N_FFN + i, attn[:, i, :].bitcast(BF16))
                take_root(10 + i, N_FFN + i, 1)
                if i >= 1:
                    xn_columns(i - 1)
            xn_columns(TILES - 1)
            router_exp(1)

            def hi_part(n, e):
                slot, uses = later_place(n, e)
                laps = UNITS_PER_EXPERT // RAW_RING
                act.wait_ge(raw_in[slot], e * (16 * laps) + 16 * uses)
                if n >= SPLIT_RING:
                    done = e * UNITS_PER_EXPERT + (n - SPLIT_RING + 1)
                    act.wait_ge(unit_mm, done)
                act.copy(sp_unit[n % SPLIT_RING][0], raw[slot]).then_inc(hi_done, 1)

            def tokens_hi(count):
                for half in range(2):
                    act.wait_ge(xe_mm, count * 2 + 1 + half)
                    act.copy(xeT[0][:, 4 * half:4 * half + 4, :], cols(6 + half, 4, SLOTS)).then_inc(xe_hi, 1)

            def hidden_hi(count):
                act.wait_ge(h_turned2, count)
                act.copy(hsT[0], cols(2, CHUNK, SLOTS)).then_inc(hs_hi, 1)

            def expert(e, last=False):
                for c in range(CHUNKS):
                    m, n = e * CHUNKS + (c + 1), 2 + 3 * c
                    left = ALL_UNITS - (EXPERTS - 1) * UNITS_PER_EXPERT if last else 1 << 30
                    more = not (last and c == CHUNKS - 1)
                    for ahead in range(3):
                        if n + 3 + ahead < left:
                            hi_part(n + 3 + ahead, e)
                        if ahead == 0 and more:
                            act.wait_ge(unit_mm, e * UNITS_PER_EXPERT + (n + 1))
                            act.wait_ge(h_done, m)
                            act.activation(silu, bank[0][0:SLOTS, 0:CW], ACT.Silu).then_inc(silu_done, 1)
                        if ahead == 1 and c == CHUNKS - 2 and not last:
                            tokens_hi(e + 2)
                    if c == CHUNKS - 1:
                        act.wait_ge(unit_mm, e * UNITS_PER_EXPERT + (n + 3 if more else n + 1))
                        act.wait_ge(gate_set, e + 1)
                        act.activation(ysc[:, 0:W], bank[4][0:SLOTS, :], ACT.Copy,
                                       scale=gate_now).then_inc(ysc_done, 1)
                    if more:
                        hidden_hi(m + 1)

            act.sem_inc(ysc_done, 2)
            act.wait_ge(xn_out, 32 * TILES)
            act.wait_ge(out_mm, 2 * TILES)
            for n in range(SPLIT_RING):
                hi_part(n, 0)
            act.wait_ge(chosen_done, 1)
            tokens_hi(1)
            act.wait_ge(unit_mm, 1)
            act.activation(silu, bank[0][0:SLOTS, 0:CW], ACT.Silu).then_inc(silu_done, 1)
            for n in (3, 4):
                hi_part(n, 0)
            hidden_hi(1)
            expert(0)
            with act.Fori(1, EXPERTS - 1) as e:
                expert(e)
            expert(EXPERTS - 1, last=True)

            act.wait_ge(scattered, 16 * EXPERTS)
            act.wait_ge(gathered, 16 * (EXPERTS + 1))
            for i in range(TILES):
                act.wait_ge(yfin_in[i], 16)
                square_sum(yfin[:, i, :], N_FIN + i, xreg[:, 0:W].bitcast(BF16))
                take_root(16 + i, N_FIN + i, 1)

        @block.vector
        def _(dve):
            steps = [0]

            def step(ins):
                steps[0] += 1
                ins.then_inc(dve_step, 1)
                dve.wait_ge(dve_step, steps[0])

            def filter_arguments(n):
                dve.wait_ge(mlp_mm, n + 1)
                if n == 0:
                    dve.wait_ge(mlp_in, 16 * 8)
                else:
                    dve.wait_ge(mlp_sin, n)
                for g in range(2):
                    lo, n_pos = FIRST_TILE[g] * P, GROUP_LEN[g]
                    ins = dve.tensor_scalar(mlp_y[:, lo:lo + n_pos], bank[6 + g][0:FILTER_HID, 0:n_pos],
                                            mlp_b[:, n:n + 1], mlp_b[:, 3:4], ALU.add, ALU.mult)
                step(ins)
                step(dve.tensor_scalar(mlp_k, mlp_y, 1.0 / (2.0 * math.pi), ROUND_MAGIC, ALU.mult, ALU.add))
                step(dve.tensor_scalar(mlp_k, mlp_k, ROUND_MAGIC, None, ALU.subtract))
                step(dve.scalar_tensor_tensor(mlp_y, mlp_k, -TWO_PI_HI, mlp_y, ALU.mult, ALU.add))
                step(dve.scalar_tensor_tensor(mlp_y, mlp_k, -TWO_PI_LO, mlp_y, ALU.mult, ALU.add))
                dve.tensor_scalar(mlp_y, mlp_y, PI_IN, -PI_IN, ALU.min, ALU.max).then_inc(mlp_pre, 1)

            def mean_square(c0, count, width, n_sums):
                dve.wait_ge(ssq_done, n_sums)
                dve.tensor_scalar(msq[:, c0:c0 + count], ssq[:, c0:c0 + count], 1.0 / width, EPS,
                                  ALU.mult, ALU.add).then_inc(msq_done, 1)

            def inverse_root(n, c0, count):
                dve.wait_ge(root_done, n)
                step(dve.reciprocal(rinv[:, c0:c0 + count], root[:, c0:c0 + count]))

            def normed(dst, src, col, gain, done):
                dve.scalar_tensor_tensor(dst, src, rinv[:, col:col + 1], gain, ALU.mult, ALU.mult).then_inc(done, 1)

            def h_low_parts(i):
                i0 = i - FIRST_TILE[1]
                if i0 < 0:
                    dve.wait_ge(h_turned, 2 * i + 2)
                    dve.tensor_copy(hT_prompt[:, 4:8, i * P:(i + 1) * P],
                                    cols(5 + 2 * (i % 2), 4, P)).then_inc(h_lo, 1)
                    return
                for half in range(2):
                    dve.wait_ge(h_hi, FIRST_TILE[1] + 2 * i0 + half + 1)
                    ks, ts = slice(4 * half, 4 * half + 4), slice(i0 * P, (i0 + 1) * P)
                    ins = dve.tensor_tensor(hT_sample[1][:, ks, ts], cols(4 + 2 * (i % 2) + half, 4, P),
                                            hT_sample[0][:, ks, ts].bitcast(F32), ALU.subtract)
                ins.then_inc(h_lo, 1)

            def w_low(n):
                dve.wait_ge(w_hi, n + 1)
                dve.tensor_tensor(w_parts[n % 2][1], w_raw[n % W_RAW], w_parts[n % 2][0].bitcast(F32),
                                  ALU.subtract).then_inc(w_lo, 1)

            for i in range(TILES):
                mean_square(N_X + i, 1, D, N_X + i + 1)
                if i >= 2:
                    h_low_parts(i - 2)
                inverse_root(i + 1, N_X + i, 1)
                if i == 0:
                    dve.wait_ge(gain_in, 16)
                normed(hrow[i % 2], x_early[:, i, :], N_X + i, gbc[:, :], h_row)
            h_low_parts(TILES - 2)
            w_low(0)
            h_low_parts(TILES - 1)
            w_low(1)
            def rows_of_v(m):
                dve.wait_ge(v_turned, m + 1)
                dve.tensor_copy(vrow[:, 3:6, m * P:(m + 1) * P],
                                cols(5 + 2 * (m % 2), 4, P)[:, 0:3, :]).then_inc(vt_dve, 1)

            def bias_scores(u):
                tile, head = divmod(u, HEADS)
                _, n_keys, c0 = attn_cols(tile)
                dve.wait_ge(score_mm, u + 1)
                if u >= 2:
                    dve.wait_ge(exp_done, u - 1)
                dve.tensor_tensor_reduce(s_sb[u % 2][:, 0:n_keys], bank[u % 2][:, 0:n_keys],
                                         bias[:, head, c0:c0 + n_keys], 1.0, 3e38, ALU.add, ALU.min,
                                         negmax[:, u:u + 1]).then_inc(biased, 1)

            for r in range(R_U):
                if r == R_U - 1:
                    dve.wait_ge(bias_in, 16)
                    dve.wait_ge(mlp_sin, 3)
                    bias_scores(0)
                    bias_scores(1)
                if r - 1 in FILTER_AFTER:
                    filter_arguments(FILTER_AFTER.index(r - 1))
                dve.wait_ge(proj_mm, r + 1)
                if r in (2, 3):
                    dve.wait_ge(v_turned, r - 1)
                dst = (vT[r % 2] if r < R_K else (kT if r < R_Q else qT)[:, r % 4, :])[:, 0:L_PROMPT]
                dve.tensor_scalar(dst, bank[2 * (r % 2) + 1][:, 0:L_PROMPT],
                                  -(DH ** -0.5) if r >= R_Q else 1.0, None, ALU.mult).then_inc(proj_dve, 1)
                if r < R_U - 1:
                    w_low(r + 2)
                if 1 <= r <= 4:
                    rows_of_v(r - 1)

            def copy_probs(u):
                _, n_keys, _ = attn_cols(u // HEADS)
                dve.wait_ge(pt_mm, u + 1)
                if u >= 2:
                    dve.wait_ge(pv_mm, u - 1)
                n = n_keys // P
                dve.tensor_copy(pT[u % 2][:, 0:n, :], cols(2 + u % 2, 4, P)[:, 0:n, :]).then_inc(pt_done, 1)

            def attention_row(tile):
                h0 = tile * HEADS
                dve.wait_ge(exp_done, h0 + HEADS)
                step(dve.reciprocal(rden[:, h0:h0 + HEADS], den[:, h0:h0 + HEADS]))
                dve.wait_ge(pv_mm, h0 + HEADS)
                dve.tensor_tensor(attn[:, tile, :].rearrange("p (h c) -> p h c", h=HEADS),
                                  cols(4 + tile % 2, HEADS, DH),
                                  rden[:, h0:h0 + HEADS].unsqueeze(2).to_broadcast([P, HEADS, DH]),
                                  ALU.mult).then_inc(attn_row, 1)

            for s in range(2, UNITS + 4):
                if s < UNITS:
                    bias_scores(s)
                if 2 <= s < UNITS + 2:
                    copy_probs(s - 2)
                if s >= 4 and (s - 4) % HEADS == HEADS - 1:
                    attention_row((s - 4) // HEADS)

            w_low(R_U + 1)
            for s in range(2):
                ins = dve.memset(uraw[s], 0.0)
            ins.then_inc(pads, 1)
            dve.wait_ge(pads, 1)
            dve.memset(zsel, 0.0).then_inc(pads, 1)
            dve.wait_ge(pads, 2)
            for g in range(2):
                tok0 = FIRST_TILE[g] * P
                dve.tensor_scalar(zsel[0:FILTER_HID, g, 0:1], hid[:, tok0:tok0 + 1], -1.0, None, ALU.mult)
                dve.memset(zsel[FILTER_HID:FILTER_HID + 1, g, 0:1], 1.0)

            def rows_of_u(r):
                dve.wait_ge(u_turned, 2 * r + 2)
                part, m = divmod(r, 4)
                dst = uv if part == 0 else x12[:, part - 1]
                dve.tensor_copy(dst[:, 3:6, m * P:(m + 1) * P],
                                cols(5 + 2 * (r % 2), 4, P)[:, 0:3, :]).then_inc(ut_dve, 1)

            for r in range(NU):
                dve.wait_ge(proj_mm, R_U + r + 1)
                dve.tensor_copy(uraw[r % 2][:, 1:L_PROMPT + 1],
                                bank[2 * (r % 2) + 1][:, 0:L_PROMPT]).then_inc(proj_dve, 1)
                if r + 2 < NU:
                    w_low(R_U + r + 2)
                if r >= 1:
                    rows_of_u(r - 1)
                if r == NU - 2:
                    dve.wait_ge(w4_in, 48)
                    step(dve.tensor_tensor(w4[:, 1], w4[:, 0], w4b_skip[0:FILTER_HID], ALU.subtract))
                    dve.tensor_tensor(w4[:, 0], w4[:, 0], w4b_skip[0:FILTER_HID], ALU.add).then_inc(w4_done, 1)
                dve.wait_ge(conv_mid, r + 1)
                step(dve.scalar_tensor_tensor(uc[r % 2], uraw[r % 2][:, 0:TOKENS + 2], convw[:, 0, r:r + 1],
                                              uc[r % 2], ALU.mult, ALU.add))
                dve.scalar_tensor_tensor(uc[r % 2], uraw[r % 2][:, 2:TOKENS + 4], convw[:, 2, r:r + 1],
                                         uc[r % 2], ALU.mult, ALU.add).then_inc(conv_done, 1)
            def times_filter(g, f, b):
                kc, ks, kmc, kms = (kf[g][:, m, f, :] for m in range(4))
                y = [ysum[g][:, m, f, :] for m in range(4)]
                uc_, us, umc, ums = (uspec[:, m, :] for m in range(4))
                first, done = steps[0], ys_before(q) + f

                def op(dst, a, b_, alu, after=None):
                    if after is not None:
                        dve.wait_ge(dve_step, first + after)
                    steps[0] += 1
                    return dve.tensor_tensor(dst, a, b_, alu).then_inc(dve_step, 1)

                ce, se = bank[b][:, :], bank[b + 2][:, :]
                co, so = odd_sums[:, n % 2, 0, :], odd_sums[:, n % 2, 1, :]
                if done > 0:
                    dve.wait_ge(y_done, done)
                op(uc_, ce, co, ALU.add)
                op(us, se, so, ALU.add)
                op(umc, se, so, ALU.subtract)
                dve.tensor_tensor(ums, ce, co, ALU.subtract).then_inc(job_read, 1)
                op(y[0], uc_, kc, ALU.mult, after=1)
                op(y[1], us, ks, ALU.mult, after=2)
                dve.wait_ge(dve_step, first + 3)
                dve.tensor_tensor(y[2], umc, kms, ALU.mult).then_inc(mirror_read, 1)
                op(y[0], y[0], y[1], ALU.subtract, after=5)
                dve.wait_ge(mirror_step, 4 * done + 1)
                dve.wait_ge(mirror_read, done + 1)
                op(y[2], y[2], y[3], ALU.add)
                op(y[1], uc_, ks, ALU.mult, after=6)
                op(uc_, us, kc, ALU.mult, after=8)
                op(uc_, y[1], uc_, ALU.add, after=9)
                op(y[1], y[0], y[2], ALU.subtract, after=10)
                dve.wait_ge(mirror_step, 4 * done + 4)
                op(y[3], uc_, umc, ALU.subtract)
                op(y[0], y[0], y[2], ALU.add, after=11)
                dve.wait_ge(dve_step, steps[0])
                dve.tensor_tensor(y[2], uc_, umc, ALU.add).then_inc(y_done, 1)

            dve.wait_ge(hy_in, 16 * 13)
            for n, (kind, q, at_tile) in enumerate(JOBS):
                g, o = HY[q]
                tile0, b = FIRST_TILE[g], 4 * (n % 2)
                if n == len(JOBS) - 1:
                    mean_square(N_MIX, TILES, W, N_HY)
                    mean_square(N_HY, FIRST_TILE[1], W, N_HY + FIRST_TILE[1])
                    inverse_root(7, N_MIX, TILES)
                    dve.wait_ge(gain_in, 48)
                    for i in range(TILES):
                        normed(attn[:, i, :], attn[:, i, :], N_MIX + i, gbc[:, 0:W], attn_normed)
                    inverse_root(8, N_HY, FIRST_TILE[1])
                    for i in range(FIRST_TILE[1]):
                        normed(uv[:, i, :], uv[:, i, :], N_HY + i, gbc[:, W:D], hy_normed)
                if n == 0:
                    rows_of_u(NU - 1)
                    dve.wait_ge(conv_done, NU)
                dve.wait_ge(job_mm, n + 1)
                if kind in "KU":
                    dve.wait_ge(job_odd, sum(job[0] in "KU" for job in JOBS[:n + 1]))
                if kind == "A":
                    for odd in range(2):
                        for part in range(2):
                            i = 2 * at_tile + odd
                            ins = dve.tensor_tensor(ab[g][:, part, i, :], bank[b + 2 * odd + part][:, :],
                                                    decay[:, tile0 + i, :], ALU.mult)
                    ins.then_inc(job_read, 1)
                if kind == "K":
                    for part in range(2):
                        even, odd = bank[b + 2 * part][:, :], odd_sums[:, n % 2, part, :]
                        dve.tensor_tensor(kf[g][:, part, at_tile, :], even, odd, ALU.add)
                        first, second = (even, odd) if part == 0 else (odd, even)
                        ins = dve.tensor_tensor(kf[g][:, 2 + part, at_tile, :], first, second, ALU.subtract)
                    ins.then_inc(job_read, 1)
                if kind == "U":
                    dve.wait_ge(job_read, through("K", q))
                    times_filter(g, at_tile, b)
                if kind == "I":
                    for i in range(2 * half_tiles(q)):
                        ins = dve.tensor_tensor(uv[:, tile0 + i, :], bank[b + i][:, :], x12[:, o, tile0 + i, :],
                                                ALU.mult)
                    ins.then_inc(job_read, 1)

            def mix_low(i):
                for hyena in range(2):
                    dve.wait_ge(mix_hi, 2 * i + hyena + 1)
                    dve.tensor_tensor(mix_place(i, hyena, 1), cols(mix_bank(i) + hyena, 4, P),
                                      mix_place(i, hyena, 0).bitcast(F32), ALU.subtract).then_inc(mix_lo, 1)

            mix_low(0)
            mix_low(1)
            mean_square(N_HY + FIRST_TILE[1], TILES - FIRST_TILE[1], W, N_FFN)
            inverse_root(9, N_HY + FIRST_TILE[1], TILES - FIRST_TILE[1])
            for i in range(FIRST_TILE[1], TILES):
                normed(uv[:, i, :], uv[:, i, :], N_HY + i, gbc[:, W:D], hy_normed)

            def xn_columns(i):
                dve.wait_ge(xn_turned, 2 * i + 2)
                if i >= 2:
                    dve.wait_ge(logit_mm, i - 1)
                dve.tensor_copy(xnT[i % 2][:, 4:8, :], cols(3, 4, P)).then_inc(xn_dve, 1)

            def softmax(g):
                n, first = GROUP_LEN[g] // P, FIRST_TILE[g]
                dve.wait_ge(logit_mm, first + n)
                logit = cols(7 - g, TILES, EXPERTS)[:, first:first + n, :]
                step(dve.tensor_reduce(lmax[g], logit, AX.X, ALU.max))
                dve.tensor_tensor(aff[g], logit, lmax[g].unsqueeze(2).to_broadcast([P, n, EXPERTS]),
                                  ALU.subtract).then_inc(logit_off, 1)
                dve.wait_ge(logit_exp, g + 1)
                step(dve.tensor_reduce(lsum[g], aff[g], AX.X, ALU.add))
                step(dve.reciprocal(lmax[g], lsum[g]))
                dve.tensor_tensor(aff[g], aff[g], lmax[g].unsqueeze(2).to_broadcast([P, n, EXPERTS]),
                                  ALU.mult).then_inc(aff_done, 1)

            def choose(g):
                dve.wait_ge(affT_mm, g + 1)
                step(dve.tensor_copy(affT[g], bank[(7, 0)[g]][0:EXPERTS, 0:GROUP_LEN[g]]))
                first, cap = ((CAP_SAMPLE, CAP_PROMPT), (0, CAP_SAMPLE))[g]
                for n in range(first, first + cap, 8):
                    step(dve.max(vals[:, n:n + 8], affT[g]))
                    step(dve.max_index(idxu[:, n:n + 8], vals[:, n:n + 8], affT[g]))
                    if n + 8 < first + cap:
                        step(dve.match_replace(affT[g], vals[:, n:n + 8], affT[g], -1.0))

            for i in range(TILES):
                if i + 2 < TILES:
                    mix_low(i + 2)
                if i == TILES - 2:
                    softmax(0)
                if i == TILES - 1:
                    choose(0)
                    dve.tensor_copy(idxf[:, CAP_SAMPLE:SLOTS], idxu[:, CAP_SAMPLE:SLOTS])
                dve.wait_ge(x_in[i], 32)
                for half in range(2):
                    dve.wait_ge(out_mm, 2 * i + half + 1)
                    dve.tensor_tensor(x[:, i, half * W:(half + 1) * W], x[:, i, half * W:(half + 1) * W],
                                      bank[4 + half][:, :], ALU.add).then_inc(res_done, 1)
                if i >= 1:
                    xn_columns(i - 1)
                mean_square(N_FFN + i, 1, D, N_FFN + i + 1)
                inverse_root(10 + i, N_FFN + i, 1)
                if i == 0:
                    dve.wait_ge(gain_in, 64)
                normed(attn[:, i, :], x[:, i, 0:W], N_FFN + i, gbc[:, 0:W], xn_row)
                normed(uv[:, i, :], x[:, i, W:D], N_FFN + i, gbc[:, W:D], xn_row)
            xn_columns(TILES - 1)

            dve.wait_ge(y_init, 16 * TILES)
            softmax(1)
            choose(1)
            dve.tensor_scalar(idxf[:, 0:CAP_SAMPLE], idxu[:, 0:CAP_SAMPLE], float(L_PROMPT), None,
                              ALU.add).then_inc(chosen, 1)
            dve.wait_ge(chosen_mm, 1)
            dve.tensor_copy(idxT[:, 0:EXPERTS], bank[2][0:SLOTS, 0:EXPERTS])
            dve.tensor_copy(idxT[:, EXPERTS:EXPERTS + 1], bank[2][0:SLOTS, EXPERTS - 1:EXPERTS])
            dve.tensor_copy(gateT, bank[3][0:SLOTS, 0:EXPERTS]).then_inc(chosen_done, 1)

            def lo_part(n, e):
                dve.wait_ge(hi_done, e * UNITS_PER_EXPERT + (n + 1))
                s = n % SPLIT_RING
                dve.tensor_tensor(sp_unit[s][1], raw[later_place(n, e)[0]], sp_unit[s][0].bitcast(F32),
                                  ALU.subtract).then_inc(lo_done, 1)

            def hidden():
                dve.tensor_tensor(h_now, bank[1][0:SLOTS, 0:CW], silu, ALU.mult).then_inc(h_done, 1)

            def tokens_lo(count):
                dve.wait_ge(xe_hi, count * 2)
                for half in range(2):
                    ks = slice(4 * half, 4 * half + 4)
                    ins = dve.tensor_tensor(xeT[1][:, ks, :], cols(6 + half, 4, SLOTS), xeT[0][:, ks, :].bitcast(F32),
                                            ALU.subtract)
                ins.then_inc(xe_done, 1)

            def hidden_lo(count):
                dve.wait_ge(hs_hi, count)
                dve.tensor_tensor(hsT[1], cols(2, CHUNK, SLOTS), hsT[0].bitcast(F32),
                                  ALU.subtract).then_inc(hs_done, 1)

            def expert(e, last=False):
                for c in range(CHUNKS):
                    m, n = e * CHUNKS + (c + 1), 2 + 3 * c
                    left = ALL_UNITS - (EXPERTS - 1) * UNITS_PER_EXPERT if last else 1 << 30
                    more = not (last and c == CHUNKS - 1)
                    for ahead in range(3):
                        if n + 3 + ahead < left:
                            lo_part(n + 3 + ahead, e)
                        if ahead == 0 and more:
                            dve.wait_ge(unit_mm, e * UNITS_PER_EXPERT + (n + 2))
                            dve.wait_ge(silu_done, m + 1)
                            dve.wait_ge(h_turned2, m)
                            hidden()
                        if ahead == 1 and c == CHUNKS - 2 and not last:
                            tokens_lo(e + 2)
                    if c == CHUNKS - 1:
                        dve.wait_ge(unit_mm, e * UNITS_PER_EXPERT + (n + 3 if more else n + 1))
                        dve.wait_ge(gate_set, e + 1)
                        dve.tensor_scalar(ysc[:, W:D], bank[5][0:SLOTS, :], gate_now, None,
                                          ALU.mult).then_inc(ysc_done, 1)
                    if more:
                        hidden_lo(m + 1)

            tokens_lo(1)
            lo_part(3, 0)
            dve.wait_ge(unit_mm, 2)
            dve.wait_ge(silu_done, 1)
            hidden()
            lo_part(4, 0)
            hidden_lo(1)
            expert(0)
            with dve.Fori(1, EXPERTS - 1) as e:
                expert(e)
            expert(EXPERTS - 1, last=True)

            dve.wait_ge(gain_in, 80)
            for i in range(TILES):
                mean_square(N_FIN + i, 1, D, N_FIN + i + 1)
                inverse_root(16 + i, N_FIN + i, 1)
                normed(yfin[:, i, :], yfin[:, i, :], N_FIN + i, gbc[:, :], fin_row)

        @block.gpsimd
        def _(pool):
            def w_out_low(half, kh):
                pool.wait_ge(w_out_hi, 2 * half + kh + 1)
                pool.tensor_tensor(w_out_parts[half][1][kh], w_out_raw[half][kh],
                                   w_out_parts[half][0][kh].bitcast(F32), ALU.subtract).then_inc(w_out_lo, 1)

            for n, (kind, q, f) in enumerate(JOBS):
                if kind != "U":
                    continue
                if (q, f) == (3, 0):
                    pool.wait_ge(y_done, ys_before(3))
                    w_out_low(0, 0)
                g, done = HY[q][0], ys_before(q) + f
                kmc, kms, y3 = kf[g][:, 2, f, :], kf[g][:, 3, f, :], ysum[g][:, 3, f, :]
                umc, ums = uspec[:, 2, :], uspec[:, 3, :]
                pool.wait_ge(job_read, n + 1)
                pool.tensor_tensor(y3, ums, kmc, ALU.mult).then_inc(mirror_step, 1)
                pool.wait_ge(mirror_step, 4 * done + 1)
                pool.tensor_tensor(ums, ums, kms, ALU.mult).then_inc(mirror_step, 1)
                pool.wait_ge(mirror_read, done + 1)
                pool.tensor_tensor(umc, umc, kmc, ALU.mult).then_inc(mirror_step, 1)
                pool.wait_ge(mirror_step, 4 * done + 3)
                pool.tensor_tensor(umc, umc, ums, ALU.subtract).then_inc(mirror_step, 1)

            pool.wait_ge(y_done, ys_before(4))
            w_out_low(0, 1)
            w_out_low(1, 0)
            w_out_low(1, 1)

            for n in range(SPLIT_RING):
                pool.wait_ge(hi_done, n + 1)
                pool.tensor_tensor(sp_unit[n][1], raw[n], sp_unit[n][0].bitcast(F32), ALU.subtract).then_inc(lo_done, 1)

            last_row = pool.to_reg(TOKENS - 1)

            def gather(index_set, count):
                pool.wait_ge(xn_out, 32 * TILES)
                pool.wait_ge(index_set, count)
                pool.indirect_dma_start(xg, None, xn_dram, bass.IndirectOffsetOnAxis(ap=idx_gather, axis=0),
                                        bounds_check=last_row).then_inc(gathered, 16)

            pool.wait_ge(chosen_done, 1)
            pool.tensor_copy(idx_gather, idxT[:, 0:1]).then_inc(pool_step, 2)
            gather(pool_step, 2)
            with pool.Fori(0, EXPERTS) as e:
                pool.tensor_copy(gate_now, gateT[:, bass.ds(e, 1)]).then_inc(gate_set, 1)
                pool.tensor_copy(idx_scatter, idxT[:, bass.ds(e, 1)]).then_inc(pool_step, 1)
                pool.wait_ge(gathered, e * 16 + 16)
                pool.wait_ge(xe_mm, e * 2 + 4)
                pool.tensor_copy(idx_gather, idxT[:, bass.ds(e + 1, 1)]).then_inc(pool_step, 1)
                gather(pool_step, e * 2 + 4)
                pool.wait_ge(y_init, 16 * TILES)
                pool.wait_ge(ysc_done, e * 2 + 4)
                pool.indirect_dma_start(y_dram, bass.IndirectOffsetOnAxis(ap=idx_scatter, axis=0), ysc, None,
                                        bounds_check=last_row, compute_op=ALU.add).then_inc(scattered, 16)
                pool.wait_ge(scattered, e * 16 + 16)
            pool.wait_ge(gathered, 16 * (EXPERTS + 1))


def shape_tables():
    f32 = np.float32
    tables = {"ident": np.eye(P, dtype=f32)}
    dist = np.abs(np.arange(P)[:, None] - (np.arange(BIAS_W)[None, :] - BIAS_OFF))
    count = np.zeros(dist.shape)
    for window, dil in PATTERNS:
        count += (dist % dil == 0) & (dist // dil <= window // (2 * dil))
    slopes = 2.0 ** (-8.0 * (np.arange(HEADS) + 1) / HEADS)
    ln = np.log(np.maximum(count, 1))
    table = np.where(count[:, None] > 0, slopes[None, :, None] * dist[:, None] - ln[:, None], -NEG)
    tables["attn_bias"] = table.reshape(P, HEADS * BIAS_W).astype(f32)
    feats, decays = [], []
    bands = np.linspace(1e-4, (FILTER_EMB - 1) // 2 - 1, (FILTER_EMB - 1) // 2, dtype=f32)[None]
    deltas = np.linspace(math.log(1e-2) / 0.3, math.log(1e-2) / 1.5, W, dtype=f32)
    for length in GROUP_LEN:
        pos = np.linspace(0.0, 1.0, length, dtype=f32)[:, None]
        wpos = f32(2.0 * math.pi) * np.arange(length, dtype=f32)[:, None] / f32(length)
        feats.append(np.concatenate([pos, np.cos(bands * wpos), -np.sin(bands * wpos)], axis=1))
        decays.append(np.exp(-pos * np.abs(deltas)))
    tables["features"] = np.ascontiguousarray(np.concatenate(feats).T.astype(f32))
    order = np.arange(TOKENS).reshape(-1, P, 2).transpose(0, 2, 1).reshape(-1)
    tables["decay"] = np.ascontiguousarray(np.concatenate(decays).astype(f32)[order])
    for name, length in zip(("prompt", "sample"), GROUP_LEN):
        f, n = np.arange(length // 2) + 0.5, order[:length]
        half = np.pi * np.outer(n + 0.5, f) / length
        lag = np.pi * np.outer(n, f) / length
        tables["fwd_" + name] = np.stack([np.cos(half), np.sin(half), np.cos(lag) / length,
                                          np.sin(lag) / length]).astype(f32)
        tables["inv_" + name] = np.stack([np.cos(half).T, np.sin(half).T]).astype(f32)
    return tables


_INS = ['x_prompt', 'x_sample', 'norm_mix_g', 'w_in', 'short_w', 'short_b', 'filt_w1', 'filt_b1', 'filt_w2',
        'filt_b2', 'filt_w3', 'filt_b3', 'filt_w4', 'filt_freq', 'hyena_skip', 'attn_out_g', 'hyena_out_g',
        'w_out', 'norm_ffn_g', 'w_router', 'w_gate', 'w_up', 'w_down', 'final_g']


def kernel(**inputs):
    import concourse.bacc as _bacc
    from concourse.bass_utils import run_bass_kernel_spmd as _run

    nc = _bacc.Bacc("TRN2", target_bir_lowering=False, num_devices=1)
    arrays, aps = {}, {}
    for name, a in [(n, np.ascontiguousarray(inputs[n])) for n in _INS] + list(shape_tables().items()):
        arrays[f"in_{name}"] = a
        aps[name] = nc.dram_tensor(f"in_{name}", a.shape, mybir.dt.from_np(a.dtype), kind="ExternalInput").ap()
    outs = [nc.dram_tensor(f"out_{n}", (1, length, D), F32, kind="ExternalOutput").ap()
            for n, length in zip(("prompt", "sample"), GROUP_LEN)]
    encoder(nc, aps, *outs)
    r = _run(nc, [arrays], core_ids=[0])
    return r.results[0]["out_prompt"], r.results[0]["out_sample"]
```
